# Optimizing a Trainium2 kernel written in Bass

```python
import math
import jax, jax.numpy as jnp
from jax import lax
import numpy as np

D_MODEL = 1024
BATCH = 1
SEQ = 256
DEPTH = 2

HEAD_DIM = 64
RET_DIM = D_MODEL // 4
RET_HEADS = RET_DIM // HEAD_DIM
RET_CHUNK = 128
SSD_DIM = D_MODEL // 2
SSD_HEADS = SSD_DIM // HEAD_DIM
SSD_GROUPS = 2
SSD_STATE = 64
SSD_CONV = 4
SSD_CHUNK = 128
SSD_CONV_DIM = SSD_DIM + 2 * SSD_GROUPS * SSD_STATE
SWA_DIM = D_MODEL // 4
SWA_HEADS = SWA_DIM // HEAD_DIM
SWA_KV_HEADS = 2
SWA_KV_DIM = SWA_KV_HEADS * HEAD_DIM
WINDOW = 128
REL_BUCKETS = 32
REL_MAX_DIST = WINDOW
MIX_DIM = RET_DIM + SSD_DIM + SWA_DIM
IN_SIZES = (RET_DIM, RET_DIM, RET_DIM, RET_DIM,
            SSD_DIM, SSD_CONV_DIM, SSD_HEADS,
            SWA_DIM, SWA_KV_DIM, SWA_KV_DIM)
IN_DIM = sum(IN_SIZES)
D_FF = 2816
N_EXPERTS = 8
TOP_K = 2
D_FF_EXPERT = 3584
N_DENSE = (DEPTH + 1) // 2
N_MOE = DEPTH // 2
DEEPNORM_ALPHA = (2 * DEPTH) ** 0.25
DEEPNORM_BETA = (8 * DEPTH) ** -0.25
LN_EPS = 1e-5


def _layer_norm(x, g, b):
    xf = x.astype(jnp.float32)
    mu = jnp.mean(xf, -1, keepdims=True)
    var = jnp.mean(jnp.square(xf - mu), -1, keepdims=True)
    return ((xf - mu) * lax.rsqrt(var + LN_EPS) * g + b).astype(x.dtype)

def _rotary(t, pos):
    half = t.shape[-1] // 2
    inv = jnp.exp(-math.log(10000.0) * jnp.arange(half, dtype=jnp.float32) / half)
    ang = pos.astype(jnp.float32)[..., None] * inv
    cos = jnp.cos(ang)[:, :, None, :]
    sin = jnp.sin(ang)[:, :, None, :]
    t1, t2 = t[..., :half], t[..., half:]
    return jnp.concatenate([t1 * cos - t2 * sin, t1 * sin + t2 * cos], -1).astype(t.dtype)

def _retention(q, k, v, g, pos):
    Bn, L, _ = q.shape
    H, d, C = RET_HEADS, HEAD_DIM, RET_CHUNK
    N = L // C
    dt = q.dtype
    q = _rotary(q.reshape(Bn, L, H, d), pos)
    k = _rotary(k.reshape(Bn, L, H, d), pos) * (d ** -0.5)
    v = v.reshape(Bn, L, H, d)
    log_gamma = jnp.log(1.0 - 2.0 ** (-5.0 - jnp.arange(H, dtype=jnp.float32)))
    idx = jnp.arange(C, dtype=jnp.float32)
    diff = idx[:, None] - idx[None, :]
    decay_in = jnp.where(diff >= 0, jnp.exp(log_gamma[:, None, None] * jnp.maximum(diff, 0.0)), 0.0).astype(dt)
    decay_q = jnp.exp(log_gamma[:, None] * (idx + 1.0)).astype(dt)
    decay_k = jnp.exp(log_gamma[:, None] * (C - 1.0 - idx)).astype(dt)
    decay_chunk = jnp.exp(log_gamma * C).astype(dt)
    qc = q.reshape(Bn, N, C, H, d)
    kc = k.reshape(Bn, N, C, H, d)
    vc = v.reshape(Bn, N, C, H, d)
    scores = jnp.einsum('bnihd,bnjhd->bnhij', qc, kc) * decay_in
    inner = jnp.einsum('bnhij,bnjhe->bnihe', scores, vc)
    chunk_kv = jnp.einsum('bnjhd,hj,bnjhe->nbhde', kc, decay_k, vc)

    def step(state, kv):
        return decay_chunk[None, :, None, None] * state + kv, state

    _, prev = lax.scan(step, jnp.zeros(chunk_kv.shape[1:], chunk_kv.dtype), chunk_kv)
    cross = jnp.einsum('bnihd,hi,nbhde->bnihe', qc, decay_q, prev)
    o = (inner + cross).reshape(Bn, L, H, d).astype(jnp.float32)
    mu = jnp.mean(o, -1, keepdims=True)
    var = jnp.mean(jnp.square(o - mu), -1, keepdims=True)
    o = ((o - mu) * lax.rsqrt(var + LN_EPS)).astype(dt).reshape(Bn, L, RET_DIM)
    return jax.nn.silu(g) * o

def _ssd(z, xbc, dt_raw, conv_w, conv_b, dt_bias, a_log, d_skip, norm_w):
    Bn, L, _ = z.shape
    G, R, P, NS, C = SSD_GROUPS, SSD_HEADS // SSD_GROUPS, HEAD_DIM, SSD_STATE, SSD_CHUNK
    NC = L // C
    xbc = lax.conv_general_dilated(xbc, conv_w[:, None, :], window_strides=(1,),
                                   padding=[(SSD_CONV - 1, 0)],
                                   dimension_numbers=('NWC', 'WIO', 'NWC'),
                                   feature_group_count=SSD_CONV_DIM) + conv_b
    xbc = jax.nn.silu(xbc)
    xs, Bm, Cm = jnp.split(xbc, [SSD_DIM, SSD_DIM + G * NS], -1)
    dt = jax.nn.softplus(dt_raw.astype(jnp.float32) + dt_bias)
    a = -jnp.exp(a_log.astype(jnp.float32)) * dt
    x = xs.reshape(Bn, NC, C, G, R, P)
    xdt = x * dt.reshape(Bn, NC, C, G, R, 1).astype(x.dtype)
    Bm = Bm.reshape(Bn, NC, C, G, NS)
    Cm = Cm.reshape(Bn, NC, C, G, NS)
    a_cs = jnp.cumsum(a.reshape(Bn, NC, C, G, R), axis=2).transpose(0, 1, 3, 4, 2)
    causal = jnp.tril(jnp.ones((C, C), dtype=bool))
    seg = a_cs[..., :, None] - a_cs[..., None, :]
    lmat = jnp.exp(jnp.where(causal, seg, -jnp.inf))
    cb = jnp.einsum('bclgn,bcsgn->bcgls', Cm, Bm)
    y_diag = jnp.einsum('bcgls,bcgrls,bcsgrp->bclgrp', cb, lmat, xdt)
    decay_states = jnp.exp(a_cs[..., -1:] - a_cs)
    states = jnp.einsum('bclgn,bcgrl,bclgrp->cbgrpn', Bm, decay_states, xdt).astype(jnp.float32)
    chunk_decay = jnp.exp(a_cs[..., -1]).transpose(1, 0, 2, 3)

    def step(S, inp):
        dec, st = inp
        return dec[..., None, None] * S + st, S

    _, prev = lax.scan(step, jnp.zeros(states.shape[1:], jnp.float32), (chunk_decay, states))
    y_off = jnp.einsum('bclgn,cbgrpn,bcgrl->bclgrp', Cm, prev, jnp.exp(a_cs))
    y = y_diag + y_off + x * d_skip.reshape(G, R, 1)
    y = y.reshape(Bn, L, SSD_DIM).astype(z.dtype)
    h = (y * jax.nn.silu(z)).astype(jnp.float32).reshape(Bn, L, G, SSD_DIM // G)
    h = h * lax.rsqrt(jnp.mean(jnp.square(h), -1, keepdims=True) + LN_EPS)
    return (h.reshape(Bn, L, SSD_DIM) * norm_w).astype(z.dtype)

def _t5_bucket(dist):
    exact = REL_BUCKETS // 2
    df = jnp.maximum(dist, 1).astype(jnp.float32)
    large = exact + (jnp.log(df / exact) / math.log(REL_MAX_DIST / exact) * (REL_BUCKETS - exact)).astype(jnp.int32)
    large = jnp.minimum(large, REL_BUCKETS - 1)
    return jnp.where(dist < exact, dist, large)

def _swa(q, k, v, rel_bias, sinks):
    Bn, L, _ = q.shape
    W, HK, GQ, d = WINDOW, SWA_KV_HEADS, SWA_HEADS // SWA_KV_HEADS, HEAD_DIM
    NB = L // W
    qb = q.reshape(Bn, NB, W, HK, GQ, d)
    kb = k.reshape(Bn, NB, W, HK, d)
    vb = v.reshape(Bn, NB, W, HK, d)

    def band(t):
        prev = jnp.concatenate([jnp.zeros_like(t[:, :1]), t[:, :-1]], axis=1)
        return jnp.concatenate([prev, t], axis=2)

    kband, vband = band(kb), band(vb)
    qi = jnp.arange(W)[:, None]
    kj = jnp.arange(2 * W)[None, :]
    dist = qi + W - kj
    in_band = (dist >= 0) & (dist < W)
    kpos = jnp.arange(NB)[:, None, None] * W - W + kj[None]
    valid = in_band[None] & (kpos >= 0)
    bias = rel_bias[_t5_bucket(jnp.clip(dist, 0, W - 1))]
    bias = bias.transpose(2, 0, 1).reshape(HK, GQ, W, 2 * W).astype(jnp.float32)
    logits = jnp.einsum('bnikgd,bnjkd->bnkgij', qb, kband).astype(jnp.float32) * (d ** -0.5) + bias
    logits = jnp.where(valid[None, :, None, None], logits, -jnp.inf)
    sink = sinks.astype(jnp.float32).reshape(HK, GQ, 1)
    m = jnp.maximum(jnp.max(logits, -1), sink)
    p = jnp.exp(logits - m[..., None])
    denom = jnp.sum(p, -1) + jnp.exp(sink - m)
    o = jnp.einsum('bnkgij,bnjkd->bnikgd', (p / denom[..., None]).astype(v.dtype), vband)
    return o.reshape(Bn, L, SWA_DIM)

def _swiglu(h, wg, wu, wd):
    return (jax.nn.silu(h @ wg) * (h @ wu)) @ wd

def _moe(h, w_router, b_router, wg, wu, wd):
    Bn, L, D = h.shape
    t = h.reshape(-1, D)
    logits = (t @ w_router).astype(jnp.float32) + b_router
    top_v, top_i = lax.top_k(logits, TOP_K)
    top_w = jax.nn.softmax(top_v, -1)
    gates = jnp.sum(jax.nn.one_hot(top_i, N_EXPERTS, dtype=jnp.float32) * top_w[..., None], axis=1)
    out = jnp.zeros_like(t)
    for e in range(N_EXPERTS):
        out = out + gates[:, e:e + 1].astype(t.dtype) * _swiglu(t, wg[e], wu[e], wd[e])
    return out.reshape(Bn, L, D)

def first_inputs(seed: int = 0) -> dict:
    key = jax.random.key(seed)
    ks = jax.random.split(key, 32)
    f32 = jnp.float32
    D = D_MODEL

    def nrm(k, shape, scale):
        return jax.random.normal(k, shape, f32) * scale

    x = nrm(ks[0], (BATCH, SEQ, D), 1.0)
    c = nrm(ks[1], (BATCH, D), 1.0)
    offsets = jax.random.randint(ks[2], (BATCH, 1), 0, 1024, dtype=jnp.int32)
    positions = offsets + jnp.arange(SEQ, dtype=jnp.int32)[None, :]
    rel_bias = nrm(ks[3], (REL_BUCKETS, SWA_HEADS), 0.5)
    w_ada = nrm(ks[4], (DEPTH, D, 6 * D), 0.1 * D ** -0.5)
    b_ada = nrm(ks[5], (DEPTH, 6 * D), 0.01)
    w_in = nrm(ks[6], (DEPTH, D, IN_DIM), D ** -0.5)
    w_out = nrm(ks[7], (DEPTH, MIX_DIM, D), DEEPNORM_BETA * MIX_DIM ** -0.5)
    conv_w = nrm(ks[8], (DEPTH, SSD_CONV, SSD_CONV_DIM), SSD_CONV ** -0.5)
    conv_b = nrm(ks[9], (DEPTH, SSD_CONV_DIM), 0.01)
    u = jax.random.uniform(ks[10], (DEPTH, SSD_HEADS), f32)
    dt0 = jnp.exp(u * (math.log(0.1) - math.log(0.001)) + math.log(0.001))
    dt_bias = dt0 + jnp.log(-jnp.expm1(-dt0))
    a_log = jnp.log(jax.random.uniform(ks[11], (DEPTH, SSD_HEADS), f32, 1.0, 16.0))
    d_skip = 1.0 + nrm(ks[12], (DEPTH, SSD_HEADS), 0.1)
    ssd_norm_w = 1.0 + nrm(ks[13], (DEPTH, SSD_DIM), 0.02)
    sinks = nrm(ks[14], (DEPTH, SWA_HEADS), 0.5)
    ln_g = 1.0 + nrm(ks[15], (DEPTH, 2, D), 0.02)
    ln_b = nrm(ks[16], (DEPTH, 2, D), 0.02)
    ffn_w_gate = nrm(ks[17], (N_DENSE, D, D_FF), D ** -0.5)
    ffn_w_up = nrm(ks[18], (N_DENSE, D, D_FF), D ** -0.5)
    ffn_w_down = nrm(ks[19], (N_DENSE, D_FF, D), DEEPNORM_BETA * D_FF ** -0.5)
    router_w = nrm(ks[20], (N_MOE, D, N_EXPERTS), D ** -0.5)
    router_b = nrm(ks[21], (N_MOE, N_EXPERTS), 0.01)
    expert_w_gate = nrm(ks[22], (N_MOE, N_EXPERTS, D, D_FF_EXPERT), D ** -0.5)
    expert_w_up = nrm(ks[23], (N_MOE, N_EXPERTS, D, D_FF_EXPERT), D ** -0.5)
    expert_w_down = nrm(ks[24], (N_MOE, N_EXPERTS, D_FF_EXPERT, D), DEEPNORM_BETA * D_FF_EXPERT ** -0.5)
    return {'x': x, 'c': c, 'positions': positions, 'rel_bias': rel_bias,
            'w_ada': w_ada, 'b_ada': b_ada, 'w_in': w_in, 'w_out': w_out,
            'conv_w': conv_w, 'conv_b': conv_b, 'dt_bias': dt_bias, 'a_log': a_log,
            'd_skip': d_skip, 'ssd_norm_w': ssd_norm_w, 'sinks': sinks,
            'ln_g': ln_g, 'ln_b': ln_b,
            'ffn_w_gate': ffn_w_gate, 'ffn_w_up': ffn_w_up, 'ffn_w_down': ffn_w_down,
            'router_w': router_w, 'router_b': router_b,
            'expert_w_gate': expert_w_gate, 'expert_w_up': expert_w_up, 'expert_w_down': expert_w_down}

def first_block(x, c, positions, rel_bias, w_ada, b_ada, w_in, w_out, conv_w, conv_b,
              dt_bias, a_log, d_skip, ssd_norm_w, sinks, ln_g, ln_b,
              ffn_w_gate, ffn_w_up, ffn_w_down, router_w, router_b,
              expert_w_gate, expert_w_up, expert_w_down):
    split_idx = np.cumsum(IN_SIZES)[:-1].tolist()
    for layer in range(DEPTH):
        mod = c @ w_ada[layer] + b_ada[layer]
        sh_a, sc_a, g_a, sh_f, sc_f, g_f = [m[:, None, :] for m in jnp.split(mod, 6, -1)]
        h = x * (1.0 + sc_a) + sh_a
        u = h @ w_in[layer]
        rq, rk, rv, rg, sz, sxbc, sdt, aq, ak, av = jnp.split(u, split_idx, -1)
        y_ret = _retention(rq, rk, rv, rg, positions)
        y_ssd = _ssd(sz, sxbc, sdt, conv_w[layer], conv_b[layer], dt_bias[layer],
                     a_log[layer], d_skip[layer], ssd_norm_w[layer])
        y_swa = _swa(aq, ak, av, rel_bias, sinks[layer])
        mix = jnp.concatenate([y_ret, y_ssd, y_swa], -1) @ w_out[layer]
        x = _layer_norm(DEEPNORM_ALPHA * x + (1.0 + g_a) * mix, ln_g[layer, 0], ln_b[layer, 0])
        h = x * (1.0 + sc_f) + sh_f
        if layer % 2 == 0:
            i = layer // 2
            f = _swiglu(h, ffn_w_gate[i], ffn_w_up[i], ffn_w_down[i])
        else:
            i = layer // 2
            f = _moe(h, router_w[i], router_b[i], expert_w_gate[i], expert_w_up[i], expert_w_down[i])
        x = _layer_norm(DEEPNORM_ALPHA * x + (1.0 + g_f) * f, ln_g[layer, 1], ln_b[layer, 1])
    return x


CHUNK = 64
N_MEM = 256
MLSTM_HEADS = 4
MLSTM_WIDTH = D_MODEL
MLSTM_HEAD_DIM = MLSTM_WIDTH // MLSTM_HEADS
QKV_BLOCK = 4
MLSTM_CONV = 4
CONV_WIDTH = D_MODEL
CONV_KERNEL = 31
XATTN_HEADS = 4
XATTN_HEAD_DIM = D_MODEL // XATTN_HEADS
FFN_CONV = 3
RMS_EPS = 1e-6
IN_COLS = 2 * MLSTM_WIDTH + 2 * CONV_WIDTH + 2 * D_MODEL


def rmsnorm(x, g):
    xf = x.astype(jnp.float32)
    y = xf * lax.rsqrt(jnp.mean(xf * xf, -1, keepdims=True) + RMS_EPS)
    return (y * g.astype(jnp.float32)).astype(x.dtype)

def layernorm(x, g, b):
    xf = x.astype(jnp.float32)
    mu = jnp.mean(xf, -1, keepdims=True)
    var = jnp.mean(jnp.square(xf - mu), -1, keepdims=True)
    y = (xf - mu) * lax.rsqrt(var + LN_EPS)
    return (y * g.astype(jnp.float32) + b.astype(jnp.float32)).astype(x.dtype)

def causal_dwconv(x, w, b):
    K, C = w.shape
    y = lax.conv_general_dilated(
        x, w[:, None, :].astype(x.dtype), window_strides=(1,), padding=[(K - 1, 0)],
        dimension_numbers=("NWC", "WIO", "NWC"), feature_group_count=C)
    return y + b.astype(x.dtype)

def mlstm_chunkwise(q, k, v, i_pre, f_pre):
    B, H, S, dh = q.shape
    nc = S // CHUNK

    def to_chunks(t):
        t = t.reshape((B, H, nc, CHUNK) + t.shape[3:])
        return jnp.moveaxis(t, 2, 0)

    qc = to_chunks(q)
    kc = to_chunks(k * (dh ** -0.5))
    vc = to_chunks(v)
    ic = to_chunks(i_pre)
    lfc = to_chunks(jax.nn.log_sigmoid(f_pre))
    causal = jnp.tril(jnp.ones((CHUNK, CHUNK), dtype=bool))

    def step(carry, inp):
        C, n, m = carry
        q_, k_, v_, i_, lf_ = inp
        b = jnp.cumsum(lf_, axis=-1)
        a = b + m[..., None]
        dmat = b[..., :, None] - b[..., None, :] + i_[..., None, :]
        dmat = jnp.where(causal, dmat, -jnp.inf)
        m_row = jnp.maximum(a, jnp.max(dmat, axis=-1))
        w_inter = jnp.exp(a - m_row)
        s = jnp.einsum("bhld,bhsd->bhls", q_, k_) * jnp.exp(dmat - m_row[..., None])
        num = (jnp.einsum("bhls,bhsd->bhld", s, v_)
               + w_inter[..., None] * jnp.einsum("bhld,bhde->bhle", q_, C))
        den = jnp.sum(s, axis=-1) + w_inter * jnp.einsum("bhld,bhd->bhl", q_, n)
        h = num / jnp.maximum(jnp.abs(den), jnp.exp(-m_row))[..., None]
        b_end = b[..., -1]
        g = b_end[..., None] - b + i_
        m_new = jnp.maximum(b_end + m, jnp.max(g, axis=-1))
        decay = jnp.exp(b_end + m - m_new)
        wk = jnp.exp(g - m_new[..., None])[..., None] * k_
        C_new = decay[..., None, None] * C + jnp.einsum("bhld,bhle->bhde", wk, v_)
        n_new = decay[..., None] * n + jnp.sum(wk, axis=2)
        return (C_new, n_new, m_new), h

    init = (jnp.zeros((B, H, dh, dh), jnp.float32),
            jnp.zeros((B, H, dh), jnp.float32),
            jnp.zeros((B, H), jnp.float32))
    _, hc = lax.scan(step, init, (qc, kc, vc, ic, lfc))
    return jnp.moveaxis(hc, 0, 2).reshape(B, H, S, dh)

def mlstm_branch(xm, z, conv_w, conv_b, wq, wk, wv, w_gate, b_gate, norm_g, skip, w_down):
    B, S, W = xm.shape
    H, dh = MLSTM_HEADS, MLSTM_HEAD_DIM
    xc = jax.nn.silu(causal_dwconv(xm, conv_w, conv_b))

    def blockdiag(t, w):
        tb = t.reshape(B, S, W // QKV_BLOCK, QKV_BLOCK)
        return jnp.einsum("bsnc,ncd->bsnd", tb, w.astype(t.dtype)).reshape(B, S, W)

    q = blockdiag(xc, wq)
    k = blockdiag(xc, wk)
    v = blockdiag(xm, wv)
    gates = (jnp.concatenate([q, k, v], axis=-1) @ w_gate + b_gate).astype(jnp.float32)
    i_pre = jnp.transpose(gates[..., :H], (0, 2, 1))
    f_pre = jnp.transpose(gates[..., H:], (0, 2, 1))

    def heads(t):
        return jnp.transpose(t.reshape(B, S, H, dh), (0, 2, 1, 3)).astype(jnp.float32)

    h = mlstm_chunkwise(heads(q), heads(k), heads(v), i_pre, f_pre)
    mu = jnp.mean(h, -1, keepdims=True)
    var = jnp.mean(jnp.square(h - mu), -1, keepdims=True)
    hn = (h - mu) * lax.rsqrt(var + LN_EPS)
    hn = jnp.transpose(hn, (0, 2, 1, 3)).reshape(B, S, W).astype(xm.dtype) * norm_g
    out = (hn + skip * xc) * jax.nn.silu(z)
    return out @ w_down

def conformer_conv_branch(a, g, dw_w, dw_b, ln_g, ln_b, w_pw, b_pw):
    u = a * jax.nn.sigmoid(g)
    u = causal_dwconv(u, dw_w, dw_b)
    u = jax.nn.silu(layernorm(u, ln_g, ln_b))
    return u @ w_pw + b_pw

def cross_attention(h, mem_n, wq, wk, wv, wo):
    B, S, _ = h.shape
    N = mem_n.shape[1]
    q = (h @ wq).reshape(B, S, XATTN_HEADS, XATTN_HEAD_DIM)
    k = (mem_n @ wk).reshape(B, N, XATTN_HEADS, XATTN_HEAD_DIM)
    v = (mem_n @ wv).reshape(B, N, XATTN_HEADS, XATTN_HEAD_DIM)
    s = jnp.einsum("bshd,bnhd->bhsn", q, k).astype(jnp.float32) * (XATTN_HEAD_DIM ** -0.5)
    p = jax.nn.softmax(s, axis=-1).astype(v.dtype)
    o = jnp.einsum("bhsn,bnhd->bshd", p, v).reshape(B, S, D_MODEL)
    return o @ wo

def conv_ffn(h, w_up, b_up, dw_w, dw_b, w_down):
    u = causal_dwconv(h @ w_up + b_up, dw_w, dw_b)
    gate, val = u[..., :D_FF], u[..., D_FF:]
    return (jax.nn.silu(gate) * val) @ w_down

def second_inputs(seed: int = 0) -> dict:
    key = jax.random.key(seed)
    ks = iter(jax.random.split(key, 48))

    def nrm(shape, scale):
        return jax.random.normal(next(ks), shape, jnp.float32) * scale

    L, D, W, CW, F, H = DEPTH, D_MODEL, MLSTM_WIDTH, CONV_WIDTH, D_FF, MLSTM_HEADS
    nb = W // QKV_BLOCK
    f_bias = jnp.broadcast_to(jnp.linspace(3.0, 6.0, H, dtype=jnp.float32), (L, H)) + nrm((L, H), 0.01)
    ml_b_gate = jnp.concatenate([nrm((L, H), 0.1), f_bias], axis=-1)
    return {
        "x": nrm((BATCH, SEQ, D), 1.0),
        "mem": nrm((BATCH, N_MEM, D), 1.0),
        "norm_mix": 1.0 + nrm((L, D), 0.02),
        "w_in": nrm((L, D, IN_COLS), D ** -0.5),
        "b_in": nrm((L, IN_COLS), 0.02),
        "ml_conv_w": nrm((L, MLSTM_CONV, W), MLSTM_CONV ** -0.5),
        "ml_conv_b": nrm((L, W), 0.02),
        "ml_wq": nrm((L, nb, QKV_BLOCK, QKV_BLOCK), QKV_BLOCK ** -0.5),
        "ml_wk": nrm((L, nb, QKV_BLOCK, QKV_BLOCK), QKV_BLOCK ** -0.5),
        "ml_wv": nrm((L, nb, QKV_BLOCK, QKV_BLOCK), QKV_BLOCK ** -0.5),
        "ml_w_gate": nrm((L, 3 * W, 2 * H), (3 * W) ** -0.5),
        "ml_b_gate": ml_b_gate,
        "ml_norm_g": 1.0 + nrm((L, W), 0.02),
        "ml_skip": 1.0 + nrm((L, W), 0.02),
        "ml_w_down": nrm((L, W, D), W ** -0.5),
        "cv_dw_w": nrm((L, CONV_KERNEL, CW), CONV_KERNEL ** -0.5),
        "cv_dw_b": nrm((L, CW), 0.02),
        "cv_ln_g": 1.0 + nrm((L, CW), 0.02),
        "cv_ln_b": nrm((L, CW), 0.02),
        "cv_w_pw": nrm((L, CW, D), CW ** -0.5),
        "cv_b_pw": nrm((L, D), 0.02),
        "w_out": nrm((L, D, D), D ** -0.5),
        "norm_x": 1.0 + nrm((L, D), 0.02),
        "norm_mem": 1.0 + nrm((L, D), 0.02),
        "xa_wq": nrm((L, D, D), D ** -0.5),
        "xa_wk": nrm((L, D, D), D ** -0.5),
        "xa_wv": nrm((L, D, D), D ** -0.5),
        "xa_wo": nrm((L, D, D), D ** -0.5),
        "norm_ffn": 1.0 + nrm((L, D), 0.02),
        "ffn_w_up": nrm((L, D, 2 * F), D ** -0.5),
        "ffn_b_up": nrm((L, 2 * F), 0.02),
        "ffn_dw_w": nrm((L, FFN_CONV, 2 * F), FFN_CONV ** -0.5),
        "ffn_dw_b": nrm((L, 2 * F), 0.02),
        "ffn_w_down": nrm((L, F, D), F ** -0.5),
        "final_norm": 1.0 + nrm((D,), 0.02),
    }

def second_block(x, mem, norm_mix, w_in, b_in, ml_conv_w, ml_conv_b, ml_wq, ml_wk, ml_wv,
              ml_w_gate, ml_b_gate, ml_norm_g, ml_skip, ml_w_down, cv_dw_w, cv_dw_b,
              cv_ln_g, cv_ln_b, cv_w_pw, cv_b_pw, w_out, norm_x, norm_mem, xa_wq, xa_wk,
              xa_wv, xa_wo, norm_ffn, ffn_w_up, ffn_b_up, ffn_dw_w, ffn_dw_b, ffn_w_down,
              final_norm):
    W, CW, D = MLSTM_WIDTH, CONV_WIDTH, D_MODEL
    o1, o2, o3, o4, o5 = W, 2 * W, 2 * W + CW, 2 * W + 2 * CW, 2 * W + 2 * CW + D
    for l in range(DEPTH):
        h = rmsnorm(x, norm_mix[l])
        p = h @ w_in[l] + b_in[l]
        y_m = mlstm_branch(p[..., :o1], p[..., o1:o2], ml_conv_w[l], ml_conv_b[l],
                           ml_wq[l], ml_wk[l], ml_wv[l], ml_w_gate[l], ml_b_gate[l],
                           ml_norm_g[l], ml_skip[l], ml_w_down[l])
        y_c = conformer_conv_branch(p[..., o2:o3], p[..., o3:o4], cv_dw_w[l], cv_dw_b[l],
                                    cv_ln_g[l], cv_ln_b[l], cv_w_pw[l], cv_b_pw[l])
        merged = jax.nn.sigmoid(p[..., o4:o5]) * y_m + jax.nn.sigmoid(p[..., o5:]) * y_c
        x = x + merged @ w_out[l]
        x = x + cross_attention(rmsnorm(x, norm_x[l]), rmsnorm(mem, norm_mem[l]),
                                xa_wq[l], xa_wk[l], xa_wv[l], xa_wo[l])
        x = x + conv_ffn(rmsnorm(x, norm_ffn[l]), ffn_w_up[l], ffn_b_up[l],
                         ffn_dw_w[l], ffn_dw_b[l], ffn_w_down[l])
    return rmsnorm(x, final_norm)


def setup_inputs(seed=0):
    out = dict(first_inputs(seed))
    for name, value in second_inputs(seed + 1).items():
        if name != "x":
            out[name + "_2"] = value
    return out


def reference(
    x, c, positions, rel_bias, w_ada, b_ada, w_in, w_out, conv_w, conv_b, dt_bias, a_log,
    d_skip, ssd_norm_w, sinks, ln_g, ln_b, ffn_w_gate, ffn_w_up, ffn_w_down, router_w, router_b,
    expert_w_gate, expert_w_up, expert_w_down, mem_2, norm_mix_2, w_in_2, b_in_2, ml_conv_w_2,
    ml_conv_b_2, ml_wq_2, ml_wk_2, ml_wv_2, ml_w_gate_2, ml_b_gate_2, ml_norm_g_2, ml_skip_2,
    ml_w_down_2, cv_dw_w_2, cv_dw_b_2, cv_ln_g_2, cv_ln_b_2, cv_w_pw_2, cv_b_pw_2, w_out_2,
    norm_x_2, norm_mem_2, xa_wq_2, xa_wk_2, xa_wv_2, xa_wo_2, norm_ffn_2, ffn_w_up_2,
    ffn_b_up_2, ffn_dw_w_2, ffn_dw_b_2, ffn_w_down_2, final_norm_2,
):
    x = first_block(
        x, c, positions, rel_bias, w_ada, b_ada, w_in, w_out, conv_w, conv_b, dt_bias, a_log,
        d_skip, ssd_norm_w, sinks, ln_g, ln_b, ffn_w_gate, ffn_w_up, ffn_w_down, router_w,
        router_b, expert_w_gate, expert_w_up, expert_w_down,
    )
    return second_block(
        x, mem_2, norm_mix_2, w_in_2, b_in_2, ml_conv_w_2, ml_conv_b_2, ml_wq_2, ml_wk_2,
        ml_wv_2, ml_w_gate_2, ml_b_gate_2, ml_norm_g_2, ml_skip_2, ml_w_down_2, cv_dw_w_2,
        cv_dw_b_2, cv_ln_g_2, cv_ln_b_2, cv_w_pw_2, cv_b_pw_2, w_out_2, norm_x_2, norm_mem_2,
        xa_wq_2, xa_wk_2, xa_wv_2, xa_wo_2, norm_ffn_2, ffn_w_up_2, ffn_b_up_2, ffn_dw_w_2,
        ffn_dw_b_2, ffn_w_down_2, final_norm_2,
    )


_drawn_inputs = setup_inputs


def setup_inputs(seed=0):
    import zlib

    import numpy as np

    out = dict(_drawn_inputs(seed))
    spreads = {}
    factors = {'conv_b': 3.517,
     'ssd_norm_w': 2.783,
     'sinks': 7.304,
     'router_b': 4.965,
     'ml_conv_b_2': 3.308,
     'ml_norm_g_2': 6.043,
     'ml_skip_2': 8.0,
     'cv_ln_g_2': 4.883,
     'cv_ln_b_2': 5.718,
     'cv_b_pw_2': 3.518,
     'norm_x_2': 8.0,
     'norm_mem_2': 8.0,
     'norm_ffn_2': 2.706,
     'ffn_b_up_2': 2.691,
     'ffn_dw_b_2': 2.776,
     'final_norm_2': 2.786}
    for name, (base, spread) in spreads.items():
        noise = np.random.default_rng([zlib.crc32(name.encode()), seed]).standard_normal(out[name].shape)
        drawn = base * np.exp(spread * noise) if base else spread * noise
        out[name] = __import__('jax').numpy.asarray(drawn.astype(out[name].dtype))
    for name, factor in factors.items():
        out[name] = (out[name] * factor).astype(out[name].dtype)
    return out
```

```python
import math

import numpy as np
import concourse.bass as bass
from concourse import mybir
from contextlib import ExitStack

F32 = mybir.dt.float32
F32R = mybir.dt.float32r
I32 = mybir.dt.int32
ACT = mybir.ActivationFunctionType
ALU = mybir.AluOpType
AX = mybir.AxisListType.X
AP = bass.AP

D = 1024
S = 256
D_FF = 2816
NEXP = 8
D_EXP = 3584
ALPHA = 4.0 ** 0.25
LN_EPS = 1e-5
RMS_EPS = 1e-6
NEG = -1.0e30
NRAW = 4
NH = 3
USZ = 2048
ARENA = 16680

C_ID, C_ONE, C_TRI, C_NEG, C_SW = 0, 128, 256, 384, 640
C_DEC, C_INV, C_BD, C_LOW, C_HOT = 768, 1792, 1824, 1856, 1920
C_N = 1920 + 384


def constants():
    c = np.zeros((128, C_N), np.float64)
    p = np.arange(128)
    c[:, C_ID:C_ID + 128] = np.eye(128)
    c[:, C_ONE:C_ONE + 128] = 1.0
    c[:, C_TRI:C_TRI + 128] = p[None, :] >= p[:, None]
    c[:, C_NEG:C_NEG + 128] = np.where(p[None, :] >= p[:, None], 0.0, NEG)
    c[:, C_SW:C_SW + 128] = np.roll(np.eye(128), 64, axis=1)
    l = np.arange(256)
    diff = l[None, :] - p[:, None]
    for h in range(4):
        lg = np.log1p(-2.0 ** (-5.0 - h))
        c[:, C_DEC + 256 * h:C_DEC + 256 * h + 256] = np.where(diff >= 0, np.exp(lg * np.maximum(diff, 0)), 0.0) * 0.125
    half = 32
    c[:, C_INV:C_INV + 32] = np.exp(np.float32(-math.log(10000.0)) * np.arange(half, dtype=np.float32) / np.float32(half))
    c[:, C_BD:C_BD + 32] = np.arange(32)[None, :] == (p[:, None] // 4)
    e = np.arange(8)
    c[:, C_LOW:C_LOW + 64] = (e[None, :] < e[:, None]).reshape(-1)
    dist = 255 - np.arange(384)
    ok = (dist >= 0) & (dist < 128)
    dc = np.clip(dist, 1, 127).astype(np.float32)
    large = 16 + (np.log(dc / np.float32(16)) / np.float32(math.log(8.0)) * np.float32(16)).astype(np.int32)
    bucket = np.where(dist < 16, np.maximum(dist, 0), np.minimum(large, 31))
    for b in range(32):
        c[b, C_HOT:C_HOT + 384] = ok & (bucket == b)
    c[32, C_HOT:C_HOT + 384] = np.where(ok, 0.0, NEG)
    return c.astype(np.float32)


def param_rows(A):
    rows = [("c", 8, A["c"].rearrange("a (r q) -> (a r) q", q=128))]
    for l in range(2):
        rows.append((f"b_ada{l}", 48, A["b_ada"][l].rearrange("(r q) -> r q", q=128)))
        rows.append((f"conv_w{l}", 24, A["conv_w"][l].rearrange("k (r q) -> (k r) q", q=128)))
        rows.append((f"conv_b{l}", 6, A["conv_b"][l].rearrange("(r q) -> r q", q=128)))
        rows.append((f"ssd_norm{l}", 4, A["ssd_norm_w"][l].rearrange("(r q) -> r q", q=128)))
    for l in range(2):
        for nm, r in (("norm_mix", 8), ("b_in", 48), ("ml_conv_b", 8), ("ml_norm_g", 8), ("ml_skip", 8),
                      ("cv_dw_b", 8), ("cv_ln_g", 8), ("cv_ln_b", 8), ("cv_b_pw", 8), ("norm_x", 8),
                      ("norm_mem", 8), ("norm_ffn", 8), ("ffn_b_up", 44), ("ffn_dw_b", 44)):
            rows.append((f"{nm}{l}", r, A[nm + "_2"][l].rearrange("(r q) -> r q", q=128)))
        for nm, r in (("ml_conv_w", 32), ("cv_dw_w", 248), ("ffn_dw_w", 132)):
            rows.append((f"{nm}{l}", r, A[nm + "_2"][l].rearrange("k (r q) -> (k r) q", q=128)))
    return rows



def u_fm(w, n0, n1, key):
    return [(key, w[:, n:min(n + 256, n1)].rearrange("(c p) n -> p c n", p=128), True) for n in range(n0, n1, 256)]


def u_tm(w, k0, k1, key):
    return [(key, w[128 * k:128 * (k + 2), :].rearrange("(c p) n -> p c n", p=128), True) for k in range(k0, k1, 2)]


def u_blk(w, n0, n1, key, kc=4):
    return [(key, w[128 * k:128 * (k + kc), n0:n1].rearrange("(c p) n -> p c n", p=128), True) for k in range(0, 8, kc)]


def u_ffn(wg, wu, wd, n_pairs, up0, key):
    out = []
    for p in range(n_pairs + 1):
        if p < n_pairs:
            out += u_fm(wg, 256 * p, 256 * p + 256, key + "g")
            out += u_fm(wu, up0 + 256 * p, up0 + 256 * p + 256, key + "u")
        if p > 0:
            out += u_tm(wd, 2 * p - 2, 2 * p, key + "d")
    return out


def stream_plan(A):
    out = []
    for l in range(2):
        out += [(k, a, False) for k, a, _ in u_fm(A["w_ada"][l], 0, 6144, f"ada{l}")]
    for l in range(2):
        w = A["w_in"][l]
        for n in (0, 512, 1024):
            out += u_blk(w, n, n + 512, f"in{l}")
        out += u_fm(w, 1536, 2304, f"in{l}") + u_fm(w, 2312, 2568, f"in{l}") + u_fm(w, 2568, 2696, f"in{l}")
        out += u_blk(w, 2696, 2824, f"in{l}", 8) + u_blk(w, 2304, 2312, f"in{l}", 8)
        out += u_tm(A["w_out"][l], 0, 8, f"out{l}")
        if l == 0:
            out += u_ffn(A["ffn_w_gate"][0], A["ffn_w_up"][0], A["ffn_w_down"][0], 11, 0, "ffn")
        else:
            for e in range(NEXP):
                out += u_ffn(A["expert_w_gate"][0, e], A["expert_w_up"][0, e], A["expert_w_down"][0, e], 14, 0, f"moe{e}")
    for l in range(2):
        w = A["w_in_2"][l]
        for n in (0, 2048, 3072, 1024):
            out += u_fm(w, n, n + 1024, f"in2{l}")
        out += u_fm(A["ml_w_down_2"][l], 0, 1024, f"mld{l}")
        for n in (4096, 5120):
            out += u_fm(w, n, n + 1024, f"in2{l}")
        out += u_fm(A["cv_w_pw_2"][l], 0, 1024, f"cvp{l}")
        out += u_tm(A["w_out_2"][l], 0, 8, f"out2{l}")
        out += u_fm(A["xa_wk_2"][l], 0, 1024, f"xk{l}")
        out += u_tm(A["xa_wv_2"][l], 0, 8, f"xv{l}")
        out += u_fm(A["xa_wq_2"][l], 0, 1024, f"xq{l}")
        out += u_tm(A["xa_wo_2"][l], 0, 8, f"xo{l}")
        out += u_ffn(A["ffn_w_up_2"][l], A["ffn_w_up_2"][l], A["ffn_w_down_2"][l], 11, D_FF, f"ff2{l}")
    return out


class Core:

    def __init__(self, nc, ctx):
        self.nc, self.ctx = nc, ctx
        self.engines = {"v": nc.vector, "a": nc.scalar, "g": nc.gpsimd, "t": nc.tensor, "s": nc.sync}
        self.sems = {e: self.sem("s_" + e) for e in "vagt"}
        self.count = {}
        self.seen = {e: {} for e in self.engines}
        self.last = {}

    def sem(self, name):
        return self.ctx.enter_context(self.nc.semaphore(name))

    def new(self, name):
        self.sems[name] = self.sem("d_" + name)
        return name

    def wait(self, eng, deps):
        for d in deps:
            if d is None:
                continue
            if isinstance(d, list):
                self.wait(eng, d)
                continue
            k, n = d
            if self.seen[eng].get(k, 0) < n:
                self.engines[eng].wait_ge(self.sems[k], n)
                self.seen[eng][k] = n

    def op(self, eng, f, deps):
        self.wait(eng, deps)
        ins = f(self.engines[eng])
        self.count[eng] = self.count.get(eng, 0) + 1
        ins.then_inc(self.sems[eng], 1)
        self.last[eng] = (eng, self.count[eng])
        return self.last[eng]

    def V(self, f, *deps):
        return self.op("v", f, deps)

    def A(self, f, *deps):
        return self.op("a", f, deps)

    def G(self, f, *deps):
        return self.op("g", f, deps)

    def T(self, f, *deps):
        return self.op("t", f, deps)

    def dma(self, eng, sem, out, in_, *deps):
        self.wait(eng, deps)
        self.engines[eng].dma_start(out, in_).then_inc(self.sems[sem], 16)
        self.count[sem] = self.count.get(sem, 0) + 16
        return (sem, self.count[sem])

    def fence(self):
        marks = [self.last[e] for e in self.last]
        for e in "vagt":
            self.wait(e, marks)
        return marks


def view(ap, *dims):
    return AP(ap.tensor, ap.offset, [list(ap.ap[0])] + [list(d) for d in dims])


def build_program(nc, A, out, dbg=None):
    with ExitStack() as ctx:
        emit_program(nc, ctx, A, out, dbg)


def emit_program(nc, ctx, A, out, dbg):
    K = Core(nc, ctx)
    V, ACTE, G, T = K.V, K.A, K.G, K.T

    def sb(name, shape, dt=F32):
        return ctx.enter_context(nc.sbuf_tensor(name, shape, dt))

    RAW = sb("RAW", [128, NRAW, USZ])
    HI = sb("HI", [128, NH, USZ], F32R)
    LO = sb("LO", [128, NH, USZ], F32R)
    X1H, X1L = sb("X1H", [128, 8, 256], F32R), sb("X1L", [128, 8, 256], F32R)
    X2H, X2L = sb("X2H", [128, 8, 256], F32R), sb("X2L", [128, 8, 256], F32R)
    X = sb("X", [128, 2, D])
    CST = sb("CST", [128, C_HOT])
    PC = sb("PC", [128, 12 * 128])
    AR = sb("AR", [128, ARENA])
    MOD = sb("MOD", [128, 2, 48])
    BT = sb("BT", [128, 4, 256])
    SM = sb("SM", [128, 640])
    PS = ctx.enter_context(nc.psum_tensor("PS", [128, 8, 512], F32))

    ident = CST[:, C_ID:C_ID + 128]
    ones = CST[:, C_ONE:C_ONE + 128]
    tri = CST[:, C_TRI:C_TRI + 128]
    negm = CST[:, C_NEG:C_NEG + 256]
    swap = CST[:, C_SW:C_SW + 128]

    def ar(off, *shape):
        n = int(np.prod(shape))
        assert off + n <= ARENA, (off, shape)
        a = AR[:, off:off + n]
        if len(shape) == 2:
            a = a.rearrange("p (a b) -> p a b", a=shape[0])
        if len(shape) == 3:
            a = a.rearrange("p (a b c) -> p a b c", a=shape[0], b=shape[1])
        return a

    sm_at = [0]

    def sm(*shape):
        n = int(np.prod(shape))
        o = sm_at[0]
        sm_at[0] += n
        assert sm_at[0] <= 640
        a = SM[:, o:o + n]
        if len(shape) == 2:
            a = a.rearrange("p (a b) -> p a b", a=shape[0])
        if len(shape) == 3:
            a = a.rearrange("p (a b c) -> p a b c", a=shape[0], b=shape[1])
        return a

    plan = stream_plan(A)
    raw_sem = [K.new(f"raw{i}") for i in range(NRAW)]
    raw_free = [None] * NRAW
    hl_free = [None] * NH
    landed, split_of = {}, {}
    st = {"dma": 0, "split": 0, "next": 0, "slot": 0}
    hslot = {}
    n_split = [0]

    def uview(tile, slot, a):
        return tile[:, slot, 0:a.shape[1] * a.shape[2]].rearrange("p (c n) -> p c n", c=a.shape[1])

    def issue_dma():
        i = st["dma"]
        if i >= len(plan):
            return
        s = i % NRAW
        landed[i] = K.dma("s", raw_sem[s], uview(RAW, s, plan[i][1]), plan[i][1], raw_free[s])
        st["dma"] += 1

    def issue_split():
        i = st["split"]
        if i >= len(plan) or i not in landed:
            return
        st["split"] += 1
        if not plan[i][2]:
            return
        s, h = i % NRAW, n_split[0] % NH
        n_split[0] += 1
        n = plan[i][1].shape[1] * plan[i][1].shape[2]
        hslot[i] = h
        r, hi, lo = RAW[:, s, 0:n], HI[:, h, 0:n], LO[:, h, 0:n]
        t1 = ACTE(lambda e: e.activation(hi, r, ACT.Copy), landed[i], hl_free[h])
        on = V if n_split[0] % 2 else G
        t2 = on(lambda e: e.tensor_tensor(lo, r, hi.bitcast(F32), ALU.subtract), landed[i], t1, hl_free[h])
        split_of[i] = [t1, t2]
        raw_free[s] = [t1, t2]
        issue_dma()

    def take(key):
        i = st["next"]
        assert plan[i][0] == key, (plan[i][0], key)
        st["next"] += 1
        if plan[i][2]:
            a = plan[i][1]
            return i, uview(HI, hslot[i], a), uview(LO, hslot[i], a), split_of[i]
        return i, uview(RAW, i % NRAW, plan[i][1]), None, landed[i]

    def done(i, tok):
        if plan[i][2]:
            hl_free[hslot[i]] = tok
            issue_split()
        else:
            raw_free[i % NRAW] = tok
            issue_dma()

    pf = [None] * 8

    def mm3(e, o, lh, ll, rh, rl, first, last, skip=False):
        e.matmul(o, lh, rh, start=first, stop=False, skip_group_check=skip)
        e.matmul(o, lh, rl, start=False, stop=False, skip_group_check=skip)
        return e.matmul(o, ll, rh, start=False, stop=last, skip_group_check=skip)

    def gemm_fm(key, ncols, act, banks, evac):
        XH, XL, ready = act
        for j, n0 in enumerate(range(0, ncols, 256)):
            w = min(256, ncols - n0)
            b = banks[j % len(banks)]
            i, hi, lo, got = take(key)

            def f(e):
                for nb in range(w // 128):
                    o = PS[:, b, 256 * nb:256 * nb + 256]
                    for kc in range(8):
                        c = slice(128 * nb, 128 * nb + 128)
                        m = mm3(e, o, hi[:, kc, c], lo[:, kc, c], XH[:, kc, :], XL[:, kc, :], kc == 0, kc == 7)
                return m
            t = T(f, got, ready, pf[b])
            pf[b] = evac(j, PS[:, b, 0:w * 2], t)
            done(i, t)

    def mm_down(e, hi, lo, LH, LL, banks, kcs, first, last):
        for c in range(kcs):
            for t in range(2):
                for nb in range(2):
                    o = PS[:, banks[2 * t + nb], :]
                    ts, ns = slice(128 * t, 128 * t + 128), slice(512 * nb, 512 * nb + 512)
                    m = mm3(e, o, LH(c)[:, ts], LL(c)[:, ts], hi[:, c, ns], lo[:, c, ns],
                            first and c == 0, last and c == kcs - 1)
        return m

    def gemm_tm(key, act, banks):
        XH, XL, ready = act
        for j in range(4):
            i, hi, lo, got = take(key)
            t = T(lambda e: mm3_tm(e, hi, lo, XH, XL, 2 * j, banks), got, ready, [pf[b] for b in banks])
            done(i, t)
        return t

    def mm3_tm(e, hi, lo, XH, XL, k0, banks):
        return mm_down(e, hi, lo, lambda c: XH[:, k0 + c, :], lambda c: XL[:, k0 + c, :], banks, 2, k0 == 0, k0 == 6)

    def gemm_blk(key, act, banks, width, kc):
        XH, XL, ready = act
        for k0 in range(0, 8, kc):
            i, hi, lo, got = take(key)

            def f(e):
                for c in range(kc):
                    for t in range(2):
                        ts = slice(128 * t, 128 * t + 128)
                        m = mm3(e, PS[:, banks[t], 0:width], XH[:, k0 + c, ts], XL[:, k0 + c, ts], hi[:, c, :],
                                lo[:, c, :], k0 + c == 0, k0 + c == 7)
                return m
            t = T(f, got, ready, [pf[b] for b in banks])
            done(i, t)
        return t

    def split_act(src, H, L, *deps):
        t1 = ACTE(lambda e: e.activation(H, src, ACT.Copy), *deps)
        t2 = V(lambda e: e.tensor_tensor(L, src, H.bitcast(F32), ALU.subtract), t1, *deps)
        return [t1, t2]

    def transposes(dst_bank, parts, *deps):
        def f(e):
            for d, s_ in parts:
                n = s_.shape[0]
                m = e.transpose(d, s_, ident[0:n, 0:n])
            return m
        return T(f, pf[dst_bank], *deps)

    def to_fm(src, H, L, banks, deps, evac=None, prev=None):
        ready = []
        for cp in range(4):
            b = banks[cp % len(banks)]
            t = transposes(b, [(PS[:, b, 256 * ci + 128 * tt:256 * ci + 128 * tt + 128],
                                src[:, tt, 128 * (2 * cp + ci):128 * (2 * cp + ci) + 128])
                               for ci in range(2) for tt in range(2)], deps)
            p = PS[:, b, :].rearrange("p (c n) -> p c n", c=2)
            hs = (H[:, 2 * cp:2 * cp + 2, :], L[:, 2 * cp:2 * cp + 2, :])
            if evac is None:
                r = split_act(p, hs[0], hs[1], t, prev)
                pf[b] = r
            else:
                te = [evac(2 * cp + ci, p[:, ci, :], t, XF[:, 2 * cp + ci, :]) for ci in range(2)]
                pf[b] = te
                r = split_act(XF[:, 2 * cp:2 * cp + 2, :], hs[0], hs[1], te, prev)
            ready += r
        return (H, L, ready)

    XF = ar(0, 8, 256)

    def pcol(name, i=0):
        o = pc_at[name] + i
        return PC[:, o:o + 1]

    def pcols(name, n, i=0):
        o = pc_at[name] + i
        return PC[:, o:o + n]

    def rsqrt(dst, src, eps, *deps):
        t = V(lambda e: e.tensor_scalar(dst, src, eps, None, ALU.add), *deps)
        t = ACTE(lambda e: e.activation(dst, dst, ACT.Ln), t)
        return ACTE(lambda e: e.activation(dst, dst, ACT.Exp, scale=-0.5), t)

    def rstd_of(mv, rs, *deps):
        return rsqrt(rs, mv, LN_EPS, *deps)

    def bn(src, stats, mv, *deps):
        n = src.shape[1]
        k = max(1, n // 512)
        t = None
        for i in range(k):
            t = V(lambda e: e.bn_stats(stats[:, 6 * i:6 * i + 6], src[:, i * (n // k):(i + 1) * (n // k)]), *deps)
        return V(lambda e: e.bn_aggr(mv, stats[:, 0:6 * k]), t)

    STT = sm(2, 12)
    MV = sm(2, 2)
    RS = sm(2)
    dtb, alog, dsk = sm(2, 8), sm(2, 8), sm(2, 8)
    snk, rbias, mbg = sm(2, 4), sm(8), sm(2, 8)
    pos_i = SM[:, sm_at[0]:sm_at[0] + 2].bitcast(I32)
    sm(2)
    posf = sm(2)
    COS, SIN = sm(2, 32), sm(2, 32)
    relb = sm(4)

    d0 = K.new("cst")
    d1 = K.new("par")
    d2 = K.new("xin")
    d3 = K.new("bt")
    d4 = K.new("ln")
    d5 = K.new("misc")
    rows = param_rows(A)
    PR = ar(0, 12, 128)
    HOT = ar(6144, 384)
    pc_at = {}
    at = 0
    n = 0
    for name, r, src in rows:
        pc_at[name] = at
        o = 0
        while o < r:
            k = min(r - o, 128 - (at + o) % 128)
            K.dma("a" if n % 2 else "s", d1, PR[(at + o) % 128:(at + o) % 128 + k, (at + o) // 128, :], src[o:o + k, :])
            o += k
            n += 1
        at += r
        if name == "c":
            K.dma("s", d0, CST[:, :], A["cst"][:, 0:C_HOT])
            K.dma("s", d0, HOT, A["cst"][:, C_HOT:C_N])
            for _ in range(NRAW):
                issue_dma()
    n_pr = -(-at // 128)
    assert n_pr <= 12
    last_rows = at - 128 * (n_pr - 1)
    for k in range(2):
        K.dma("a", d2, X[:, k, :], A["x"][0, 128 * k:128 * k + 128, :])
        K.dma("s", d2, pos_i[:, k:k + 1], A["positions"][0, 128 * k:128 * k + 128].rearrange("(p a) -> p a", a=1))
    for dst, src, cnt in ((dtb, A["dt_bias"], 16), (alog, A["a_log"], 16), (dsk, A["d_skip"], 16), (snk, A["sinks"], 8),
                          (rbias, A["router_b"], 8), (mbg, A["ml_b_gate_2"], 16)):
        flat = view(dst, [1, cnt])
        K.dma("s", d2, flat, AP(src.tensor, src.offset, [[0, 128], [1, cnt]]))
    V(lambda e: e.memset(relb[0:64, :], 1.0))
    K.dma("a", d2, relb[0:32, :], A["rel_bias"], K.last["v"])
    WR = sb("WR", [128, 8, 8])
    K.dma("a", d5, WR[:, :, :], A["router_w"][0].rearrange("(c p) n -> p c n", p=128))
    cst, par, xin, misc = (d0, 32), (d1, K.count[d1]), (d2, K.count[d2]), (d5, K.count[d5])
    for e in "vagt":
        K.wait(e, [cst, par, xin, misc])

    for i in range(n_pr):
        b = i % 4
        r = 128 if i < n_pr - 1 else last_rows
        t = transposes(b, [(PS[:, b, 0:r], PR[0:r, i, :])])
        pf[b] = V(lambda e: e.tensor_copy(PC[:, 128 * i:128 * i + r], PS[:, b, 0:r]), t)
    t_pc = pf[b]

    ang = ar(2048, 2, 32)
    kk = ar(2112, 2, 32)
    t = V(lambda e: e.tensor_copy(posf, pos_i))
    for k in range(2):
        t2 = V(lambda e: e.tensor_scalar(ang[:, k, :], CST[:, C_INV:C_INV + 32], posf[:, k:k + 1], None, ALU.mult), t)
    MAGIC = 12582912.0
    t = V(lambda e: e.tensor_scalar(kk, ang, 1.0 / (2 * math.pi), MAGIC, ALU.mult, ALU.add), t2)
    t = V(lambda e: e.tensor_scalar(kk, kk, MAGIC, None, ALU.subtract), t)
    c1 = 6.28125
    c2 = float((np.array([2 * math.pi - c1], np.float32).view(np.uint32) & np.uint32(0xFFFFF000)).view(np.float32)[0])
    c3 = 2 * math.pi - c1 - c2
    for cc in (c1, c2, c3):
        t = V(lambda e: e.scalar_tensor_tensor(ang, kk, -cc, ang, ALU.mult, ALU.add), t)
    t = V(lambda e: e.tensor_scalar(ang, ang, math.pi, -math.pi, ALU.min, ALU.max), t)
    t1 = ACTE(lambda e: e.activation(SIN, ang, ACT.Sin), t)
    t2 = ACTE(lambda e: e.activation(COS, ang, ACT.Sin, scale=0.5), t)
    t = V(lambda e: e.tensor_tensor(COS, COS, COS, ALU.mult), t2)
    t_rot = [t1, V(lambda e: e.tensor_scalar(COS, COS, -2.0, 1.0, ALU.mult, ALU.add), t)]

    RB = ar(4096, 4, 384)
    scr = nc.dram_tensor("scr_bias", [4, 128, 384], F32)
    for h in range(4):
        b = 4 + h
        lhs = view(relb[0:33, h:h + 1], [0, 128])
        t = T(lambda e: e.matmul(PS[:, b, 0:384], lhs, HOT[0:33, :], start=True, stop=True), pf[b])
        t = ACTE(lambda e: e.activation(RB[:, h, :], PS[:, b, 0:384], ACT.Copy), t)
        pf[b] = t
    tb = K.dma("a", d3, scr[:].rearrange("h p n -> p h n"), RB, t)
    scr0 = scr[0, 0:1, 0:1]
    for h in range(4):
        tb2 = K.dma("a", d3, BT[:, h, :], AP(scr0.tensor, h * 128 * 384 + 127, [[383, 128], [1, 256]]), tb)
    t_bt = tb2

    tmod = []
    for l in range(2):
        for j in range(24):
            i, raw, _, got = take(f"ada{l}")

            def f(e):
                for nb in range(2):
                    for kc in range(8):
                        m = e.matmul(PS[:, l, 2 * j + nb:2 * j + nb + 1], raw[:, kc, 128 * nb:128 * nb + 128],
                                     pcol("c", kc), start=(kc == 0), stop=(kc == 7))
                return m
            t = T(f, got, t_pc, pf[l])
            done(i, t)
        if l == 1:
            st["split"] = 48
            for _ in range(NH):
                issue_split()
        pf[l] = V(lambda e: e.tensor_tensor(MOD[:, l, :], PS[:, l, 0:48], pcols(f"b_ada{l}", 48), ALU.add), t)
        t = pf[l]
        for o in (8, 16, 32, 40):
            t = V(lambda e: e.tensor_scalar(MOD[:, l, o:o + 8], MOD[:, l, o:o + 8], 1.0, None, ALU.add), t)
        tmod.append(t)
    marks = K.fence()

    def modc(l, part, c):
        return MOD[:, l, 8 * part + c:8 * part + c + 1]

    def scaled(scale, bias):
        def evac(c, p, t, dst):
            return V(lambda e: e.tensor_scalar(dst, p, scale(c), bias(c) if bias else None, ALU.mult,
                                               ALU.add if bias else ALU.bypass), t)
        return evac

    LNR = ar(2048, 2, 1024)
    GB = ar(4096, 1024)
    DG = ar(5120, 8, 128)

    def residual(l, j, banks, tok):
        part = 2 if j == 0 else 5
        tl = K.dma("s", d4, LNR[:, 0, :], AP(A["ln_g"].tensor, A["ln_g"].offset + (2 * l + j) * D, [[0, 128], [1, D]]),
                   K.last["t"], K.last["v"], K.last["a"], K.last["g"])
        tl = K.dma("s", d4, LNR[:, 1, :], AP(A["ln_b"].tensor, A["ln_b"].offset + (2 * l + j) * D, [[0, 128], [1, D]]))
        t = None
        for c in range(8):
            t = V(lambda e: e.tensor_scalar(DG[:, c, :], ident, modc(l, part, c), None, ALU.mult))
        for h in range(2):
            b = h
            t2 = T(lambda e: [e.matmul(PS[:, b, 128 * c:128 * c + 128], ones, DG[:, 4 * h + c, :], start=True, stop=True)
                              for c in range(4)][-1], t, pf[b])
            pf[b] = ACTE(lambda e: e.activation(GB[:, 512 * h:512 * h + 512], PS[:, b, :], ACT.Copy), t2)
        tg = [pf[0], pf[1]]
        TT = ar(0, 2, 1024)
        for k in range(2):
            for nb in range(2):
                b = banks[2 * k + nb]
                pf[b] = V(lambda e: e.tensor_tensor(TT[:, k, 512 * nb:512 * nb + 512], PS[:, b, :],
                                                    GB[:, 512 * nb:512 * nb + 512], ALU.mult), tok, tg)
            t = V(lambda e: e.scalar_tensor_tensor(X[:, k, :], X[:, k, :], ALPHA, TT[:, k, :], ALU.mult, ALU.add),
                  K.last["v"], K.last["t"])
            t = bn(X[:, k, :], STT[:, k, :], MV[:, k, :], t)
        t = rstd_of(MV[:, :, 1], RS, t)
        for k in range(2):
            t1 = V(lambda e: e.tensor_scalar(X[:, k, :], X[:, k, :], MV[:, k, 0:1], RS[:, k:k + 1], ALU.subtract,
                                             ALU.mult), t)
            t1 = V(lambda e: e.tensor_tensor(X[:, k, :], X[:, k, :], LNR[:, 0, :], ALU.mult), t1, tl)
            t1 = V(lambda e: e.tensor_tensor(X[:, k, :], X[:, k, :], LNR[:, 1, :], ALU.add), t1)
        return t1

    def ffn(key, n_pairs, act, evac_h, first, last):
        ring = {}
        prev = [None]
        RH = X2H[:, :, :].rearrange("p a b -> p (a b)").rearrange("p (s c n) -> p s c n", s=4, c=2)
        RL = X2L[:, :, :].rearrange("p a b -> p (a b)").rearrange("p (s c n) -> p s c n", s=4, c=2)
        XH, XL, ready = act
        for p in range(n_pairs + 1):
            if p < n_pairs:
                s_ = p % 3
                got2 = []
                for half, kk_ in ((0, "g"), (1, "u")):
                    b = (p % 2) * 2 + half
                    i, hi, lo, got = take(key + kk_)

                    def f(e):
                        for nb in range(2):
                            for kc in range(8):
                                c = slice(128 * nb, 128 * nb + 128)
                                m = mm3(e, PS[:, b, 256 * nb:256 * nb + 256], hi[:, kc, c], lo[:, kc, c],
                                        XH[:, kc, :], XL[:, kc, :], kc == 0, kc == 7)
                        return m
                    t = T(f, got, ready, pf[b])
                    got2.append((b, t))
                    done(i, t)
                hf, tf = evac_h(p, got2)
                ring[p] = split_act(hf, RH[:, s_].rearrange("p c n -> p (c n)"), RL[:, s_].rearrange("p c n -> p (c n)"),
                                    tf, ring.get(("down", p - 3)))
            if p > 0:
                q = p - 1
                i, hi, lo, got = take(key + "d")
                RHs, RLs = RH[:, q % 3], RL[:, q % 3]
                t = T(lambda e: mm_down(e, hi, lo, lambda c: RHs[:, c, :], lambda c: RLs[:, c, :], [4, 5, 6, 7], 2,
                                        first and q == 0, last and q == n_pairs - 1),
                      got, ring[q], [pf[b] for b in (4, 5, 6, 7)] if first and q == 0 else None)
                ring[("down", q)] = t
                done(i, t)
        return t

    SG = ar(6144, 2, 512)
    HF = ar(7168, 2, 512)
    GT = ar(8192, 8, 256)
    hst = {"n": 0}

    def swiglu_evac(gate):
        def evac(p, got):
            n_ = hst["n"] % 2
            hst["n"] += 1
            (bg, tg_), (bu, tu) = got
            t = ACTE(lambda e: e.activation(SG[:, n_, :], PS[:, bg, :], ACT.Silu), tg_, hst.get(("hf", n_)))
            pf[bg] = t
            t = V(lambda e: e.tensor_tensor(HF[:, n_, :], SG[:, n_, :], PS[:, bu, :], ALU.mult), t, tu,
                  hst.get(("sp", n_)))
            pf[bu] = t
            hst[("hf", n_)] = t
            if gate is not None:
                hv = HF[:, n_, :].rearrange("p (c n) -> p c n", c=2)
                t = V(lambda e: e.tensor_tensor(hv, hv, view(GT[:, gate, :], [0, 2], [1, 256]), ALU.mult), t)
            hst[("sp", n_)] = t
            return HF[:, n_, :], t
        return evac

    def layer1(l):
        marks = K.fence()
        act = to_fm(X, X1H, X1L, [4, 5], marks, scaled(lambda c: modc(l, 1, c), lambda c: modc(l, 0, c)))
        R = ar(6144, 2, 1024)
        SZ = ar(8192, 2, 512)
        XP = ar(9216, 6, 259)
        XC = ar(10770, 6, 256)
        QK = ar(12306, 4, 256)
        AVD = ar(13330, 2, 136)
        XS = ar(13602, 2, 512)
        XD = ar(14626, 2, 512)
        QT = ar(15650, 4, 256)
        E8 = ar(0, 8, 384)
        RT = ar(3072, 4, 384)
        LG = ar(4608, 4, 384)
        PT = ar(9216, 4, 384)
        f0 = K.fence()
        for blk in range(3):
            bb = [[0, 1], [2, 3], [0, 1]][blk]
            t = gemm_blk(f"in{l}", act, bb, 512, 4)
            for k in range(2):
                dst = R[:, k, 512 * blk:512 * blk + 512] if blk < 2 else SZ[:, k, :]
                fn = ACT.Copy if blk < 2 else ACT.Silu
                pf[bb[k]] = ACTE(lambda e: e.activation(dst, PS[:, bb[k], :], fn), t, f0)
        t_r = K.last["a"]
        t_sz = t_r
        tz = G(lambda e: e.memset(XP[:, :, 0:3], 0.0), f0)

        txp = []

        def ev_x(j, p, t):
            r = ACTE(lambda e: e.activation(XP[:, 2 * j:2 * j + 2, 3:259], p.rearrange("p (c n) -> p c n", c=2),
                                            ACT.Copy), t, tz)
            txp.append(r)
            return [r]
        gemm_fm(f"in{l}", 768, act, [4, 5], ev_x)

        def ev_q(j, p, t):
            return [ACTE(lambda e: e.activation(QK[:, 0:2, :], p.rearrange("p (c n) -> p c n", c=2), ACT.Copy), t)]
        gemm_fm(f"in{l}", 256, act, [6], ev_q)

        def ev_k(j, p, t):
            return [ACTE(lambda e: e.activation(QK[:, 2, :], p, ACT.Copy), t)]
        gemm_fm(f"in{l}", 128, act, [7], ev_k)
        t_k = K.last["a"]
        t = gemm_blk(f"in{l}", act, [2, 3], 128, 8)
        for k in range(2):
            pf[2 + k] = ACTE(lambda e: e.activation(AVD[:, k, 0:128], PS[:, 2 + k, 0:128], ACT.Copy), t)
        t = gemm_blk(f"in{l}", act, [0, 1], 8, 8)
        for k in range(2):
            pf[k] = ACTE(lambda e: e.activation(AVD[:, k, 128:136], PS[:, k, 0:8], ACT.Copy), t)
        t_av = K.last["a"]
        t = T(lambda e: e.matmul(PS[:, 6, 0:256], swap, QK[:, 2, :], start=True, stop=True), t_k, pf[6])
        t_ks = pf[6] = ACTE(lambda e: e.activation(QK[:, 3, :], PS[:, 6, 0:256], ACT.Copy), t)

        tcv = []
        for c in range(6):
            dst = XC[:, c, :]
            t = V(lambda e: e.tensor_scalar(dst, XP[:, c, 0:256], pcol(f"conv_w{l}", c), pcol(f"conv_b{l}", c),
                                            ALU.mult, ALU.add), txp, tz)
            for k in range(1, 4):
                t = V(lambda e: e.scalar_tensor_tensor(dst, XP[:, c, k:k + 256], pcol(f"conv_w{l}", 6 * k + c), dst,
                                                       ALU.mult, ALU.add), t)
            tcv.append(t)
        t_xc = ACTE(lambda e: e.activation(XC, XC, ACT.Silu), tcv)

        rq = R[:, :, 0:512].rearrange("p t (h x d) -> p t h x d", h=8, x=2)
        tmp = [ar(512 * i, 2, 8, 32) for i in range(4)]
        bc = lambda tab: AP(tab.tensor, tab.offset, [list(tab.ap[0]), [32, 2], [0, 8], [1, 32]])
        ops = ((0, COS), (1, SIN), (0, SIN), (1, COS))
        for i, (half, tab) in enumerate(ops):
            t = V(lambda e: e.tensor_tensor(tmp[i], rq[:, :, :, half, :], bc(tab), ALU.mult), t_r, t_rot, f0)
        t = V(lambda e: e.tensor_tensor(rq[:, :, :, 0, :], tmp[0], tmp[1], ALU.subtract), t)
        t = V(lambda e: e.tensor_tensor(rq[:, :, :, 1, :], tmp[2], tmp[3], ALU.add), t)
        for cp in range(2):
            b = 6 + cp
            t2 = transposes(b, [(PS[:, b, 256 * ci + 128 * tt:256 * ci + 128 * tt + 128],
                                 R[:, tt, 128 * (2 * cp + ci):128 * (2 * cp + ci) + 128])
                                for ci in range(2) for tt in range(2)], t)
            pf[b] = ACTE(lambda e: e.activation(QT[:, 2 * cp:2 * cp + 2, :], PS[:, b, :].rearrange(
                "p (c n) -> p c n", c=2), ACT.Copy), t2)
        t_qt = [pf[6], pf[7]]
        tr = []
        for h in range(4):
            b = 4 + h % 2
            pr, ch = slice(64 * (h % 2), 64 * (h % 2) + 64), h // 2

            def f(e):
                e.matmul(PS[:, b, 0:256], QT[pr, 2 + ch, 0:128], QT[pr, ch, :], start=True, stop=True)
                return e.matmul(PS[:, b, 256:384], QT[pr, 2 + ch, 128:256], QT[pr, ch, 128:256], start=True, stop=True)
            t = T(f, t_qt, pf[b])
            dec = CST[:, C_DEC + 256 * h:C_DEC + 256 * h + 256]
            V(lambda e: e.tensor_tensor(RT[:, h, 0:256], PS[:, b, 0:256], dec, ALU.mult), t, f0)
            pf[b] = V(lambda e: e.tensor_tensor(RT[:, h, 256:384], PS[:, b, 256:384], dec[:, 0:128], ALU.mult), t)
            tr.append(pf[b])
        rv = lambda k, h: R[:, k, 512 + 64 * h:512 + 64 * h + 64]

        def f(e):
            for h in range(4):
                e.matmul(PS[:, 0, 64 * h:64 * h + 64], RT[:, h, 0:128], rv(0, h), start=True, stop=True)
                e.matmul(PS[:, 0, 256 + 64 * h:256 + 64 * h + 64], RT[:, h, 128:256], rv(0, h), start=True, stop=False)
                m = e.matmul(PS[:, 0, 256 + 64 * h:256 + 64 * h + 64], RT[:, h, 256:384], rv(1, h), start=False,
                             stop=True)
            return m
        t = T(f, tr, t_r, pf[0])
        O8 = ar(2048, 8, 64)
        O8s = ar(2560, 8, 64)
        m8, v8 = SMT[:, 0:8], SMT[:, 8:16]
        b8 = lambda a: view(a, [1, 8], [0, 64])
        po = PS[:, 0, :].rearrange("p (a b) -> p a b", a=8)
        t = V(lambda e: e.tensor_reduce(m8, po, AX, ALU.add), t, f0)
        t = V(lambda e: e.tensor_scalar(m8, m8, 1.0 / 64, None, ALU.mult), t)
        t = V(lambda e: e.tensor_tensor(O8, po, b8(m8), ALU.subtract), t)
        pf[0] = t
        t = V(lambda e: e.tensor_tensor(O8s, O8, O8, ALU.mult), t)
        t = V(lambda e: e.tensor_reduce(v8, O8s, AX, ALU.add), t)
        t = V(lambda e: e.tensor_scalar(v8, v8, 1.0 / 64, None, ALU.mult), t)
        t = rsqrt(v8, v8, LN_EPS, t)
        t = V(lambda e: e.tensor_tensor(O8, O8, b8(v8), ALU.mult), t)
        t2 = ACTE(lambda e: e.activation(R[:, :, 768:1024], R[:, :, 768:1024], ACT.Silu), t_r)
        t_ret = V(lambda e: e.tensor_tensor(R[:, :, 0:256], R[:, :, 768:1024],
                                            O8.rearrange("p (t h) d -> p t (h d)", t=2), ALU.mult), t, t2,
                  K.last["t"])

        for c in range(4):
            b = 1 + c % 2
            t = transposes(b, [(PS[:, b, 128 * tt:128 * tt + 128], XC[:, c, 128 * tt:128 * tt + 128])
                               for tt in range(2)], t_xc)
            pf[b] = ACTE(lambda e: e.activation(XS[:, :, 128 * c:128 * c + 128], PS[:, b, 0:256].rearrange(
                "p (t n) -> p t n", t=2), ACT.Copy), t, f0)
        t_xs = pf[b]
        DTt, AA, T8, U8, CS, CSN = [SMT[:, 16 + 16 * i:32 + 16 * i] for i in range(6)]
        g2 = lambda a: a.rearrange("p (t h) -> p t h", t=2)
        dtr = AVD[:, :, 128:136]
        t = V(lambda e: e.tensor_tensor(g2(DTt), dtr, view(dtb[:, l, :], [0, 2], [1, 8]), ALU.add), t_av)
        t = softplus(DTt, DTt, 1.0, (T8, U8, CS, CSN, AA), t)
        t_dt = t
        ta = ACTE(lambda e: e.activation(T8[:, 0:8], alog[:, l, :], ACT.Exp), t)
        t = V(lambda e: e.scalar_tensor_tensor(g2(AA), g2(DTt), -1.0, view(T8, [0, 2], [1, 8]), ALU.mult, ALU.mult), t,
              ta)
        t_a = t

        def f(e):
            e.matmul(PS[:, 3, 0:8], tri, AA[:, 0:8], start=True, stop=True)
            e.matmul(PS[:, 3, 8:16], ones, AA[:, 0:8], start=True, stop=False)
            return e.matmul(PS[:, 3, 8:16], tri, AA[:, 8:16], start=False, stop=True)
        t = T(f, t, pf[3])
        pf[3] = t_cs = V(lambda e: e.tensor_copy(CS, PS[:, 3, 0:16]), t)
        t_xd = V(lambda e: e.tensor_tensor(XD.rearrange("p t (h d) -> p t h d", h=8),
                                           XS.rearrange("p t (h d) -> p t h d", h=8),
                                           view(DTt, [8, 2], [1, 8], [0, 64]), ALU.mult), t_xs, t_dt, f0)
        tt2 = []
        for h in range(8):
            b = 4 + h % 4
            col = lambda k: view(AA[:, 8 * k + h:8 * k + h + 1], [0, 128])

            def f(e):
                e.matmul(PS[:, b, 0:128], col(0), tri, start=True, stop=True)
                e.matmul(PS[:, b, 128:256], col(0), ones, start=True, stop=False)
                return e.matmul(PS[:, b, 128:256], col(1), tri, start=False, stop=True)
            t = T(f, t_a, pf[b])
            V(lambda e: e.scalar_tensor_tensor(E8[:, h, 0:256], negm, CS[:, h:h + 1], PS[:, b, 0:256], ALU.subtract,
                                               ALU.add), t, t_cs, t_ret)
            pf[b] = V(lambda e: e.scalar_tensor_tensor(E8[:, h, 256:384], negm[:, 0:128], CS[:, 8 + h:9 + h],
                                                       PS[:, b, 128:256], ALU.subtract, ALU.add), t, t_cs)
            tt2.append(pf[b])
        t_e = ACTE(lambda e: e.activation(E8, E8, ACT.Exp), tt2)
        for g in range(2):
            b = 2 + g
            pr = slice(64 * g, 64 * g + 64)

            def f(e):
                e.matmul(PS[:, b, 0:256], XC[pr, 4, 0:128], XC[pr, 5, :], start=True, stop=True)
                return e.matmul(PS[:, b, 256:384], XC[pr, 4, 128:256], XC[pr, 5, 128:256], start=True, stop=True)
            t = T(f, t_xc, pf[b])
            for r in range(4):
                h = 4 * g + r
                t2 = V(lambda e: e.tensor_tensor(E8[:, h, :], E8[:, h, :], PS[:, b, 0:384], ALU.mult), t, t_e)
            pf[b] = t2

        def f(e):
            for h in range(8):
                v = lambda k: XD[:, k, 64 * h:64 * h + 64]
                e.matmul(PS[:, 4, 64 * h:64 * h + 64], E8[:, h, 0:128], v(0), start=True, stop=True)
                e.matmul(PS[:, 5, 64 * h:64 * h + 64], E8[:, h, 128:256], v(0), start=True, stop=False)
                m = e.matmul(PS[:, 5, 64 * h:64 * h + 64], E8[:, h, 256:384], v(1), start=False, stop=True)
            return m
        t = T(f, t2, t_xd, pf[4], pf[5])
        h8 = lambda a: a.rearrange("p t (h d) -> p t h d", h=8)
        t3 = V(lambda e: e.tensor_tensor(h8(XS), h8(XS), view(dsk[:, l, :], [0, 2], [1, 8], [0, 64]), ALU.mult), t_xd)
        for k in range(2):
            pf[4 + k] = V(lambda e: e.tensor_tensor(XS[:, k, :], PS[:, 4 + k, :], XS[:, k, :], ALU.add), t, t3)
        t = V(lambda e: e.tensor_tensor(XS, XS, SZ, ALU.mult), pf[4], pf[5], t_sz)
        t = V(lambda e: e.tensor_tensor(XD, XS, XS, ALU.mult), t, K.last["t"])
        m4 = SMT[:, 0:4]
        t = V(lambda e: e.tensor_reduce(m4, XD.rearrange("p t (g d) -> p (t g) d", g=2), AX, ALU.add), t, t_ret)
        t = V(lambda e: e.tensor_scalar(m4, m4, 1.0 / 256, None, ALU.mult), t)
        t = rsqrt(m4, m4, LN_EPS, t)
        t_ssd = V(lambda e: e.tensor_tensor(R[:, :, 256:768].rearrange("p t (g d) -> p t g d", g=2),
                                            XS.rearrange("p t (g d) -> p t g d", g=2),
                                            view(m4, [2, 2], [1, 2], [0, 256]), ALU.mult), t, K.last["t"], t_ret)

        mx, ng, den, ek = [SMT[:, 128 + 8 * i:136 + 8 * i] for i in range(4)]
        for h in range(4):
            b = 4 + h
            base, kv = 64 * (h % 2), h // 2
            kc = 2 if base == 64 * kv else 3
            pr = slice(base, base + 64)

            def f(e):
                e.matmul(PS[:, b, 0:128], QK[pr, h // 2, 0:128], QK[pr, kc, 0:128], start=True, stop=True)
                return e.matmul(PS[:, b, 128:384], QK[pr, h // 2, 128:256], QK[pr, kc, :], start=True, stop=True)
            t = T(f, t_ks, t_k, pf[b])
            V(lambda e: e.scalar_tensor_tensor(LG[:, h, 0:128], PS[:, b, 0:128], 0.125, BT[:, h, 128:256], ALU.mult,
                                               ALU.add), t, t_bt, f0)
            pf[b] = V(lambda e: e.scalar_tensor_tensor(LG[:, h, 128:384], PS[:, b, 128:384], 0.125, BT[:, h, :],
                                                       ALU.mult, ALU.add), t)
        t = pf[7]
        V(lambda e: e.tensor_reduce(mx[:, 0:4], LG[:, :, 0:128], AX, ALU.max), t)
        t = V(lambda e: e.tensor_reduce(mx[:, 4:8], LG[:, :, 128:384], AX, ALU.max), t)
        t = V(lambda e: e.tensor_tensor(g2(mx), g2(mx), view(snk[:, l, :], [0, 2], [1, 4]), ALU.max), t)
        tn = V(lambda e: e.tensor_scalar(ng, mx, -1.0, None, ALU.mult), t)
        t = V(lambda e: e.tensor_tensor(g2(ek), g2(ng), view(snk[:, l, :], [0, 2], [1, 4]), ALU.add), tn)
        t5 = ACTE(lambda e: e.activation(ek, ek, ACT.Exp), t)
        for h in range(4):
            ACTE(lambda e: e.activation(LG[:, h, 0:128], LG[:, h, 0:128], ACT.Exp, bias=ng[:, h:h + 1],
                                        accum_out=den[:, h:h + 1]), tn)
            t = ACTE(lambda e: e.activation(LG[:, h, 128:384], LG[:, h, 128:384], ACT.Exp, bias=ng[:, 4 + h:5 + h],
                                            accum_out=den[:, 4 + h:5 + h]), tn)
        t = V(lambda e: e.tensor_tensor(den, den, ek, ALU.add), t, t5)
        t_den = V(lambda e: e.reciprocal(den, den), t)
        tp = []
        for h in range(4):
            b = 4 + h
            t = transposes(b, [(PS[:, b, 128 * i:128 * i + 128], LG[:, h, 128 * i:128 * i + 128]) for i in range(3)],
                           t_den)
            pf[b] = ACTE(lambda e: e.activation(PT[:, h, :], PS[:, b, 0:384], ACT.Copy), t, tcv)
            tp.append(pf[b])

        def f(e):
            for h in range(4):
                v = lambda k: AVD[:, k, 64 * (h // 2):64 * (h // 2) + 64]
                e.matmul(PS[:, 0, 64 * h:64 * h + 64], PT[:, h, 0:128], v(0), start=True, stop=True)
                e.matmul(PS[:, 0, 256 + 64 * h:256 + 64 * h + 64], PT[:, h, 128:256], v(0), start=True, stop=False)
                m = e.matmul(PS[:, 0, 256 + 64 * h:256 + 64 * h + 64], PT[:, h, 256:384], v(1), start=False, stop=True)
            return m
        t = T(f, tp, t_av, pf[0])
        pf[0] = V(lambda e: e.tensor_tensor(R[:, :, 768:1024].rearrange("p t (h d) -> p t h d", h=4),
                                            PS[:, 0, :].rearrange("p (t h d) -> p t h d", t=2, h=4),
                                            view(den, [4, 2], [1, 4], [0, 64]), ALU.mult), t, t_den, t_ret)
        t = [pf[0], t_ssd, t_ret]
        if dbg:
            dbg(K, f"mix{l}", R, t)
        marks = K.fence()

        def ev(c, p, t, dst):
            if 2 <= c < 6:
                return V(lambda e: e.tensor_scalar(dst, p, pcol(f"ssd_norm{l}", c - 2), None, ALU.mult), t)
            return V(lambda e: e.tensor_copy(dst, p), t)
        act = to_fm(R, X2H, X2L, [2, 3], marks, ev)
        t = gemm_tm(f"out{l}", act, [4, 5, 6, 7])
        t = residual(l, 0, [4, 5, 6, 7], t)
        if dbg:
            dbg(K, f"xa{l}", X, [t])
        marks = K.fence()
        act = to_fm(X, X1H, X1L, [2, 3], marks, scaled(lambda c: modc(l, 4, c), lambda c: modc(l, 3, c)))
        if l == 0:
            t = ffn("ffn", 11, act, swiglu_evac(None), True, True)
        else:
            tg_ = router(act)
            for e in range(NEXP):
                t = ffn(f"moe{e}", 14, act, swiglu_evac(e), e == 0, e == NEXP - 1)
        t = residual(l, 1, [4, 5, 6, 7], t)
        if dbg:
            dbg(K, f"x{l}", X, [t])

    SMT = sm(256)

    def softplus(dst, src, sign, tmps, *deps):
        a, tt_, u, w, z = tmps
        t = V(lambda e: e.tensor_scalar(a, src, sign, None, ALU.mult), *deps)
        t = ACTE(lambda e: e.activation(tt_, a, ACT.Abs), t)
        t = ACTE(lambda e: e.activation(tt_, tt_, ACT.Exp, scale=-1.0), t)
        t = V(lambda e: e.tensor_scalar(u, tt_, 1.0, None, ALU.add), t)
        t2 = ACTE(lambda e: e.activation(w, u, ACT.Ln), t)
        t = V(lambda e: e.tensor_scalar(u, u, -1.0, None, ALU.add), t, t2)
        t = V(lambda e: e.tensor_scalar(z, u, 0.0, None, ALU.is_equal), t)
        t = V(lambda e: e.tensor_tensor(u, u, z, ALU.add), t)
        t = V(lambda e: e.reciprocal(u, u), t)
        t = V(lambda e: e.tensor_tensor(w, w, tt_, ALU.mult), t)
        t = V(lambda e: e.tensor_tensor(w, w, u, ALU.mult), t)
        t = V(lambda e: e.tensor_tensor(z, z, tt_, ALU.mult), t)
        t = V(lambda e: e.tensor_tensor(w, w, z, ALU.add), t)
        return V(lambda e: e.scalar_tensor_tensor(dst, a, 0.0, w, ALU.max, ALU.add), t)

    def router(act):
        XH, XL, ready = act
        LGT, CMP, CM2, RK, GG = (ar(10240, 2, 8), ar(10256, 2, 8, 8), ar(10384, 2, 8, 8), ar(10512, 2, 8),
                                 ar(10528, 2, 8))
        m1, den = ar(10544, 2), ar(10546, 2)
        DGT = ar(10560, 16, 128)

        def f(e):
            for k in range(2):
                for c in range(8):
                    m = e.matmul(PS[:, 0, 8 * k:8 * k + 8], XF[:, c, 128 * k:128 * k + 128], WR[:, c, :],
                                 start=(c == 0), stop=(c == 7))
            return m
        t = T(f, ready, pf[0])
        t = V(lambda e: e.tensor_tensor(LGT, PS[:, 0, 0:16].rearrange("p (k n) -> p k n", k=2),
                                        view(rbias, [0, 2], [1, 8]), ALU.add), t)
        pf[0] = t
        mine = view(LGT, [8, 2], [1, 8], [0, 8])
        other = view(LGT, [8, 2], [0, 8], [1, 8])
        low = view(CST[:, C_LOW:C_LOW + 64], [0, 2], [8, 8], [1, 8])
        t1 = V(lambda e: e.tensor_tensor(CMP, other, mine, ALU.is_gt), t)
        t2 = V(lambda e: e.tensor_tensor(CM2, other, mine, ALU.is_equal), t)
        t2 = V(lambda e: e.tensor_tensor(CM2, CM2, low, ALU.mult), t2)
        t2 = V(lambda e: e.tensor_tensor(CMP, CMP, CM2, ALU.add), t1, t2)
        t2 = V(lambda e: e.tensor_reduce(RK, CMP, AX, ALU.add), t2)
        t2 = V(lambda e: e.tensor_scalar(RK, RK, 1.5, None, ALU.is_lt), t2)
        t = V(lambda e: e.tensor_reduce(m1, LGT, AX, ALU.max), t)
        t = V(lambda e: e.tensor_tensor(GG, LGT, view(m1, [1, 2], [0, 8]), ALU.subtract), t)
        t = ACTE(lambda e: e.activation(GG, GG, ACT.Exp), t)
        t = V(lambda e: e.tensor_tensor(GG, GG, RK, ALU.mult), t, t2)
        t = V(lambda e: e.tensor_reduce(den, GG, AX, ALU.add), t)
        t = V(lambda e: e.reciprocal(den, den), t)
        t = V(lambda e: e.tensor_tensor(GG, GG, view(den, [1, 2], [0, 8]), ALU.mult), t)
        for e_ in range(8):
            for k in range(2):
                t2 = V(lambda e: e.tensor_scalar(DGT[:, 2 * e_ + k, :], ident, GG[:, k, e_:e_ + 1], None, ALU.mult), t)
        for q in range(4):
            b = q
            t = T(lambda e: [e.matmul(PS[:, b, 128 * j:128 * j + 128], ones, DGT[:, 4 * q + j, :], start=True, stop=True)
                             for j in range(4)][-1], t2, pf[b])
            t3 = ACTE(lambda e: e.activation(GT[:, 2 * q:2 * q + 2, :], PS[:, b, :].rearrange(
                "p (c n) -> p c n", c=2), ACT.Copy), t)
            pf[b] = t3
        marks_ = K.fence()
        return t3

    U = BT[:, :, :].rearrange("p h n -> p (h n)")
    WG = U[:, 0:384].rearrange("p (l c n) -> p l c n", l=2, c=24)
    WB = U[:, 384:576].rearrange("p (j n) -> p j n", j=6)

    def load_small():
        marks = K.fence()
        for l in range(2):
            K.dma("a", d5, WG[:, l], A["ml_w_gate_2"][l].rearrange("(c p) n -> p c n", p=128), marks)
            for j, nm in enumerate(("ml_wq_2", "ml_wk_2", "ml_wv_2")):
                K.dma("a", d5, WB[:, 3 * l + j, :].rearrange("p (c d) -> p c d", d=4),
                      A[nm][l].rearrange("(c n) k d -> (n k) c d", n=32))
        return (d5, K.count[d5])

    def rms(src, dst, *deps):
        for k in range(2):
            t = ACTE(lambda e: e.activation(dst[:, k, :], src[:, k, :], ACT.Square, accum_out=RS[:, k:k + 1]), *deps)
        t = V(lambda e: e.tensor_scalar(RS, RS, 1.0 / D, None, ALU.mult), t)
        t = rsqrt(RS, RS, RMS_EPS, t)
        for k in range(2):
            t2 = V(lambda e: e.tensor_scalar(dst[:, k, :], src[:, k, :], RS[:, k:k + 1], None, ALU.mult), t)
        return t2

    def by_col(name):
        def evac(c, p, t, dst):
            return V(lambda e: e.tensor_scalar(dst, p, pcol(name, c), None, ALU.mult), t)
        return evac

    def add_x(banks, t):
        for k in range(2):
            for nb in range(2):
                b = banks[2 * k + nb]
                xs = X[:, k, 512 * nb:512 * nb + 512]
                pf[b] = V(lambda e: e.tensor_tensor(xs, xs, PS[:, b, :], ALU.add), t)
        return pf[b]

    def fm_to(dst, func, name, off, pad=0, extra=None, into=None):
        def evac(j, p, t):
            for ci in range(2):
                c = 2 * j + ci
                o = dst[:, c, pad:pad + 256]
                s_ = p[:, 256 * ci:256 * ci + 256]
                if name is None:
                    r = ACTE(lambda e: e.activation(o, s_, func), t, extra)
                else:
                    r = ACTE(lambda e: e.activation(o, s_, func, bias=pcol(name, off + c)), t, extra)
            if into is not None:
                into(j, r)
            return [r]
        return evac

    def layer2(l, t_small):
        XN = ar(2048, 2, 1024)
        XM = ar(2048, 8, 259)
        UP = ar(4120, 8, 286)
        XC = ar(6408, 8, 256)
        R8 = ar(8456, 8, 256)
        UC = ar(10504, 8, 256)
        QF = ar(12552, 8, 256)
        KF = ar(14600, 8, 256)
        VT = ar(0, 2, 1024)
        marks = K.fence()
        t = rms(X, XN, marks)
        act = to_fm(XN, X1H, X1L, [4, 5, 6, 7], t, by_col(f"norm_mix{l}"))
        tz = [G(lambda e: e.memset(UP[:, :, 0:30], 0.0), marks)]
        tz.append(G(lambda e: e.memset(XM[:, :, 0:3], 0.0), act[2]))
        gemm_fm(f"in2{l}", 1024, act, [0, 1], fm_to(XM, ACT.Identity, f"b_in{l}", 0, 3, tz))
        t_xm = K.last["a"]
        tcv = []
        for c in range(8):
            dst = XC[:, c, :]
            t = V(lambda e: e.tensor_scalar(dst, XM[:, c, 0:256], pcol(f"ml_conv_w{l}", c), pcol(f"ml_conv_b{l}", c),
                                            ALU.mult, ALU.add), t_xm, tz)
            for k in range(1, 4):
                t = V(lambda e: e.scalar_tensor_tensor(dst, XM[:, c, k:k + 256], pcol(f"ml_conv_w{l}", 8 * k + c), dst,
                                                       ALU.mult, ALU.add), t)
            tcv.append(t)
        t_xc = ACTE(lambda e: e.activation(XC, XC, ACT.Silu), tcv)
        gemm_fm(f"in2{l}", 1024, act, [0, 1], fm_to(UP, ACT.Identity, f"b_in{l}", 16, 30, tz))
        t_a = K.last["a"]

        def ev_g(j, p, t):
            for ci in range(2):
                c = 2 * j + ci
                r = ACTE(lambda e: e.activation(R8[:, c, :], p[:, 256 * ci:256 * ci + 256], ACT.Sigmoid,
                                                bias=pcol(f"b_in{l}", 24 + c)), t)
            V(lambda e: e.tensor_tensor(UP[:, 2 * j:2 * j + 2, 30:286], UP[:, 2 * j:2 * j + 2, 30:286],
                                        R8[:, 2 * j:2 * j + 2, :], ALU.mult), r, t_a)
            return [r]
        gemm_fm(f"in2{l}", 1024, act, [0, 1], ev_g)
        t_u = K.last["v"]

        bd = [UC[:, 4 * i:4 * i + 4, :].rearrange("p a b -> p (a b)").rearrange("p (c n) -> p c n", c=8)
              for i in range(2)]
        tq = {}
        prev = {}
        for j, src in enumerate((XC, XC, XM)):
            B_ = bd[j % 2]
            t = V(lambda e: e.tensor_tensor(view(B_, [128, 8], [4, 32], [1, 4]), view(WB[:, 3 * l + j, :], [4, 8], [0, 32],
                                            [1, 4]), view(CST[:, C_BD:C_BD + 32], [0, 8], [1, 32], [0, 4]), ALU.mult),
                  t_small, prev.get(j - 2), marks)
            dst = (QF, KF, R8)[j]
            off = 3 if j == 2 else 0
            for cp in range(4):
                b = 2 + cp % 2

                def f(e):
                    for ci in range(2):
                        c = 2 * cp + ci
                        m = e.matmul(PS[:, b, 256 * ci:256 * ci + 256], B_[:, c, :], src[:, c, off:off + 256],
                                     start=True, stop=True)
                    return m
                t2 = T(f, t, t_xc, t_xm, pf[b])
                pf[b] = ACTE(lambda e: e.activation(dst[:, 2 * cp:2 * cp + 2, :], PS[:, b, :].rearrange(
                    "p (c n) -> p c n", c=2), ACT.Copy), t2, t_u)
                prev[j] = t2
            tq[j] = pf[b]
        for k in range(2):
            for hf in range(2):
                b = 4 + 2 * k + hf
                t2 = T(lambda e: [e.matmul(PS[:, b, 128 * c:128 * c + 128], XM[:, 4 * hf + c, 3 + 128 * k:131 + 128 * k],
                                           B_[:, 4 * hf + c, :], start=True, stop=True) for c in range(4)][-1], pf[b])
                pf[b] = ACTE(lambda e: e.activation(VT[:, k, 512 * hf:512 * hf + 512], PS[:, b, :], ACT.Copy), t2,
                             act[2])
        t_vt = pf[b]
        t_bd = t2

        def f(e):
            for k in range(2):
                for i in range(24):
                    src = (QF, KF, R8)[i // 8]
                    m = e.matmul(PS[:, 0, 8 * k:8 * k + 8], src[:, i % 8, 128 * k:128 * k + 128], WG[:, l, i, :],
                                 start=(i == 0), stop=(i == 23))
            return m
        t = T(f, tq[0], tq[1], tq[2], pf[0])
        t_gt = t
        GA, SPF, CSF, Gc, NM, DN = [SMT[:, 16 * i:16 * i + 16] for i in range(6)]
        g2 = lambda a, n=8: a[:, 0:2 * n].rearrange("p (t h) -> p t h", t=2)
        pf[0] = V(lambda e: e.tensor_tensor(g2(GA), PS[:, 0, 0:16].rearrange("p (t h) -> p t h", t=2),
                                            view(mbg[:, l, :], [0, 2], [1, 8]), ALU.add), t, marks)
        t = softplus(SPF, GA, -1.0, [SMT[:, 96 + 16 * i:112 + 16 * i] for i in range(5)], pf[0])

        def f(e):
            e.matmul(PS[:, 1, 0:8], tri, SPF[:, 0:8], start=True, stop=True)
            e.matmul(PS[:, 1, 8:16], ones, SPF[:, 0:8], start=True, stop=False)
            return e.matmul(PS[:, 1, 8:16], tri, SPF[:, 8:16], start=False, stop=True)
        t = T(f, t, pf[1])
        t = pf[1] = V(lambda e: e.tensor_copy(CSF, PS[:, 1, 0:16]), t)
        t = V(lambda e: e.tensor_tensor(g2(Gc, 4), g2(GA)[:, :, 0:4], g2(CSF)[:, :, 4:8], ALU.add), t)
        t_g = t
        t = transposes(1, [(PS[0:4, 1, 128 * k:128 * k + 128], Gc[:, 4 * k:4 * k + 4]) for k in range(2)], t)
        GR, MR = ROWS[0:4, 0, :], ROWS[0:4, 1, :]
        pf[1] = V(lambda e: e.tensor_copy(GR, PS[0:4, 1, 0:256]), t)
        t = V(lambda e: e.tensor_tensor_scan(MR, GR, GR, 0.0, ALU.max, ALU.max), pf[1])
        t_mr = t
        t = transposes(1, [(PS[:, 1, 4 * k:4 * k + 4], MR[:, 128 * k:128 * k + 128]) for k in range(2)], t)
        pf[1] = V(lambda e: e.tensor_tensor(g2(NM, 4), g2(CSF)[:, :, 4:8], PS[:, 1, 0:8].rearrange(
            "p (t h) -> p t h", t=2), ALU.subtract), t)
        t_nm = ACTE(lambda e: e.activation(NM[:, 0:8], NM[:, 0:8], ACT.Exp), pf[1])
        EE = ar(8456, 4, 384)
        te = []
        for h in range(4):
            b = 4 + h
            t = T(lambda e: e.matmul(PS[:, b, 0:256], view(ident[0:4, h:h + 1], [0, 128]), MR, start=True, stop=True),
                  t_mr, pf[b])
            V(lambda e: e.scalar_tensor_tensor(EE[:, h, 0:256], negm, Gc[:, h:h + 1], PS[:, b, 0:256], ALU.add,
                                               ALU.subtract), t, t_g, t_gt)
            pf[b] = V(lambda e: e.scalar_tensor_tensor(EE[:, h, 256:384], negm[:, 0:128], Gc[:, 4 + h:5 + h],
                                                       PS[:, b, 128:256], ALU.add, ALU.subtract), t)
            te.append(ACTE(lambda e: e.activation(EE[:, h, :], EE[:, h, :], ACT.Exp), pf[b]))
        tp = []
        for h in range(4):
            b = 2 + h % 2

            def f(e):
                for c in (2 * h, 2 * h + 1):
                    e.matmul(PS[:, b, 0:256], KF[:, c, 0:128], QF[:, c, :], start=(c == 2 * h), stop=(c == 2 * h + 1))
                for c in (2 * h, 2 * h + 1):
                    m = e.matmul(PS[:, b, 256:384], KF[:, c, 128:256], QF[:, c, 128:256], start=(c == 2 * h),
                                 stop=(c == 2 * h + 1))
                return m
            t = T(f, tq[0], tq[1], pf[b])
            pf[b] = V(lambda e: e.scalar_tensor_tensor(EE[:, h, :], PS[:, b, 0:384], 0.0625, EE[:, h, :], ALU.mult,
                                                       ALU.mult), t, te[h])
            tp.append(pf[b])

        def f(e):
            for h in range(4):
                e.matmul(PS[:, 0, h:h + 1], EE[:, h, 0:128], ones[:, 0:1], start=True, stop=True)
                e.matmul(PS[:, 0, 4 + h:5 + h], EE[:, h, 128:256], ones[:, 0:1], start=True, stop=False)
                m = e.matmul(PS[:, 0, 4 + h:5 + h], EE[:, h, 256:384], ones[:, 0:1], start=False, stop=True)
            return m
        t = T(f, tp, pf[0])
        t = pf[0] = ACTE(lambda e: e.activation(DN[:, 0:8], PS[:, 0, 0:8], ACT.Abs), t)
        t = V(lambda e: e.tensor_tensor(DN[:, 0:8], DN[:, 0:8], NM[:, 0:8], ALU.max), t, t_nm)
        t_dn = V(lambda e: e.reciprocal(DN[:, 0:8], DN[:, 0:8]), t)
        HT = ar(2048, 2, 1024)
        MV8, R8s, ST8 = SMT[:, 96:112], SMT[:, 112:120], SMT[:, 176:224].rearrange("p (a b) -> p a b", a=8)
        for h in range(4):
            b = 4 + h

            def f(e):
                v = lambda k: VT[:, k, 256 * h:256 * h + 256]
                e.matmul(PS[:, b, 0:256], EE[:, h, 0:128], v(0), start=True, stop=True)
                e.matmul(PS[:, b, 256:512], EE[:, h, 128:256], v(0), start=True, stop=False)
                return e.matmul(PS[:, b, 256:512], EE[:, h, 256:384], v(1), start=False, stop=True)
            t = T(f, tp[h], t_vt, pf[b])
            for k in range(2):
                pf[b] = V(lambda e: e.tensor_scalar(HT[:, k, 256 * h:256 * h + 256], PS[:, b, 256 * k:256 * k + 256],
                                                    DN[:, 4 * k + h:4 * k + h + 1], None, ALU.mult), t, t_dn, t_bd)
        t = pf[7]
        for i in range(8):
            k, h = i // 4, i % 4
            t2 = V(lambda e: e.bn_stats(ST8[:, i, :], HT[:, k, 256 * h:256 * h + 256]), t)
        for i in range(8):
            t = V(lambda e: e.bn_aggr(MV8[:, 2 * i:2 * i + 2], ST8[:, i, :]), t2)
        t = rsqrt(R8s, view(MV8[:, 1:2], [2, 8]), LN_EPS, t)
        for i in range(8):
            k, h = i // 4, i % 4
            hv = HT[:, k, 256 * h:256 * h + 256]
            t2 = V(lambda e: e.tensor_scalar(hv, hv, MV8[:, 2 * i:2 * i + 1], R8s[:, i:i + 1], ALU.subtract, ALU.mult),
                   t)
        t_hn = t2
        for c in range(8):
            t_sk = ACTE(lambda e: e.activation(XC[:, c, :], XC[:, c, :], ACT.Copy, scale=pcol(f"ml_skip{l}", c)), t_bd)
        tuc = []

        def conv31(c, on):
            dst = UC[:, c, :]
            t = on(lambda e: e.tensor_scalar(dst, UP[:, c, 0:256], pcol(f"cv_dw_w{l}", c), pcol(f"cv_dw_b{l}", c),
                                             ALU.mult, ALU.add), t_u, t_bd)
            for k in range(1, 31):
                t = on(lambda e: e.scalar_tensor_tensor(dst, UP[:, c, k:k + 256], pcol(f"cv_dw_w{l}", 8 * k + c), dst,
                                                        ALU.mult, ALU.add), t)
            tuc.append(t)
        todo = [0, 1, 2, 3, 4, 5, 6, 7]

        def ev_z(j, p, t):
            for ci in range(2):
                c = 2 * j + ci
                r = ACTE(lambda e: e.activation(R8[:, c, :], p[:, 256 * ci:256 * ci + 256], ACT.Silu,
                                                bias=pcol(f"b_in{l}", 8 + c)), t, K.last["t"])
            conv31(todo.pop(0), V)
            return [r]
        gemm_fm(f"in2{l}", 1024, act, [0, 1], ev_z)
        t_z = K.last["a"]

        def ev(c, p, t, dst):
            t = V(lambda e: e.scalar_tensor_tensor(dst, p, pcol(f"ml_norm_g{l}", c), XC[:, c, :], ALU.mult, ALU.add), t,
                  t_sk)
            return V(lambda e: e.tensor_tensor(dst, dst, R8[:, c, :], ALU.mult), t, t_z)
        act2 = to_fm(HT, X2H, X2L, [2, 3], t_hn, ev)
        YM, YC = QF, R8

        def ev_y(dst, name):
            def evac(j, p, t):
                o = dst[:, 2 * j:2 * j + 2, :]
                s_ = p.rearrange("p (c n) -> p c n", c=2)
                if name is None:
                    r = ACTE(lambda e: e.activation(o, s_, ACT.Copy), t, K.last["v"])
                else:
                    for ci in range(2):
                        r = ACTE(lambda e: e.activation(o[:, ci, :], s_[:, ci, :], ACT.Identity,
                                                        bias=pcol(name, 2 * j + ci)), t, K.last["v"])
                if todo:
                    conv31(todo.pop(0), V)
                return [r]
            return evac
        gemm_fm(f"mld{l}", 1024, act2, [0, 1], ev_y(YM, None))
        t_ym = K.last["a"]
        while todo:
            conv31(todo.pop(0), V)
        UT = ar(14600, 2, 1024)
        for cp in range(4):
            b = 2 + cp % 2
            t = transposes(b, [(PS[:, b, 256 * tt + 128 * ci:256 * tt + 128 * ci + 128],
                                UC[:, 2 * cp + ci, 128 * tt:128 * tt + 128]) for ci in range(2) for tt in range(2)], tuc)
            pf[b] = ACTE(lambda e: e.activation(UT[:, :, 256 * cp:256 * cp + 256], PS[:, b, :].rearrange(
                "p (t n) -> p t n", t=2), ACT.Copy), t)
        t = pf[b]
        for k in range(2):
            t2 = bn(UT[:, k, :], STT[:, k, :], MV[:, k, :], t)
        t = rstd_of(MV[:, :, 1], RS, t2)
        for k in range(2):
            t2 = V(lambda e: e.tensor_scalar(UT[:, k, :], UT[:, k, :], MV[:, k, 0:1], RS[:, k:k + 1], ALU.subtract,
                                             ALU.mult), t)
        t_ut = t2
        GS = UC

        def ev_sig(off, into):
            def evac(j, p, t):
                for ci in range(2):
                    c = 2 * j + ci
                    r = ACTE(lambda e: e.activation(GS[:, c, :], p[:, 256 * ci:256 * ci + 256], ACT.Sigmoid,
                                                    bias=pcol(f"b_in{l}", off + c)), t, t_ut, K.last["v"])
                into(j, r)
                return [r]
            return evac

        def into_ym(j, r):
            o = YM[:, 2 * j:2 * j + 2, :]
            V(lambda e: e.tensor_tensor(o, o, GS[:, 2 * j:2 * j + 2, :], ALU.mult), r, t_ym)
        gemm_fm(f"in2{l}", 1024, act, [0, 1], ev_sig(32, into_ym))
        t_ymg = K.last["v"]

        def ev(c, p, t, dst):
            return ACTE(lambda e: e.activation(dst, p, ACT.Silu, bias=pcol(f"cv_ln_b{l}", c),
                                               scale=pcol(f"cv_ln_g{l}", c)), t, K.last["v"])

        act2 = to_fm(UT, X2H, X2L, [2, 3], t_ut, ev, K.last["t"])

        def into_keep(j, r):
            return None
        gemm_fm(f"in2{l}", 1024, act, [0, 1], ev_sig(40, into_keep))
        t_g5 = K.last["a"]

        def ev_c(j, p, t):
            o = YC[:, 2 * j:2 * j + 2, :]
            for ci in range(2):
                c = 2 * j + ci
                r = ACTE(lambda e: e.activation(YC[:, c, :], p[:, 256 * ci:256 * ci + 256], ACT.Identity,
                                                bias=pcol(f"cv_b_pw{l}", c)), t, K.last["v"])
            ym = YM[:, 2 * j:2 * j + 2, :]
            t3 = V(lambda e: e.tensor_tensor(o, o, GS[:, 2 * j:2 * j + 2, :], ALU.mult), r, t_g5)
            t3 = V(lambda e: e.tensor_tensor(ym, ym, o, ALU.add), t3, t_ymg)
            mer.extend(split_act(ym, X1H[:, 2 * j:2 * j + 2, :], X1L[:, 2 * j:2 * j + 2, :], t3, K.last["t"]))
            return [r]
        mer = []
        gemm_fm(f"cvp{l}", 1024, act2, [0, 1], ev_c)
        t = gemm_tm(f"out2{l}", (X1H, X1L, mer), [4, 5, 6, 7])
        t = add_x([4, 5, 6, 7], t)
        if dbg:
            dbg(K, f"b{l}", X, [t])

        marks = K.fence()
        MEM = ar(4096, 2, 1024)
        XN = ar(2048, 2, 1024)
        for k in range(2):
            tm_ = K.dma("s", d4, MEM[:, k, :], A["mem_2"][0, 128 * k:128 * k + 128, :], marks)
        t = rms(MEM, XN, tm_)
        act2 = to_fm(XN, X2H, X2L, [4, 5, 6, 7], t, by_col(f"norm_mem{l}"))
        KT, VM, QT = ar(6408, 8, 256), ar(8456, 2, 1024), ar(10504, 8, 256)
        P4, PT = ar(12552, 4, 512), ar(14600, 4, 512)
        gemm_fm(f"xk{l}", 1024, act2, [0, 1], ev_y(KT, None))
        t = gemm_tm(f"xv{l}", act2, [4, 5, 6, 7])
        for k in range(2):
            for nb in range(2):
                b = 4 + 2 * k + nb
                pf[b] = ACTE(lambda e: e.activation(VM[:, k, 512 * nb:512 * nb + 512], PS[:, b, :], ACT.Copy), t)
        t_v = pf[7]
        t = rms(X, XN, act2[2])
        act = to_fm(XN, X1H, X1L, [2, 3], t, by_col(f"norm_x{l}"))
        gemm_fm(f"xq{l}", 1024, act, [0, 1], ev_y(QT, None))
        t_q = K.last["a"]
        mx, ng, den = [SMT[:, 8 * i:8 * i + 8] for i in range(3)]
        at_o = []
        for h in range(4):
            b = 4 + h

            def f(e):
                for k in range(2):
                    for c in (2 * h, 2 * h + 1):
                        m = e.matmul(PS[:, b, 256 * k:256 * k + 256], QT[:, c, 128 * k:128 * k + 128], KT[:, c, :],
                                     start=(c == 2 * h), stop=(c == 2 * h + 1))
                return m
            t = T(f, t_q, pf[b])
            t = V(lambda e: e.tensor_reduce(mx[:, 2 * h:2 * h + 2], PS[:, b, :].rearrange("p (k n) -> p k n", k=2), AX,
                                            ALU.max), t)
            t = V(lambda e: e.tensor_scalar(ng[:, 2 * h:2 * h + 2], mx[:, 2 * h:2 * h + 2], -0.0625, None, ALU.mult), t)
            for k in range(2):
                pf[b] = ACTE(lambda e: e.activation(P4[:, h, 256 * k:256 * k + 256], PS[:, b, 256 * k:256 * k + 256],
                                                    ACT.Exp, bias=ng[:, 2 * h + k:2 * h + k + 1], scale=0.0625,
                                                    accum_out=den[:, 2 * h + k:2 * h + k + 1]), t)
            t = V(lambda e: e.reciprocal(den[:, 2 * h:2 * h + 2], den[:, 2 * h:2 * h + 2]), pf[b])
            for k in range(2):
                pv = P4[:, h, 256 * k:256 * k + 256]
                t2 = V(lambda e: e.tensor_scalar(pv, pv, den[:, 2 * h + k:2 * h + k + 1], None, ALU.mult), t)
            at_o.append(t2)
        for h in range(4):
            b = 2 + h % 2
            t = transposes(b, [(PS[:, b, 256 * n_ + 128 * k:256 * n_ + 128 * k + 128],
                                P4[:, h, 256 * k + 128 * n_:256 * k + 128 * n_ + 128])
                               for n_ in range(2) for k in range(2)], at_o[h])
            pf[b] = ACTE(lambda e: e.activation(PT[:, h, :], PS[:, b, :], ACT.Copy), t)
            at_o[h] = pf[b]
        oo = []
        for h in range(4):
            b = 4 + h

            def f(e):
                for dc in range(2):
                    for n_ in range(2):
                        m = e.matmul(PS[:, b, 256 * dc:256 * dc + 256], VM[:, n_, 256 * h + 128 * dc:256 * h + 128 * dc + 128],
                                     PT[:, h, 256 * n_:256 * n_ + 256], start=(n_ == 0), stop=(n_ == 1))
                return m
            t = T(f, at_o[h], t_v, pf[b])
            pf[b] = split_act(PS[:, b, :].rearrange("p (c n) -> p c n", c=2), X2H[:, 2 * h:2 * h + 2, :],
                              X2L[:, 2 * h:2 * h + 2, :], t)
            oo += pf[b]
        t = gemm_tm(f"xo{l}", (X2H, X2L, oo), [4, 5, 6, 7])
        t = add_x([4, 5, 6, 7], t)
        if dbg:
            dbg(K, f"c{l}", X, [t])

        marks = K.fence()
        t = rms(X, XN, marks)
        act = to_fm(XN, X1H, X1L, [2, 3], t, by_col(f"norm_ffn{l}"))
        PD = ar(4096, 2, 4, 258)
        CV = ar(6160, 2, 4, 256)
        tz = G(lambda e: e.memset(PD[:, :, :, 0:2], 0.0), marks)
        cst_ = {"n": 0}

        def conv_evac(p, got):
            n_ = cst_["n"] % 2
            cst_["n"] += 1
            (bg, tg_), (bu, tu) = got
            for q, (b, t) in enumerate(((bg, tg_), (bu, tu))):
                for ci in range(2):
                    c = 22 * q + 2 * p + ci
                    r = ACTE(lambda e: e.activation(PD[:, n_, 2 * q + ci, 2:258], PS[:, b, 256 * ci:256 * ci + 256],
                                                    ACT.Identity, bias=pcol(f"ffn_b_up{l}", c)), t, tz,
                             cst_.get(("cv", n_)))
                pf[b] = r
                for ci in range(2):
                    c = 22 * q + 2 * p + ci
                    s_, dst = PD[:, n_, 2 * q + ci, :], CV[:, n_, 2 * q + ci, :]
                    t = V(lambda e: e.tensor_scalar(dst, s_[:, 0:256], pcol(f"ffn_dw_w{l}", c), pcol(f"ffn_dw_b{l}", c),
                                                    ALU.mult, ALU.add), r, cst_.get(("sp", n_)))
                    for k in (1, 2):
                        t = V(lambda e: e.scalar_tensor_tensor(dst, s_[:, k:k + 256], pcol(f"ffn_dw_w{l}", 44 * k + c),
                                                               dst, ALU.mult, ALU.add), t)
                if q == 0:
                    sg = ACTE(lambda e: e.activation(CV[:, n_, 0:2, :], CV[:, n_, 0:2, :], ACT.Silu), t)
            cst_[("cv", n_)] = t
            hv = CV[:, n_, 2:4, :]
            t = V(lambda e: e.tensor_tensor(hv, hv, CV[:, n_, 0:2, :], ALU.mult), t, sg)
            cst_[("sp", n_)] = t
            return hv.rearrange("p c n -> p (c n)"), t
        t = ffn(f"ff2{l}", 11, act, conv_evac, True, True)
        t = add_x([4, 5, 6, 7], t)

    ROWS = sb("ROWS", [4, 2, 256])

    layer1(0)
    if dbg and dbg.stop == 0:
        return finish(K, out, X)
    layer1(1)
    if dbg and dbg.stop == 1:
        return finish(K, out, X)
    t_small = load_small()
    layer2(0, t_small)
    layer2(1, t_small)
    marks = K.fence()
    FN = ar(4096, 1024)
    XN = ar(2048, 2, 1024)
    tf = K.dma("s", d4, FN, AP(A["final_norm_2"].tensor, A["final_norm_2"].offset, [[0, 128], [1, D]]), marks)
    t = rms(X, XN, marks)
    for k in range(2):
        t = V(lambda e: e.tensor_tensor(XN[:, k, :], XN[:, k, :], FN, ALU.mult), t, tf)
    finish(K, out, XN)


def finish(K, out, X):
    d = K.new("out")
    marks = K.fence()
    for k in range(2):
        t = K.dma("s", d, out[0, 128 * k:128 * k + 128, :], X[:, k, :], marks)
    K.wait("s", [t])


_INS = ["x", "c", "positions", "rel_bias", "w_ada", "b_ada", "w_in", "w_out", "conv_w", "conv_b", "dt_bias", "a_log",
        "d_skip", "ssd_norm_w", "sinks", "ln_g", "ln_b", "ffn_w_gate", "ffn_w_up", "ffn_w_down", "router_w",
        "router_b", "expert_w_gate", "expert_w_up", "expert_w_down", "mem_2", "norm_mix_2", "w_in_2", "b_in_2",
        "ml_conv_w_2", "ml_conv_b_2", "ml_wq_2", "ml_wk_2", "ml_wv_2", "ml_w_gate_2", "ml_b_gate_2", "ml_norm_g_2",
        "ml_skip_2", "ml_w_down_2", "cv_dw_w_2", "cv_dw_b_2", "cv_ln_g_2", "cv_ln_b_2", "cv_w_pw_2", "cv_b_pw_2",
        "w_out_2", "norm_x_2", "norm_mem_2", "xa_wq_2", "xa_wk_2", "xa_wv_2", "xa_wo_2", "norm_ffn_2", "ffn_w_up_2",
        "ffn_b_up_2", "ffn_dw_w_2", "ffn_dw_b_2", "ffn_w_down_2", "final_norm_2"]


def kernel(**inputs):
    import concourse.bacc as _bacc
    from concourse.bass_utils import run_bass_kernel_spmd as _run

    nc = _bacc.Bacc("TRN2", target_bir_lowering=False, num_devices=1)
    arrays, A = {}, {}
    for name in _INS:
        a = np.ascontiguousarray(inputs[name])
        arrays[f"in_{name}_dram"] = a
        A[name] = nc.dram_tensor(f"in_{name}_dram", a.shape, mybir.dt.from_np(a.dtype), kind="ExternalInput").ap()
    a = constants()
    arrays["in_cst_dram"] = a
    A["cst"] = nc.dram_tensor("in_cst_dram", a.shape, mybir.dt.float32, kind="ExternalInput").ap()
    out = nc.dram_tensor("out_0_dram", (1, S, D), mybir.dt.float32, kind="ExternalOutput").ap()
    build_program(nc, A, out)
    r = _run(nc, [arrays], core_ids=[0])
    return r.results[0]["out_0_dram"]
```

```python
import math

import numpy as np
import concourse.bass as bass
from concourse import mybir
from contextlib import ExitStack

F32 = mybir.dt.float32
F32R = mybir.dt.float32r
I32 = mybir.dt.int32
ACT = mybir.ActivationFunctionType
ALU = mybir.AluOpType
AX = mybir.AxisListType.X
AP = bass.AP

D = 1024
S = 256
D_FF = 2816
NEXP = 8
D_EXP = 3584
ALPHA = 4.0 ** 0.25
LN_EPS = 1e-5
RMS_EPS = 1e-6
NEG = -1.0e30
NRAW = 4
NH = 3
USZ = 2048
ARENA = 16680

C_ID, C_ONE, C_TRI, C_NEG, C_SW = 0, 128, 256, 384, 640
C_DEC, C_INV, C_BD, C_LOW, C_IOT, C_HOT = 768, 1792, 1824, 1856, 1920, 2048
C_N = 2048 + 384


def constants():
    c = np.zeros((128, C_N), np.float64)
    p = np.arange(128)
    c[:, C_ID:C_ID + 128] = np.eye(128)
    c[:, C_ONE:C_ONE + 128] = 1.0
    c[:, C_TRI:C_TRI + 128] = p[None, :] >= p[:, None]
    c[:, C_NEG:C_NEG + 128] = np.where(p[None, :] >= p[:, None], 0.0, NEG)
    c[:, C_SW:C_SW + 128] = np.roll(np.eye(128), 64, axis=1)
    l = np.arange(256)
    diff = l[None, :] - p[:, None]
    for h in range(4):
        lg = np.log1p(-2.0 ** (-5.0 - h))
        c[:, C_DEC + 256 * h:C_DEC + 256 * h + 256] = np.where(diff >= 0, np.exp(lg * np.maximum(diff, 0)), 0.0) * 0.125
    half = 32
    c[:, C_INV:C_INV + 32] = np.exp(np.float32(-math.log(10000.0)) * np.arange(half, dtype=np.float32) / np.float32(half))
    c[:, C_BD:C_BD + 32] = np.arange(32)[None, :] == (p[:, None] // 4)
    e = np.arange(8)
    c[:, C_LOW:C_LOW + 64] = (e[None, :] < e[:, None]).reshape(-1)
    c[:, C_IOT:C_IOT + 128] = p[None, :]
    dist = 255 - np.arange(384)
    ok = (dist >= 0) & (dist < 128)
    dc = np.clip(dist, 1, 127).astype(np.float32)
    large = 16 + (np.log(dc / np.float32(16)) / np.float32(math.log(8.0)) * np.float32(16)).astype(np.int32)
    bucket = np.where(dist < 16, np.maximum(dist, 0), np.minimum(large, 31))
    for b in range(32):
        c[b, C_HOT:C_HOT + 384] = ok & (bucket == b)
    c[32, C_HOT:C_HOT + 384] = np.where(ok, 0.0, NEG)
    return c.astype(np.float32)


def param_rows(A):
    rows = [("c", 8, A["c"].rearrange("a (r q) -> (a r) q", q=128))]
    for l in range(2):
        rows.append((f"b_ada{l}", 48, A["b_ada"][l].rearrange("(r q) -> r q", q=128)))
        rows.append((f"conv_w{l}", 24, A["conv_w"][l].rearrange("k (r q) -> (k r) q", q=128)))
        rows.append((f"conv_b{l}", 6, A["conv_b"][l].rearrange("(r q) -> r q", q=128)))
        rows.append((f"ssd_norm{l}", 4, A["ssd_norm_w"][l].rearrange("(r q) -> r q", q=128)))
    for l in range(2):
        for nm, r in (("norm_mix", 8), ("b_in", 48), ("ml_conv_b", 8), ("ml_norm_g", 8), ("ml_skip", 8),
                      ("cv_dw_b", 8), ("cv_ln_g", 8), ("cv_ln_b", 8), ("cv_b_pw", 8), ("norm_x", 8),
                      ("norm_mem", 8), ("norm_ffn", 8), ("ffn_b_up", 44), ("ffn_dw_b", 44)):
            rows.append((f"{nm}{l}", r, A[nm + "_2"][l].rearrange("(r q) -> r q", q=128)))
        for nm, r in (("ml_conv_w", 32), ("cv_dw_w", 248), ("ffn_dw_w", 132)):
            rows.append((f"{nm}{l}", r, A[nm + "_2"][l].rearrange("k (r q) -> (k r) q", q=128)))
    return rows



def u_fm(w, n0, n1, key):
    return [(key, w[:, n:min(n + 256, n1)].rearrange("(c p) n -> p c n", p=128), True) for n in range(n0, n1, 256)]


def u_tm(w, k0, k1, key):
    return [(key, w[128 * k:128 * (k + 2), :].rearrange("(c p) n -> p c n", p=128), True) for k in range(k0, k1, 2)]


def u_blk(w, n0, n1, key, kc=4):
    return [(key, w[128 * k:128 * (k + kc), n0:n1].rearrange("(c p) n -> p c n", p=128), True) for k in range(0, 8, kc)]


def u_ffn(wg, wu, wd, n_pairs, up0, key):
    out = []
    for p in range(n_pairs + 1):
        if p < n_pairs:
            out += u_fm(wg, 256 * p, 256 * p + 256, key + "g")
            out += u_fm(wu, up0 + 256 * p, up0 + 256 * p + 256, key + "u")
        if p > 0:
            out += u_tm(wd, 2 * p - 2, 2 * p, key + "d")
    return out


def u_ada(w, b):
    return [("ada", w[128 * k:128 * k + 128, 2048 * b:2048 * b + 2048].rearrange("p (c n) -> p c n", c=1), False)
            for k in range(8)]


def u_moe(wg, wu, wd):
    out = []
    for b in range(8):
        if b < 7:
            out += u_blk(wg, 512 * b, 512 * b + 512, "mg") + u_blk(wu, 512 * b, 512 * b + 512, "mu")
        if b > 0:
            out += u_tm(wd, 4 * b - 4, 4 * b, "md")
    return out


def weave(main, side):
    out, side = [], list(side)
    for u in main:
        out.append(u)
        if side:
            out.append(side.pop(0))
    return out + side


def stream_plan(A):
    out = u_ada(A["w_ada"][0], 0)
    for l in range(2):
        w = A["w_in"][l]
        ins = []
        for n in (0, 512, 1024):
            ins += u_blk(w, n, n + 512, f"in{l}")
        ins += u_fm(w, 1536, 2304, f"in{l}") + u_fm(w, 2312, 2568, f"in{l}") + u_fm(w, 2568, 2696, f"in{l}")
        ins += u_blk(w, 2696, 2824, f"in{l}", 8) + u_blk(w, 2304, 2312, f"in{l}", 8)
        out += weave(ins, u_ada(A["w_ada"][0], 1) + u_ada(A["w_ada"][0], 2)) if l == 0 else ins
        out += u_tm(A["w_out"][l], 0, 8, f"out{l}")
        if l == 0:
            out += weave(u_ffn(A["ffn_w_gate"][0], A["ffn_w_up"][0], A["ffn_w_down"][0], 11, 0, "ffn"),
                         u_ada(A["w_ada"][1], 0) + u_ada(A["w_ada"][1], 1) + u_ada(A["w_ada"][1], 2))
        else:
            for e in range(NEXP):
                out += u_moe(A["expert_w_gate"][0, e], A["expert_w_up"][0, e], A["expert_w_down"][0, e])
    for l in range(2):
        w = A["w_in_2"][l]
        for n in (0, 2048, 3072, 1024):
            out += u_fm(w, n, n + 1024, f"in2{l}")
        out += u_fm(A["ml_w_down_2"][l], 0, 1024, f"mld{l}")
        for n in (4096, 5120):
            out += u_fm(w, n, n + 1024, f"in2{l}")
        out += u_fm(A["cv_w_pw_2"][l], 0, 1024, f"cvp{l}")
        out += u_tm(A["w_out_2"][l], 0, 8, f"out2{l}")
        out += u_fm(A["xa_wk_2"][l], 0, 1024, f"xk{l}")
        out += u_tm(A["xa_wv_2"][l], 0, 8, f"xv{l}")
        out += u_fm(A["xa_wq_2"][l], 0, 1024, f"xq{l}")
        out += u_tm(A["xa_wo_2"][l], 0, 8, f"xo{l}")
        out += u_ffn(A["ffn_w_up_2"][l], A["ffn_w_up_2"][l], A["ffn_w_down_2"][l], 11, D_FF, f"ff2{l}")
    return out


class Core:

    def __init__(self, nc, ctx, tag="", only=None, sems=None):
        self.nc, self.ctx, self.only, self.tag = nc, ctx, only, tag
        self.engines = {"v": nc.vector, "a": nc.scalar, "g": nc.gpsimd, "t": nc.tensor, "s": nc.sync}
        self.sems = {e: self.sem("s_" + tag + e) for e in "vagt"} if sems is None else sems
        self.count = {}
        self.seen = {e: {} for e in self.engines}
        self.last = {}

    def sem(self, name):
        return self.ctx.enter_context(self.nc.semaphore(name))

    def new(self, name):
        if name not in self.sems:
            self.sems[name] = self.sem("d_" + name)
        return name

    def wait(self, eng, deps):
        for d in deps:
            if d is None:
                continue
            if isinstance(d, list):
                self.wait(eng, d)
                continue
            k, n = d
            if self.seen[eng].get(k, 0) < n:
                if self.only in (None, eng):
                    self.engines[eng].wait_ge(self.sems[k], n)
                self.seen[eng][k] = n

    def op(self, eng, f, deps):
        self.wait(eng, deps)
        self.count[eng] = self.count.get(eng, 0) + 1
        if self.only in (None, eng):
            f(self.engines[eng]).then_inc(self.sems[eng], 1)
        self.last[eng] = (eng, self.count[eng])
        return self.last[eng]

    def V(self, f, *deps):
        return self.op("v", f, deps)

    def A(self, f, *deps):
        return self.op("a", f, deps)

    def G(self, f, *deps):
        return self.op("g", f, deps)

    def T(self, f, *deps):
        return self.op("t", f, deps)

    def dma(self, eng, sem, out, in_, *deps):
        self.wait(eng, deps)
        if self.only in (None, eng):
            self.engines[eng].dma_start(out, in_).then_inc(self.sems[sem], 16)
        self.count[sem] = self.count.get(sem, 0) + 16
        return (sem, self.count[sem])

    def fence(self):
        marks = [self.last[e] for e in self.last]
        for e in "vagt":
            self.wait(e, marks)
        return marks


def view(ap, *dims):
    return AP(ap.tensor, ap.offset, [list(ap.ap[0])] + [list(d) for d in dims])


def build_program(nc, A, out):
    with ExitStack() as ctx:
        emit_program(nc, ctx, A, out)


def emit_program(nc, ctx, A, out):
    K = Core(nc, ctx)
    V, ACTE, G, T = K.V, K.A, K.G, K.T

    def sb(name, shape, dt=F32):
        return ctx.enter_context(nc.sbuf_tensor(name, shape, dt))

    RAW = sb("RAW", [128, NRAW, USZ])
    HI = sb("HI", [128, NH, USZ], F32R)
    LO = sb("LO", [128, NH, USZ], F32R)
    X1H, X1L = sb("X1H", [128, 8, 256], F32R), sb("X1L", [128, 8, 256], F32R)
    X2H, X2L = sb("X2H", [128, 8, 256], F32R), sb("X2L", [128, 8, 256], F32R)
    X = sb("X", [128, 2, D])
    CST = sb("CST", [128, C_HOT])
    PC = sb("PC", [128, 12 * 128])
    AR = sb("AR", [128, ARENA])
    MOD = sb("MOD", [128, 2, 48])
    BT = sb("BT", [128, 4, 256])
    SM = sb("SM", [128, 640])
    PS = ctx.enter_context(nc.psum_tensor("PS", [128, 8, 512], F32))

    ident = CST[:, C_ID:C_ID + 128]
    ones = CST[:, C_ONE:C_ONE + 128]
    tri = CST[:, C_TRI:C_TRI + 128]
    negm = CST[:, C_NEG:C_NEG + 256]
    swap = CST[:, C_SW:C_SW + 128]

    def ar(off, *shape):
        n = int(np.prod(shape))
        assert off + n <= ARENA, (off, shape)
        a = AR[:, off:off + n]
        if len(shape) == 2:
            a = a.rearrange("p (a b) -> p a b", a=shape[0])
        if len(shape) == 3:
            a = a.rearrange("p (a b c) -> p a b c", a=shape[0], b=shape[1])
        return a

    sm_at = [0]

    def sm(*shape):
        n = int(np.prod(shape))
        o = sm_at[0]
        sm_at[0] += n
        assert sm_at[0] <= 640
        a = SM[:, o:o + n]
        if len(shape) == 2:
            a = a.rearrange("p (a b) -> p a b", a=shape[0])
        if len(shape) == 3:
            a = a.rearrange("p (a b c) -> p a b c", a=shape[0], b=shape[1])
        return a

    plan = stream_plan(A)
    raw_sem = [K.new(f"raw{i}") for i in range(NRAW)]
    raw_free = {}
    hl_free = [None] * NH
    landed, split_of = {}, {}
    st = {"dma": 0, "split": 0, "next": 0, "open": 0, "aux": 7}
    hslot = {}
    n_split = [0]

    def uview(tile, slot, a):
        return tile[:, slot, 0:a.shape[1] * a.shape[2]].rearrange("p (c n) -> p c n", c=a.shape[1])

    def issue_dma():
        while st["dma"] < len(plan):
            i = st["dma"]
            if i >= NRAW and i - NRAW not in raw_free:
                return
            s = i % NRAW
            landed[i] = K.dma("s", raw_sem[s], uview(RAW, s, plan[i][1]), plan[i][1], raw_free.get(i - NRAW))
            st["dma"] += 1

    def pump():
        while st["split"] < st["dma"]:
            i = st["split"]
            if not plan[i][2]:
                st["split"] += 1
                continue
            if st["open"] == NH:
                return
            st["split"] += 1
            st["open"] += 1
            s, h = i % NRAW, n_split[0] % NH
            n_split[0] += 1
            n = plan[i][1].shape[1] * plan[i][1].shape[2]
            hslot[i] = h
            r, hi, lo = RAW[:, s, 0:n], HI[:, h, 0:n], LO[:, h, 0:n]
            t1 = ACTE(lambda e: e.activation(hi, r, ACT.Copy), landed[i], hl_free[h])
            on = V if n_split[0] % 2 else G
            t2 = on(lambda e: e.tensor_tensor(lo, r, hi.bitcast(F32), ALU.subtract), landed[i], t1, hl_free[h])
            split_of[i] = [t1, t2]
            raw_free[i] = [t1, t2]
            issue_dma()

    def take(key):
        i = st["next"]
        assert plan[i][0] == key, (plan[i][0], key)
        st["next"] += 1
        if plan[i][2]:
            a = plan[i][1]
            return i, uview(HI, hslot[i], a), uview(LO, hslot[i], a), split_of[i]
        return i, uview(RAW, i % NRAW, plan[i][1]), None, landed[i]

    def done(i, tok):
        hl_free[hslot[i]] = tok
        st["open"] -= 1
        pump()
        if side:
            side.pop(0)()

    side = []

    def ada_unit(acc, k):
        i, raw, _, got = take("ada")
        w = raw.rearrange("p c n -> p (c n)")
        if k == 0:
            t = V(lambda e: e.tensor_scalar(acc, w, pcol("c", 0), None, ALU.mult), got, t_pc, st.get("acc"))
        else:
            t = V(lambda e: e.scalar_tensor_tensor(acc, w, pcol("c", k), acc, ALU.mult, ALU.add), got, K.last["v"])
        raw_free[i] = t
        issue_dma()
        pump()

    def ada_block(l, b, acc):
        def step(k):
            ada_unit(acc, k)
            if k == 7:
                ada_sum(l, b, acc)
        return [lambda k=k: step(k) for k in range(8)]

    def ada_sum(l, b, acc):
        t0 = K.last["v"]
        for q in range(4):
            bk = st["aux"]
            t = transposes(bk, [(PS[:, bk, 128 * j:128 * j + 128], acc[:, 512 * q + 128 * j:512 * q + 128 * j + 128])
                                for j in range(4)], t0)
            o = MOD[:, l, 16 * b + 4 * q:16 * b + 4 * q + 4]
            pf[bk] = V(lambda e: e.tensor_reduce(o, PS[:, bk, :].rearrange("p (a n) -> p a n", a=4), AX, ALU.add), t)
        o = MOD[:, l, 16 * b:16 * b + 16]
        t = V(lambda e: e.tensor_tensor(o, o, pcols(f"b_ada{l}", 16, 16 * b), ALU.add), pf[bk])
        for q in (8, 16, 32, 40):
            if 16 * b <= q < 16 * b + 16:
                t = V(lambda e: e.tensor_scalar(MOD[:, l, q:q + 8], MOD[:, l, q:q + 8], 1.0, None, ALU.add), t)
        st["mod"] = t

    pf = [None] * 8

    def mm3(e, o, lh, ll, rh, rl, first, last, skip=False):
        e.matmul(o, lh, rh, start=first, stop=False, skip_group_check=skip)
        e.matmul(o, lh, rl, start=False, stop=False, skip_group_check=skip)
        return e.matmul(o, ll, rh, start=False, stop=last, skip_group_check=skip)

    def gemm_fm(key, ncols, act, banks, evac):
        XH, XL, ready = act
        for j, n0 in enumerate(range(0, ncols, 256)):
            w = min(256, ncols - n0)
            b = banks[j % len(banks)]
            i, hi, lo, got = take(key)

            def f(e):
                for nb in range(w // 128):
                    o = PS[:, b, 256 * nb:256 * nb + 256]
                    for kc in range(8):
                        c = slice(128 * nb, 128 * nb + 128)
                        m = mm3(e, o, hi[:, kc, c], lo[:, kc, c], XH[:, kc, :], XL[:, kc, :], kc == 0, kc == 7)
                return m
            t = T(f, got, ready, pf[b])
            pf[b] = evac(j, PS[:, b, 0:w * 2], t)
            done(i, t)

    def mm_down(e, hi, lo, LH, LL, banks, kcs, first, last):
        for c in range(kcs):
            for t in range(2):
                for nb in range(2):
                    o = PS[:, banks[2 * t + nb], :]
                    ts, ns = slice(128 * t, 128 * t + 128), slice(512 * nb, 512 * nb + 512)
                    m = mm3(e, o, LH(c)[:, ts], LL(c)[:, ts], hi[:, c, ns], lo[:, c, ns],
                            first and c == 0, last and c == kcs - 1)
        return m

    def gemm_tm(key, act, banks):
        XH, XL, ready = act
        for j in range(4):
            i, hi, lo, got = take(key)
            t = T(lambda e: mm3_tm(e, hi, lo, XH, XL, 2 * j, banks), got, ready, [pf[b] for b in banks])
            done(i, t)
        return t

    def mm3_tm(e, hi, lo, XH, XL, k0, banks):
        return mm_down(e, hi, lo, lambda c: XH[:, k0 + c, :], lambda c: XL[:, k0 + c, :], banks, 2, k0 == 0, k0 == 6)

    def gemm_blk(key, act, banks, width, kc):
        XH, XL, ready = act
        for k0 in range(0, 8, kc):
            i, hi, lo, got = take(key)

            def f(e):
                for c in range(kc):
                    for t in range(2):
                        ts = slice(128 * t, 128 * t + 128)
                        m = mm3(e, PS[:, banks[t], 0:width], XH[:, k0 + c, ts], XL[:, k0 + c, ts], hi[:, c, :],
                                lo[:, c, :], k0 + c == 0, k0 + c == 7)
                return m
            t = T(f, got, ready, [pf[b] for b in banks])
            done(i, t)
        return t

    def split_act(src, H, L, *deps):
        t1 = ACTE(lambda e: e.activation(H, src, ACT.Copy), *deps)
        t2 = V(lambda e: e.tensor_tensor(L, src, H.bitcast(F32), ALU.subtract), t1, *deps)
        return [t1, t2]

    def transposes(dst_bank, parts, *deps):
        def f(e):
            for d, s_ in parts:
                n = s_.shape[0]
                m = e.transpose(d, s_, ident[0:n, 0:n])
            return m
        return T(f, pf[dst_bank], *deps)

    def to_fm(src, H, L, banks, deps, evac=None, prev=None):
        ready = []
        for cp in range(4):
            b = banks[cp % len(banks)]
            t = transposes(b, [(PS[:, b, 256 * ci + 128 * tt:256 * ci + 128 * tt + 128],
                                src[:, tt, 128 * (2 * cp + ci):128 * (2 * cp + ci) + 128])
                               for ci in range(2) for tt in range(2)], deps)
            p = PS[:, b, :].rearrange("p (c n) -> p c n", c=2)
            hs = (H[:, 2 * cp:2 * cp + 2, :], L[:, 2 * cp:2 * cp + 2, :])
            if evac is None:
                r = split_act(p, hs[0], hs[1], t, prev)
                pf[b] = r
            else:
                te = [evac(2 * cp + ci, p[:, ci, :], t, XF[:, 2 * cp + ci, :]) for ci in range(2)]
                pf[b] = te
                r = split_act(XF[:, 2 * cp:2 * cp + 2, :], hs[0], hs[1], te, prev)
            ready += r
        return (H, L, ready)

    XF = ar(0, 8, 256)

    def pcol(name, i=0):
        o = pc_at[name] + i
        return PC[:, o:o + 1]

    def pcols(name, n, i=0):
        o = pc_at[name] + i
        return PC[:, o:o + n]

    def rsqrt(dst, src, eps, *deps):
        t = V(lambda e: e.tensor_scalar(dst, src, eps, None, ALU.add), *deps)
        t = ACTE(lambda e: e.activation(dst, dst, ACT.Ln), t)
        return ACTE(lambda e: e.activation(dst, dst, ACT.Exp, scale=-0.5), t)

    def rstd_of(mv, rs, *deps):
        return rsqrt(rs, mv, LN_EPS, *deps)

    def bn(src, stats, mv, *deps):
        n = src.shape[1]
        k = max(1, n // 512)
        t = None
        for i in range(k):
            t = V(lambda e: e.bn_stats(stats[:, 6 * i:6 * i + 6], src[:, i * (n // k):(i + 1) * (n // k)]), *deps)
        return V(lambda e: e.bn_aggr(mv, stats[:, 0:6 * k]), t)

    STT = sm(2, 12)
    MV = sm(2, 2)
    RS = sm(2)
    dtb, alog, dsk = sm(2, 8), sm(2, 8), sm(2, 8)
    snk, rbias, mbg = sm(2, 4), sm(8), sm(2, 8)
    pos_i = SM[:, sm_at[0]:sm_at[0] + 2].bitcast(I32)
    sm(2)
    posf = sm(2)
    COS, SIN = sm(2, 32), sm(2, 32)
    relb = sm(4)

    d0 = K.new("cst")
    d1 = K.new("par")
    d2 = K.new("xin")
    d3 = K.new("bt")
    d4 = K.new("ln")
    d5 = K.new("misc")
    rows = param_rows(A)
    PR = ar(0, 12, 128)
    HOT = ar(6144, 384)
    pc_at = {}
    at = 0
    n = 0
    for name, r, src in rows:
        pc_at[name] = at
        o = 0
        while o < r:
            k = min(r - o, 128 - (at + o) % 128)
            K.dma("a" if n % 2 else "s", d1, PR[(at + o) % 128:(at + o) % 128 + k, (at + o) // 128, :], src[o:o + k, :])
            o += k
            n += 1
        at += r
        if name == "c":
            K.dma("s", d0, CST[:, :], A["cst"][:, 0:C_HOT])
            K.dma("s", d0, HOT, A["cst"][:, C_HOT:C_N])
            issue_dma()
    n_pr = -(-at // 128)
    assert n_pr <= 12
    last_rows = at - 128 * (n_pr - 1)
    for k in range(2):
        K.dma("a", d2, X[:, k, :], A["x"][0, 128 * k:128 * k + 128, :])
        K.dma("s", d2, pos_i[:, k:k + 1], A["positions"][0, 128 * k:128 * k + 128].rearrange("(p a) -> p a", a=1))
    for dst, src, cnt in ((dtb, A["dt_bias"], 16), (alog, A["a_log"], 16), (dsk, A["d_skip"], 16), (snk, A["sinks"], 8),
                          (rbias, A["router_b"], 8), (mbg, A["ml_b_gate_2"], 16)):
        flat = view(dst, [1, cnt])
        K.dma("s", d2, flat, AP(src.tensor, src.offset, [[0, 128], [1, cnt]]))
    V(lambda e: e.memset(relb[0:64, :], 1.0))
    K.dma("a", d2, relb[0:32, :], A["rel_bias"], K.last["v"])
    WR = sb("WR", [128, 8, 8])
    K.dma("a", d5, WR[:, :, :], A["router_w"][0].rearrange("(c p) n -> p c n", p=128))
    cst, par, xin, misc = (d0, 32), (d1, K.count[d1]), (d2, K.count[d2]), (d5, K.count[d5])
    for e in "vagt":
        K.wait(e, [cst, par, xin, misc])

    for i in range(n_pr):
        b = i % 4
        r = 128 if i < n_pr - 1 else last_rows
        t = transposes(b, [(PS[:, b, 0:r], PR[0:r, i, :])])
        pf[b] = V(lambda e: e.tensor_copy(PC[:, 128 * i:128 * i + r], PS[:, b, 0:r]), t)
    t_pc = pf[b]

    ang = ar(2048, 2, 32)
    kk = ar(2112, 2, 32)
    t = V(lambda e: e.tensor_copy(posf, pos_i))
    for k in range(2):
        t2 = V(lambda e: e.tensor_scalar(ang[:, k, :], CST[:, C_INV:C_INV + 32], posf[:, k:k + 1], None, ALU.mult), t)
    MAGIC = 12582912.0
    t = V(lambda e: e.tensor_scalar(kk, ang, 1.0 / (2 * math.pi), MAGIC, ALU.mult, ALU.add), t2)
    t = V(lambda e: e.tensor_scalar(kk, kk, MAGIC, None, ALU.subtract), t)
    c1 = 6.28125
    c2 = float((np.array([2 * math.pi - c1], np.float32).view(np.uint32) & np.uint32(0xFFFFF000)).view(np.float32)[0])
    c3 = 2 * math.pi - c1 - c2
    for cc in (c1, c2, c3):
        t = V(lambda e: e.scalar_tensor_tensor(ang, kk, -cc, ang, ALU.mult, ALU.add), t)
    t = V(lambda e: e.tensor_scalar(ang, ang, math.pi, -math.pi, ALU.min, ALU.max), t)
    t1 = ACTE(lambda e: e.activation(SIN, ang, ACT.Sin), t)
    t2 = ACTE(lambda e: e.activation(COS, ang, ACT.Sin, scale=0.5), t)
    t = V(lambda e: e.tensor_tensor(COS, COS, COS, ALU.mult), t2)
    t_rot = [t1, V(lambda e: e.tensor_scalar(COS, COS, -2.0, 1.0, ALU.mult, ALU.add), t)]

    RB = ar(4096, 4, 384)
    scr = nc.dram_tensor("scr_bias", [4, 128, 384], F32)
    for h in range(4):
        b = 4 + h
        lhs = view(relb[0:33, h:h + 1], [0, 128])
        t = T(lambda e: e.matmul(PS[:, b, 0:384], lhs, HOT[0:33, :], start=True, stop=True), pf[b])
        t = ACTE(lambda e: e.activation(RB[:, h, :], PS[:, b, 0:384], ACT.Copy), t)
        pf[b] = t
    tb = K.dma("a", d3, scr[:].rearrange("h p n -> p h n"), RB, t)
    scr0 = scr[0, 0:1, 0:1]
    for h in range(4):
        tb2 = K.dma("a", d3, BT[:, h, :], AP(scr0.tensor, h * 128 * 384 + 127, [[383, 128], [1, 256]]), tb)
    t_bt = tb2

    for f_ in ada_block(0, 0, ar(8192, 2048)):
        f_()
    marks = K.fence()

    def modc(l, part, c):
        return MOD[:, l, 8 * part + c:8 * part + c + 1]

    def scaled(scale, bias):
        def evac(c, p, t, dst):
            return V(lambda e: e.tensor_scalar(dst, p, scale(c), bias(c) if bias else None, ALU.mult,
                                               ALU.add if bias else ALU.bypass), t)
        return evac

    LNR = ar(2048, 2, 1024)
    GB = ar(4096, 1024)
    DG = ar(5120, 8, 128)

    def rows_of(l, part, dst, banks=(0, 1)):
        for c in range(8):
            t = V(lambda e: e.tensor_scalar(DG[:, c, :], ident, modc(l, part, c), None, ALU.mult), K.last["t"])
        for h in range(2):
            b = banks[h]
            t2 = T(lambda e: [e.matmul(PS[:, b, 128 * c:128 * c + 128], ones, DG[:, 4 * h + c, :], start=True, stop=True)
                              for c in range(4)][-1], t, pf[b])
            pf[b] = ACTE(lambda e: e.activation(dst[:, 512 * h:512 * h + 512], PS[:, b, :], ACT.Copy), t2)
        return [pf[banks[0]], pf[banks[1]]]

    def residual(l, j, banks, tok, src=None):
        part = 2 if j == 0 else 5
        tl = K.dma("s", d4, LNR[:, 0, :], AP(A["ln_g"].tensor, A["ln_g"].offset + (2 * l + j) * D, [[0, 128], [1, D]]),
                   K.last["t"], K.last["v"], K.last["a"], K.last["g"])
        tl = K.dma("s", d4, LNR[:, 1, :], AP(A["ln_b"].tensor, A["ln_b"].offset + (2 * l + j) * D, [[0, 128], [1, D]]))
        tg = rows_of(l, part, GB)
        TT = ar(0, 2, 1024)
        for k in range(2):
            for nb in range(2):
                ns = slice(512 * nb, 512 * nb + 512)
                y = src[:, k, ns] if src is not None else PS[:, banks[2 * k + nb], :]
                t = V(lambda e: e.tensor_tensor(TT[:, k, ns], y, GB[:, ns], ALU.mult), tok, tg)
                if src is None:
                    pf[banks[2 * k + nb]] = t
            t = V(lambda e: e.scalar_tensor_tensor(X[:, k, :], X[:, k, :], ALPHA, TT[:, k, :], ALU.mult, ALU.add),
                  K.last["v"], K.last["t"])
            t = bn(X[:, k, :], STT[:, k, :], MV[:, k, :], t)
        t = rstd_of(MV[:, :, 1], RS, t)
        for k in range(2):
            t1 = V(lambda e: e.tensor_scalar(X[:, k, :], X[:, k, :], MV[:, k, 0:1], RS[:, k:k + 1], ALU.subtract,
                                             ALU.mult), t)
            t1 = V(lambda e: e.tensor_tensor(X[:, k, :], X[:, k, :], LNR[:, 0, :], ALU.mult), t1, tl)
            t1 = V(lambda e: e.tensor_tensor(X[:, k, :], X[:, k, :], LNR[:, 1, :], ALU.add), t1)
        return t1

    def ffn(key, n_pairs, act, evac_h, first, last):
        ring = {}
        prev = [None]
        RH = X2H[:, :, :].rearrange("p a b -> p (a b)").rearrange("p (s c n) -> p s c n", s=4, c=2)
        RL = X2L[:, :, :].rearrange("p a b -> p (a b)").rearrange("p (s c n) -> p s c n", s=4, c=2)
        XH, XL, ready = act
        for p in range(n_pairs + 1):
            st["aux"] = 2 * ((p + 1) % 2)
            if p < n_pairs:
                s_ = p % 3
                got2 = []
                for half, kk_ in ((0, "g"), (1, "u")):
                    b = (p % 2) * 2 + half
                    i, hi, lo, got = take(key + kk_)

                    def f(e):
                        for nb in range(2):
                            for kc in range(8):
                                c = slice(128 * nb, 128 * nb + 128)
                                m = mm3(e, PS[:, b, 256 * nb:256 * nb + 256], hi[:, kc, c], lo[:, kc, c],
                                        XH[:, kc, :], XL[:, kc, :], kc == 0, kc == 7)
                        return m
                    t = T(f, got, ready, pf[b])
                    got2.append((b, t))
                    done(i, t)
                hf, tf = evac_h(p, got2)
                ring[p] = split_act(hf, RH[:, s_].rearrange("p c n -> p (c n)"), RL[:, s_].rearrange("p c n -> p (c n)"),
                                    tf, ring.get(("down", p - 3)))
            if p > 0:
                q = p - 1
                i, hi, lo, got = take(key + "d")
                RHs, RLs = RH[:, q % 3], RL[:, q % 3]
                t = T(lambda e: mm_down(e, hi, lo, lambda c: RHs[:, c, :], lambda c: RLs[:, c, :], [4, 5, 6, 7], 2,
                                        first and q == 0, last and q == n_pairs - 1),
                      got, ring[q], [pf[b] for b in (4, 5, 6, 7)] if first and q == 0 else None)
                ring[("down", q)] = t
                done(i, t)
        return t

    SG = ar(6144, 2, 512)
    HF = ar(7168, 2, 512)
    hst = {"n": 0}

    def swiglu_evac():
        def evac(p, got):
            n_ = hst["n"] % 2
            hst["n"] += 1
            (bg, tg_), (bu, tu) = got
            t = ACTE(lambda e: e.activation(SG[:, n_, :], PS[:, bg, :], ACT.Silu), tg_, hst.get(("hf", n_)))
            pf[bg] = t
            t = V(lambda e: e.tensor_tensor(HF[:, n_, :], SG[:, n_, :], PS[:, bu, :], ALU.mult), t, tu,
                  hst.get(("sp", n_)))
            pf[bu] = t
            hst[("hf", n_)] = t
            hst[("sp", n_)] = t
            return HF[:, n_, :], t
        return evac

    def layer1(l):
        marks = K.fence()
        act = to_fm(X, X1H, X1L, [4, 5], marks, scaled(lambda c: modc(l, 1, c), lambda c: modc(l, 0, c)))
        R = ar(6144, 2, 1024)
        SZ = ar(8192, 2, 512)
        XP = ar(9216, 6, 259)
        XC = ar(10770, 6, 256)
        QK = ar(12306, 4, 256)
        AVD = ar(13330, 2, 136)
        XS = ar(13602, 2, 512)
        XD = ar(14626, 2, 512)
        QT = ar(15650, 4, 256)
        E8 = ar(0, 8, 384)
        RT = ar(3072, 4, 384)
        LG = ar(4608, 4, 384)
        PT = ar(9216, 4, 384)
        f0 = K.fence()
        if l == 0:
            side.extend(ada_block(0, 1, ar(2048, 2048)) + ada_block(0, 2, ar(4096, 2048)))
        for blk in range(3):
            bb = [[0, 1], [2, 3], [0, 1]][blk]
            t = gemm_blk(f"in{l}", act, bb, 512, 4)
            for k in range(2):
                dst = R[:, k, 512 * blk:512 * blk + 512] if blk < 2 else SZ[:, k, :]
                fn = ACT.Copy if blk < 2 else ACT.Silu
                pf[bb[k]] = ACTE(lambda e: e.activation(dst, PS[:, bb[k], :], fn), t, f0)
        t_r = K.last["a"]
        t_sz = t_r
        tz = G(lambda e: e.memset(XP[:, :, 0:3], 0.0), f0)

        txp = []

        def ev_x(j, p, t):
            r = ACTE(lambda e: e.activation(XP[:, 2 * j:2 * j + 2, 3:259], p.rearrange("p (c n) -> p c n", c=2),
                                            ACT.Copy), t, tz)
            txp.append(r)
            return [r]
        gemm_fm(f"in{l}", 768, act, [4, 5], ev_x)

        def ev_q(j, p, t):
            return [ACTE(lambda e: e.activation(QK[:, 0:2, :], p.rearrange("p (c n) -> p c n", c=2), ACT.Copy), t)]
        gemm_fm(f"in{l}", 256, act, [6], ev_q)

        def ev_k(j, p, t):
            return [ACTE(lambda e: e.activation(QK[:, 2, :], p, ACT.Copy), t)]
        gemm_fm(f"in{l}", 128, act, [7], ev_k)
        t_k = K.last["a"]
        t = gemm_blk(f"in{l}", act, [2, 3], 128, 8)
        for k in range(2):
            pf[2 + k] = ACTE(lambda e: e.activation(AVD[:, k, 0:128], PS[:, 2 + k, 0:128], ACT.Copy), t)
        t = gemm_blk(f"in{l}", act, [0, 1], 8, 8)
        for k in range(2):
            pf[k] = ACTE(lambda e: e.activation(AVD[:, k, 128:136], PS[:, k, 0:8], ACT.Copy), t)
        t_av = K.last["a"]
        while side:
            side.pop(0)()
        f0 = [f0, K.last["v"], K.last["t"]]
        t = T(lambda e: e.matmul(PS[:, 6, 0:256], swap, QK[:, 2, :], start=True, stop=True), t_k, pf[6])
        t_ks = pf[6] = ACTE(lambda e: e.activation(QK[:, 3, :], PS[:, 6, 0:256], ACT.Copy), t)

        tcv = []
        for c in range(6):
            dst = XC[:, c, :]
            t = V(lambda e: e.tensor_scalar(dst, XP[:, c, 0:256], pcol(f"conv_w{l}", c), pcol(f"conv_b{l}", c),
                                            ALU.mult, ALU.add), txp, tz)
            for k in range(1, 4):
                t = V(lambda e: e.scalar_tensor_tensor(dst, XP[:, c, k:k + 256], pcol(f"conv_w{l}", 6 * k + c), dst,
                                                       ALU.mult, ALU.add), t)
            tcv.append(t)
        t_xc = ACTE(lambda e: e.activation(XC, XC, ACT.Silu), tcv)

        rq = R[:, :, 0:512].rearrange("p t (h x d) -> p t h x d", h=8, x=2)
        tmp = [ar(512 * i, 2, 8, 32) for i in range(4)]
        bc = lambda tab: AP(tab.tensor, tab.offset, [list(tab.ap[0]), [32, 2], [0, 8], [1, 32]])
        ops = ((0, COS), (1, SIN), (0, SIN), (1, COS))
        for i, (half, tab) in enumerate(ops):
            t = V(lambda e: e.tensor_tensor(tmp[i], rq[:, :, :, half, :], bc(tab), ALU.mult), t_r, t_rot, f0)
        t = V(lambda e: e.tensor_tensor(rq[:, :, :, 0, :], tmp[0], tmp[1], ALU.subtract), t)
        t = V(lambda e: e.tensor_tensor(rq[:, :, :, 1, :], tmp[2], tmp[3], ALU.add), t)
        for cp in range(2):
            b = 6 + cp
            t2 = transposes(b, [(PS[:, b, 256 * ci + 128 * tt:256 * ci + 128 * tt + 128],
                                 R[:, tt, 128 * (2 * cp + ci):128 * (2 * cp + ci) + 128])
                                for ci in range(2) for tt in range(2)], t)
            pf[b] = ACTE(lambda e: e.activation(QT[:, 2 * cp:2 * cp + 2, :], PS[:, b, :].rearrange(
                "p (c n) -> p c n", c=2), ACT.Copy), t2)
        t_qt = [pf[6], pf[7]]
        tr = []
        for h in range(4):
            b = 4 + h % 2
            pr, ch = slice(64 * (h % 2), 64 * (h % 2) + 64), h // 2

            def f(e):
                e.matmul(PS[:, b, 0:256], QT[pr, 2 + ch, 0:128], QT[pr, ch, :], start=True, stop=True)
                return e.matmul(PS[:, b, 256:384], QT[pr, 2 + ch, 128:256], QT[pr, ch, 128:256], start=True, stop=True)
            t = T(f, t_qt, pf[b])
            dec = CST[:, C_DEC + 256 * h:C_DEC + 256 * h + 256]
            V(lambda e: e.tensor_tensor(RT[:, h, 0:256], PS[:, b, 0:256], dec, ALU.mult), t, f0)
            pf[b] = V(lambda e: e.tensor_tensor(RT[:, h, 256:384], PS[:, b, 256:384], dec[:, 0:128], ALU.mult), t)
            tr.append(pf[b])
        rv = lambda k, h: R[:, k, 512 + 64 * h:512 + 64 * h + 64]

        def f(e):
            for h in range(4):
                e.matmul(PS[:, 0, 64 * h:64 * h + 64], RT[:, h, 0:128], rv(0, h), start=True, stop=True)
                e.matmul(PS[:, 0, 256 + 64 * h:256 + 64 * h + 64], RT[:, h, 128:256], rv(0, h), start=True, stop=False)
                m = e.matmul(PS[:, 0, 256 + 64 * h:256 + 64 * h + 64], RT[:, h, 256:384], rv(1, h), start=False,
                             stop=True)
            return m
        t = T(f, tr, t_r, pf[0])
        O8 = ar(2048, 8, 64)
        O8s = ar(2560, 8, 64)
        m8, v8 = SMT[:, 0:8], SMT[:, 8:16]
        b8 = lambda a: view(a, [1, 8], [0, 64])
        po = PS[:, 0, :].rearrange("p (a b) -> p a b", a=8)
        t = V(lambda e: e.tensor_reduce(m8, po, AX, ALU.add), t, f0)
        t = V(lambda e: e.tensor_scalar(m8, m8, 1.0 / 64, None, ALU.mult), t)
        t = V(lambda e: e.tensor_tensor(O8, po, b8(m8), ALU.subtract), t)
        pf[0] = t
        t = V(lambda e: e.tensor_tensor(O8s, O8, O8, ALU.mult), t)
        t = V(lambda e: e.tensor_reduce(v8, O8s, AX, ALU.add), t)
        t = V(lambda e: e.tensor_scalar(v8, v8, 1.0 / 64, None, ALU.mult), t)
        t = rsqrt(v8, v8, LN_EPS, t)
        t = V(lambda e: e.tensor_tensor(O8, O8, b8(v8), ALU.mult), t)
        t2 = ACTE(lambda e: e.activation(R[:, :, 768:1024], R[:, :, 768:1024], ACT.Silu), t_r)
        t_ret = V(lambda e: e.tensor_tensor(R[:, :, 0:256], R[:, :, 768:1024],
                                            O8.rearrange("p (t h) d -> p t (h d)", t=2), ALU.mult), t, t2,
                  K.last["t"])

        for c in range(4):
            b = 1 + c % 2
            t = transposes(b, [(PS[:, b, 128 * tt:128 * tt + 128], XC[:, c, 128 * tt:128 * tt + 128])
                               for tt in range(2)], t_xc)
            pf[b] = ACTE(lambda e: e.activation(XS[:, :, 128 * c:128 * c + 128], PS[:, b, 0:256].rearrange(
                "p (t n) -> p t n", t=2), ACT.Copy), t, f0)
        t_xs = pf[b]
        DTt, AA, T8, U8, CS, CSN = [SMT[:, 16 + 16 * i:32 + 16 * i] for i in range(6)]
        g2 = lambda a: a.rearrange("p (t h) -> p t h", t=2)
        dtr = AVD[:, :, 128:136]
        t = V(lambda e: e.tensor_tensor(g2(DTt), dtr, view(dtb[:, l, :], [0, 2], [1, 8]), ALU.add), t_av)
        t = softplus(DTt, DTt, 1.0, (T8, U8, CS, CSN, AA), t)
        t_dt = t
        ta = ACTE(lambda e: e.activation(T8[:, 0:8], alog[:, l, :], ACT.Exp), t)
        t = V(lambda e: e.scalar_tensor_tensor(g2(AA), g2(DTt), -1.0, view(T8, [0, 2], [1, 8]), ALU.mult, ALU.mult), t,
              ta)
        t_a = t

        def f(e):
            e.matmul(PS[:, 3, 0:8], tri, AA[:, 0:8], start=True, stop=True)
            e.matmul(PS[:, 3, 8:16], ones, AA[:, 0:8], start=True, stop=False)
            return e.matmul(PS[:, 3, 8:16], tri, AA[:, 8:16], start=False, stop=True)
        t = T(f, t, pf[3])
        pf[3] = t_cs = V(lambda e: e.tensor_copy(CS, PS[:, 3, 0:16]), t)
        t_xd = V(lambda e: e.tensor_tensor(XD.rearrange("p t (h d) -> p t h d", h=8),
                                           XS.rearrange("p t (h d) -> p t h d", h=8),
                                           view(DTt, [8, 2], [1, 8], [0, 64]), ALU.mult), t_xs, t_dt, f0)
        tt2 = []
        for h in range(8):
            b = 4 + h % 4
            col = lambda k: view(AA[:, 8 * k + h:8 * k + h + 1], [0, 128])

            def f(e):
                e.matmul(PS[:, b, 0:128], col(0), tri, start=True, stop=True)
                e.matmul(PS[:, b, 128:256], col(0), ones, start=True, stop=False)
                return e.matmul(PS[:, b, 128:256], col(1), tri, start=False, stop=True)
            t = T(f, t_a, pf[b])
            V(lambda e: e.scalar_tensor_tensor(E8[:, h, 0:256], negm, CS[:, h:h + 1], PS[:, b, 0:256], ALU.subtract,
                                               ALU.add), t, t_cs, t_ret)
            pf[b] = V(lambda e: e.scalar_tensor_tensor(E8[:, h, 256:384], negm[:, 0:128], CS[:, 8 + h:9 + h],
                                                       PS[:, b, 128:256], ALU.subtract, ALU.add), t, t_cs)
            tt2.append(pf[b])
        t_e = ACTE(lambda e: e.activation(E8, E8, ACT.Exp), tt2)
        for g in range(2):
            b = 2 + g
            pr = slice(64 * g, 64 * g + 64)

            def f(e):
                e.matmul(PS[:, b, 0:256], XC[pr, 4, 0:128], XC[pr, 5, :], start=True, stop=True)
                return e.matmul(PS[:, b, 256:384], XC[pr, 4, 128:256], XC[pr, 5, 128:256], start=True, stop=True)
            t = T(f, t_xc, pf[b])
            for r in range(4):
                h = 4 * g + r
                t2 = V(lambda e: e.tensor_tensor(E8[:, h, :], E8[:, h, :], PS[:, b, 0:384], ALU.mult), t, t_e)
            pf[b] = t2

        def f(e):
            for h in range(8):
                v = lambda k: XD[:, k, 64 * h:64 * h + 64]
                e.matmul(PS[:, 4, 64 * h:64 * h + 64], E8[:, h, 0:128], v(0), start=True, stop=True)
                e.matmul(PS[:, 5, 64 * h:64 * h + 64], E8[:, h, 128:256], v(0), start=True, stop=False)
                m = e.matmul(PS[:, 5, 64 * h:64 * h + 64], E8[:, h, 256:384], v(1), start=False, stop=True)
            return m
        t = T(f, t2, t_xd, pf[4], pf[5])
        h8 = lambda a: a.rearrange("p t (h d) -> p t h d", h=8)
        t3 = V(lambda e: e.tensor_tensor(h8(XS), h8(XS), view(dsk[:, l, :], [0, 2], [1, 8], [0, 64]), ALU.mult), t_xd)
        for k in range(2):
            pf[4 + k] = V(lambda e: e.tensor_tensor(XS[:, k, :], PS[:, 4 + k, :], XS[:, k, :], ALU.add), t, t3)
        t = V(lambda e: e.tensor_tensor(XS, XS, SZ, ALU.mult), pf[4], pf[5], t_sz)
        t = V(lambda e: e.tensor_tensor(XD, XS, XS, ALU.mult), t, K.last["t"])
        m4 = SMT[:, 0:4]
        t = V(lambda e: e.tensor_reduce(m4, XD.rearrange("p t (g d) -> p (t g) d", g=2), AX, ALU.add), t, t_ret)
        t = V(lambda e: e.tensor_scalar(m4, m4, 1.0 / 256, None, ALU.mult), t)
        t = rsqrt(m4, m4, LN_EPS, t)
        t_ssd = V(lambda e: e.tensor_tensor(R[:, :, 256:768].rearrange("p t (g d) -> p t g d", g=2),
                                            XS.rearrange("p t (g d) -> p t g d", g=2),
                                            view(m4, [2, 2], [1, 2], [0, 256]), ALU.mult), t, K.last["t"], t_ret)

        mx, ng, den, ek = [SMT[:, 128 + 8 * i:136 + 8 * i] for i in range(4)]
        for h in range(4):
            b = 4 + h
            base, kv = 64 * (h % 2), h // 2
            kc = 2 if base == 64 * kv else 3
            pr = slice(base, base + 64)

            def f(e):
                e.matmul(PS[:, b, 0:128], QK[pr, h // 2, 0:128], QK[pr, kc, 0:128], start=True, stop=True)
                return e.matmul(PS[:, b, 128:384], QK[pr, h // 2, 128:256], QK[pr, kc, :], start=True, stop=True)
            t = T(f, t_ks, t_k, pf[b])
            V(lambda e: e.scalar_tensor_tensor(LG[:, h, 0:128], PS[:, b, 0:128], 0.125, BT[:, h, 128:256], ALU.mult,
                                               ALU.add), t, t_bt, f0)
            pf[b] = V(lambda e: e.scalar_tensor_tensor(LG[:, h, 128:384], PS[:, b, 128:384], 0.125, BT[:, h, :],
                                                       ALU.mult, ALU.add), t)
        t = pf[7]
        V(lambda e: e.tensor_reduce(mx[:, 0:4], LG[:, :, 0:128], AX, ALU.max), t)
        t = V(lambda e: e.tensor_reduce(mx[:, 4:8], LG[:, :, 128:384], AX, ALU.max), t)
        t = V(lambda e: e.tensor_tensor(g2(mx), g2(mx), view(snk[:, l, :], [0, 2], [1, 4]), ALU.max), t)
        tn = V(lambda e: e.tensor_scalar(ng, mx, -1.0, None, ALU.mult), t)
        t = V(lambda e: e.tensor_tensor(g2(ek), g2(ng), view(snk[:, l, :], [0, 2], [1, 4]), ALU.add), tn)
        t5 = ACTE(lambda e: e.activation(ek, ek, ACT.Exp), t)
        for h in range(4):
            ACTE(lambda e: e.activation(LG[:, h, 0:128], LG[:, h, 0:128], ACT.Exp, bias=ng[:, h:h + 1],
                                        accum_out=den[:, h:h + 1]), tn)
            t = ACTE(lambda e: e.activation(LG[:, h, 128:384], LG[:, h, 128:384], ACT.Exp, bias=ng[:, 4 + h:5 + h],
                                            accum_out=den[:, 4 + h:5 + h]), tn)
        t = V(lambda e: e.tensor_tensor(den, den, ek, ALU.add), t, t5)
        t_den = V(lambda e: e.reciprocal(den, den), t)
        tp = []
        for h in range(4):
            b = 4 + h
            t = transposes(b, [(PS[:, b, 128 * i:128 * i + 128], LG[:, h, 128 * i:128 * i + 128]) for i in range(3)],
                           t_den)
            pf[b] = ACTE(lambda e: e.activation(PT[:, h, :], PS[:, b, 0:384], ACT.Copy), t, tcv)
            tp.append(pf[b])

        def f(e):
            for h in range(4):
                v = lambda k: AVD[:, k, 64 * (h // 2):64 * (h // 2) + 64]
                e.matmul(PS[:, 0, 64 * h:64 * h + 64], PT[:, h, 0:128], v(0), start=True, stop=True)
                e.matmul(PS[:, 0, 256 + 64 * h:256 + 64 * h + 64], PT[:, h, 128:256], v(0), start=True, stop=False)
                m = e.matmul(PS[:, 0, 256 + 64 * h:256 + 64 * h + 64], PT[:, h, 256:384], v(1), start=False, stop=True)
            return m
        t = T(f, tp, t_av, pf[0])
        pf[0] = V(lambda e: e.tensor_tensor(R[:, :, 768:1024].rearrange("p t (h d) -> p t h d", h=4),
                                            PS[:, 0, :].rearrange("p (t h d) -> p t h d", t=2, h=4),
                                            view(den, [4, 2], [1, 4], [0, 64]), ALU.mult), t, t_den, t_ret)
        t = [pf[0], t_ssd, t_ret]
        marks = K.fence()

        def ev(c, p, t, dst):
            if 2 <= c < 6:
                return V(lambda e: e.tensor_scalar(dst, p, pcol(f"ssd_norm{l}", c - 2), None, ALU.mult), t)
            return V(lambda e: e.tensor_copy(dst, p), t)
        act = to_fm(R, X2H, X2L, [2, 3], marks, ev)
        t = gemm_tm(f"out{l}", act, [4, 5, 6, 7])
        t = residual(l, 0, [4, 5, 6, 7], t)
        marks = K.fence()
        if l == 0:
            act = to_fm(X, X1H, X1L, [2, 3], marks, scaled(lambda c: modc(l, 4, c), lambda c: modc(l, 3, c)))
            for b_ in range(3):
                side.extend(ada_block(1, b_, ar(10240 + 2048 * b_, 2048)))
            t = ffn("ffn", 11, act, swiglu_evac(), True, True)
            while side:
                side.pop(0)()
            t = residual(l, 1, [4, 5, 6, 7], t)
        else:
            t = moe()
            t = residual(l, 1, None, t, ar(14080, 2, 1024))

    SMT = sm(256)
    FLAG = SM[:, sm_at[0]:sm_at[0] + 1].bitcast(I32)
    sm(1)

    def softplus(dst, src, sign, tmps, *deps):
        a, tt_, u, w, z = tmps
        t = V(lambda e: e.tensor_scalar(a, src, sign, None, ALU.mult), *deps)
        t = ACTE(lambda e: e.activation(tt_, a, ACT.Abs), t)
        t = ACTE(lambda e: e.activation(tt_, tt_, ACT.Exp, scale=-1.0), t)
        t = V(lambda e: e.tensor_scalar(u, tt_, 1.0, None, ALU.add), t)
        t2 = ACTE(lambda e: e.activation(w, u, ACT.Ln), t)
        t = V(lambda e: e.tensor_scalar(u, u, -1.0, None, ALU.add), t, t2)
        t = V(lambda e: e.tensor_scalar(z, u, 0.0, None, ALU.is_equal), t)
        t = V(lambda e: e.tensor_tensor(u, u, z, ALU.add), t)
        t = V(lambda e: e.reciprocal(u, u), t)
        t = V(lambda e: e.tensor_tensor(w, w, tt_, ALU.mult), t)
        t = V(lambda e: e.tensor_tensor(w, w, u, ALU.mult), t)
        t = V(lambda e: e.tensor_tensor(z, z, tt_, ALU.mult), t)
        t = V(lambda e: e.tensor_tensor(w, w, z, ALU.add), t)
        return V(lambda e: e.scalar_tensor_tensor(dst, a, 0.0, w, ALU.max, ALU.add), t)

    HM = ar(6144, 2, 1024)
    RK, RP, RP2, GG, LGT = [ar(8192 + 16 * i, 2, 8) for i in range(5)]
    m1, den2, CNT = ar(8272, 2), ar(8274, 2), ar(8280, 8)
    PP, PG, PGT = ar(8448, 2, 2, 128), ar(8960, 2, 2, 128), ar(9472, 2, 256)
    SGm, HFm = ar(9984, 2, 512), ar(11008, 2, 512)
    YE = ar(12032, 2, 1024)
    FACC = ar(14080, 2, 1024)

    def router():
        CMP, CM2 = ar(9984, 2, 8, 8), ar(10112, 2, 8, 8)
        SCR, SHR = ar(12032, 1024), ar(13056, 1024)
        t1 = rows_of(1, 4, SCR)
        t2 = rows_of(1, 3, SHR)
        for k in range(2):
            t = V(lambda e: e.tensor_tensor(HM[:, k, :], X[:, k, :], SCR, ALU.mult), t1, K.last["v"])
            t = V(lambda e: e.tensor_tensor(HM[:, k, :], HM[:, k, :], SHR, ALU.add), t, t2)
        for cp in range(4):
            b = 2 + cp % 2
            t3 = transposes(b, [(PS[:, b, 256 * ci + 128 * tt:256 * ci + 128 * tt + 128],
                                 HM[:, tt, 128 * (2 * cp + ci):128 * (2 * cp + ci) + 128])
                                for ci in range(2) for tt in range(2)], t)
            pf[b] = ACTE(lambda e: e.activation(XF[:, 2 * cp:2 * cp + 2, :], PS[:, b, :].rearrange(
                "p (c n) -> p c n", c=2), ACT.Copy), t3)

        def f(e):
            for k in range(2):
                for c in range(8):
                    m = e.matmul(PS[:, 0, 8 * k:8 * k + 8], XF[:, c, 128 * k:128 * k + 128], WR[:, c, :],
                                 start=(c == 0), stop=(c == 7))
            return m
        t = T(f, pf[2], pf[3], pf[0])
        t = V(lambda e: e.tensor_tensor(LGT, PS[:, 0, 0:16].rearrange("p (k n) -> p k n", k=2),
                                        view(rbias, [0, 2], [1, 8]), ALU.add), t)
        pf[0] = t
        mine = view(LGT, [8, 2], [1, 8], [0, 8])
        other = view(LGT, [8, 2], [0, 8], [1, 8])
        low = view(CST[:, C_LOW:C_LOW + 64], [0, 2], [8, 8], [1, 8])
        t1 = V(lambda e: e.tensor_tensor(CMP, other, mine, ALU.is_gt), t)
        t2 = V(lambda e: e.tensor_tensor(CM2, other, mine, ALU.is_equal), t)
        t2 = V(lambda e: e.tensor_tensor(CM2, CM2, low, ALU.mult), t2)
        t2 = V(lambda e: e.tensor_tensor(CMP, CMP, CM2, ALU.add), t1, t2)
        t2 = V(lambda e: e.tensor_reduce(RK, CMP, AX, ALU.add), t2)
        t_sel = V(lambda e: e.tensor_scalar(RK, RK, 1.5, None, ALU.is_lt), t2)
        t = V(lambda e: e.tensor_reduce(m1, LGT, AX, ALU.max), t)
        t = V(lambda e: e.tensor_tensor(GG, LGT, view(m1, [1, 2], [0, 8]), ALU.subtract), t)
        t = ACTE(lambda e: e.activation(GG, GG, ACT.Exp), t)
        t = V(lambda e: e.tensor_tensor(GG, GG, RK, ALU.mult), t, t_sel)
        t = V(lambda e: e.tensor_reduce(den2, GG, AX, ALU.add), t)
        t = V(lambda e: e.reciprocal(den2, den2), t)
        t_gg = V(lambda e: e.tensor_tensor(GG, GG, view(den2, [1, 2], [0, 8]), ALU.mult), t)

        def f(e):
            e.matmul(PS[:, 1, 0:8], tri, RK[:, 0, :], start=True, stop=True)
            e.matmul(PS[:, 1, 8:16], ones, RK[:, 0, :], start=True, stop=False)
            e.matmul(PS[:, 1, 8:16], tri, RK[:, 1, :], start=False, stop=True)
            e.matmul(PS[:, 1, 16:24], ones, RK[:, 0, :], start=True, stop=False)
            return e.matmul(PS[:, 1, 16:24], ones, RK[:, 1, :], start=False, stop=True)
        t = T(f, t_sel, pf[1])
        t2 = V(lambda e: e.tensor_scalar(RP, RK, -1001.0, 1000.0, ALU.mult, ALU.add), t_sel)
        t2 = V(lambda e: e.tensor_tensor(RP, RP, PS[:, 1, 0:16].rearrange("p (k n) -> p k n", k=2), ALU.add), t, t2)
        t_rp = V(lambda e: e.tensor_scalar(RP2, RP, -128.0, None, ALU.add), t2)
        pf[1] = t3 = V(lambda e: e.tensor_reduce(CNT[:, 0:1], PS[:, 1, 16:24], AX, ALU.max), t)
        t_fl = V(lambda e: e.tensor_scalar(FLAG, CNT[:, 0:1], 128.5, None, ALU.is_gt), t3)
        return [t_gg, t_rp, t_fl]

    def moe():
        t_r = router()
        f0 = K.fence()
        t_f = V(lambda e: e.memset(FACC, 0.0), f0)
        GH = X1H[:, :, :].rearrange("p a b -> p (a b)").rearrange("p (s c n) -> p s c n", s=2, c=8)
        GL = X1L[:, :, :].rearrange("p a b -> p (a b)").rearrange("p (s c n) -> p s c n", s=2, c=8)
        RH = X2H[:, :, :].rearrange("p a b -> p (a b)").rearrange("p (s c n) -> p s c n", s=4, c=4)
        RL = X2L[:, :, :].rearrange("p a b -> p (a b)").rearrange("p (s c n) -> p s c n", s=4, c=4)
        iota = CST[:, C_IOT:C_IOT + 128]
        gx, pgt, used, yev = {}, {}, {}, {}

        def select(e_):
            s_ = e_ % 2
            for k in range(2):
                V(lambda e: e.tensor_scalar(PP[:, s_, k, :], iota, RP[:, k, e_:e_ + 1], None, ALU.is_equal), t_r,
                  used.get(("p", e_ - 2)))
                t = V(lambda e: e.tensor_scalar(PG[:, s_, k, :], iota, RP[:, k, e_:e_ + 1], GG[:, k, e_:e_ + 1],
                                                ALU.is_equal, ALU.mult))
            gx[e_] = []
            pgt[("pp", e_)] = t

        def gather(e_, half):
            s_ = e_ % 2

            def f(e):
                for c in range(4):
                    for k in range(2):
                        m = e.matmul(PS[:, 7, 128 * c:128 * c + 128], HM[:, k, 512 * half + 128 * c:512 * half + 128 * c + 128],
                                     PP[:, s_, k, :], start=(k == 0), stop=(k == 1))
                return m
            t = T(f, pgt[("pp", e_)], pf[7])
            pf[7] = split_act(PS[:, 7, :].rearrange("p (c n) -> p c n", c=4), GH[:, s_, 4 * half:4 * half + 4, :],
                              GL[:, s_, 4 * half:4 * half + 4, :], t, used.get(("x", e_ - 2)))
            gx[e_] += pf[7]

        def turn(e_):
            s_ = e_ % 2
            t = transposes(7, [(PS[:, 7, 128 * k:128 * k + 128], PG[:, s_, k, :]) for k in range(2)],
                           pgt[("pp", e_)])
            used[("p", e_)] = t
            pf[7] = pgt[e_] = ACTE(lambda e: e.activation(PGT[:, s_, :], PS[:, 7, 0:256], ACT.Copy), t,
                                   used.get(("s", e_ - 2)))

        def scatter(e_, q):
            s_, k, nb = e_ % 2, q // 2, q % 2
            ns = slice(512 * nb, 512 * nb + 512)
            t = T(lambda e: e.matmul(PS[:, 7, :], PGT[:, s_, 128 * k:128 * k + 128], YE[:, s_, ns], start=True, stop=True),
                  pgt[e_], yev[e_], pf[7])
            used[("s", e_)] = t
            pf[7] = V(lambda e: e.tensor_tensor(FACC[:, k, ns], FACC[:, k, ns], PS[:, 7, :], ALU.add), t, t_f)

        todo = []

        def between():
            if todo:
                todo.pop(0)()

        select(0)
        gather(0, 0)
        gather(0, 1)
        turn(0)
        hid = {}
        n = 0
        for e_ in range(NEXP):
            XH, XL = GH[:, e_ % 2], GL[:, e_ % 2]
            if e_ > 0:
                todo.extend([lambda q=q, e_=e_: scatter(e_ - 1, q) for q in range(4)])
            if e_ < NEXP - 1:
                todo.extend([lambda e_=e_: select(e_ + 1), lambda e_=e_: gather(e_ + 1, 0),
                             lambda e_=e_: gather(e_ + 1, 1), lambda e_=e_: turn(e_ + 1)])
            for b_ in range(8):
                if b_ < 7:
                    got2 = []
                    for q, kk_ in ((0, "mg"), (1, "mu")):
                        bk = 2 * q + b_ % 2
                        for k0 in (0, 4):
                            i, hi, lo, got = take(kk_)

                            def f(e):
                                for c in range(4):
                                    m = mm3(e, PS[:, bk, :], XH[:, k0 + c, :], XL[:, k0 + c, :], hi[:, c, :], lo[:, c, :],
                                            k0 + c == 0, k0 + c == 7)
                                return m
                            t = T(f, got, gx[e_], pf[bk])
                            done(i, t)
                            if q == 0 and k0 == 0 and b_ > 0:
                                tr = transposes(4, [(PS[:, 4, 128 * j:128 * j + 128], HFm[:, (b_ - 1) % 2, 128 * j:128 * j + 128])
                                                    for j in range(4)], hid["t"])
                                sl = (7 * e_ + b_ - 1) % 3
                                hid[("tr", (b_ - 1) % 2)] = tr
                                pf[4] = hid["s"] = split_act(PS[:, 4, :].rearrange("p (c n) -> p c n", c=4), RH[:, sl],
                                                             RL[:, sl], tr, hid.get(("d", sl)))
                            else:
                                between()
                        got2.append((bk, t))
                    (bg, tg_), (bu, tu) = got2
                    s2 = b_ % 2
                    if b_ == 6:
                        used[("x", e_)] = tu
                    t = ACTE(lambda e: e.activation(SGm[:, s2, :], PS[:, bg, :], ACT.Silu), tg_, hid.get(("h", s2)))
                    pf[bg] = t
                    t = V(lambda e: e.tensor_tensor(HFm[:, s2, :], SGm[:, s2, :], PS[:, bu, :], ALU.mult), t, tu,
                          hid.get(("tr", s2)))
                    pf[bu] = hid[("h", s2)] = hid["t"] = t
                else:
                    tr = transposes(4, [(PS[:, 4, 128 * j:128 * j + 128], HFm[:, (b_ - 1) % 2, 128 * j:128 * j + 128])
                                        for j in range(4)], hid["t"])
                    sl = (7 * e_ + b_ - 1) % 3
                    hid[("tr", (b_ - 1) % 2)] = tr
                    pf[4] = hid["s"] = split_act(PS[:, 4, :].rearrange("p (c n) -> p c n", c=4), RH[:, sl], RL[:, sl], tr,
                                                 hid.get(("d", sl)))
                if b_ > 0:
                    sl = (7 * e_ + b_ - 1) % 3
                    for half in range(2):
                        i, hi, lo, got = take("md")

                        def f(e):
                            for c in range(2):
                                q = 2 * half + c
                                for nb in range(2):
                                    ns = slice(512 * nb, 512 * nb + 512)
                                    m = mm3(e, PS[:, 5 + nb, :], RH[:, sl, q, :], RL[:, sl, q, :], hi[:, c, ns],
                                            lo[:, c, ns], b_ == 1 and q == 0, b_ == 7 and q == 3)
                            return m
                        t = T(f, got, hid["s"], [pf[5], pf[6]] if b_ == 1 and half == 0 else None)
                        hid[("d", sl)] = t
                        done(i, t)
                        between()
            for nb in range(2):
                ns = slice(512 * nb, 512 * nb + 512)
                pf[5 + nb] = ACTE(lambda e: e.activation(YE[:, e_ % 2, ns], PS[:, 5 + nb, :], ACT.Copy), t,
                                  used.get(("s", e_ - 2)))
            yev[e_] = [pf[5], pf[6]]
            assert not todo
        for q in range(4):
            scatter(NEXP - 1, q)
        marks = K.fence()
        K.wait("s", marks)
        rest_of_rows()
        return marks

    def rest_of_rows():
        sems = {e: K.sem("s_r" + e) for e in "vagt"}
        sems.update({f"r{i}": K.sem(f"s_r{i}") for i in range(2)})
        names = {"v": "vector", "a": "scalar", "g": "gpsimd", "t": "tensor", "s": "sync"}
        with nc.Block() as blk:
            def part(n):
                def _(eng):
                    over = eng.value_load(FLAG[0:1, 0:1], min_val=0, max_val=1)
                    with eng.If(over > 0):
                        rest_body(Core(nc, ctx, "r", n, sems))
                return _
            blk.vector(part("v"))
            blk.scalar(part("a"))
            blk.gpsimd(part("g"))
            blk.tensor(part("t"))
            blk.sync(part("s"))

    def rest_body(R):
        XG, HT2 = ar(0, 8, 128), ar(1024, 4, 128)
        WB2 = [ar(2048, 2048), ar(4096, 2048)]
        P1, G1, GT1, Y1 = ar(8448, 2, 128), ar(8704, 2, 128), ar(8960, 256), ar(12032, 1024)
        H1 = ar(9984, 512)
        iota = CST[:, C_IOT:C_IOT + 128]
        free = [None, None]
        n = [0]

        def load(src):
            i = n[0] % 2
            n[0] += 1
            dst = WB2[i].rearrange("p (c n) -> p c n", c=src.shape[1])
            return i, dst, R.dma("s", f"r{i}", dst, src, free[i])
        t_e = None
        for e_ in range(NEXP):
            for k in range(2):
                R.V(lambda e: e.tensor_scalar(P1[:, k, :], iota, RP2[:, k, e_:e_ + 1], None, ALU.is_equal), t_e)
                t = R.V(lambda e: e.tensor_scalar(G1[:, k, :], iota, RP2[:, k, e_:e_ + 1], GG[:, k, e_:e_ + 1],
                                                  ALU.is_equal, ALU.mult))
            for half in range(2):
                def f(e):
                    for c in range(4):
                        for k in range(2):
                            m = e.matmul(PS[:, half, 128 * c:128 * c + 128],
                                         HM[:, k, 512 * half + 128 * c:512 * half + 128 * c + 128], P1[:, k, :],
                                         start=(k == 0), stop=(k == 1))
                    return m
                t2 = R.T(f, t)
                tx = R.A(lambda e: e.activation(XG[:, 4 * half:4 * half + 4, :], PS[:, half, :].rearrange(
                    "p (c n) -> p c n", c=4), ACT.Copy), t2)

            def f(e):
                for k in range(2):
                    m = e.transpose(PS[:, 2, 128 * k:128 * k + 128], G1[:, k, :], ident)
                return m
            t2 = R.T(f, t)
            tgt = R.A(lambda e: e.activation(GT1, PS[:, 2, 0:256], ACT.Copy), t2)
            th = None
            for b_ in range(7):
                for q, w in ((0, A["expert_w_gate"][0, e_]), (1, A["expert_w_up"][0, e_])):
                    for _, src, _ in u_blk(w, 512 * b_, 512 * b_ + 512, ""):
                        i, wt, tw = load(src)
                        k0 = 0 if src.offset == w[0:1, 512 * b_:512 * b_ + 1].offset else 4

                        def f(e):
                            for c in range(4):
                                m = e.matmul(PS[:, q, :], XG[:, k0 + c, :], wt[:, c, :], start=(k0 + c == 0),
                                             stop=(k0 + c == 7))
                            return m
                        t = R.T(f, tw, tx, th)
                        free[i] = t
                t2 = R.A(lambda e: e.activation(H1, PS[:, 0, :], ACT.Silu), t)
                t2 = R.V(lambda e: e.tensor_tensor(H1, H1, PS[:, 1, :], ALU.mult), t2)

                def f(e):
                    for j in range(4):
                        m = e.transpose(PS[:, 3, 128 * j:128 * j + 128], H1[:, 128 * j:128 * j + 128], ident)
                    return m
                t2 = R.T(f, t2)
                th = R.A(lambda e: e.activation(HT2, PS[:, 3, :].rearrange("p (c n) -> p c n", c=4), ACT.Copy), t2)
                for half, (_, src, _) in enumerate(u_tm(A["expert_w_down"][0, e_], 4 * b_, 4 * b_ + 4, "")):
                    i, wt, tw = load(src)

                    def f(e):
                        for c in range(2):
                            q = 2 * half + c
                            for nb in range(2):
                                m = e.matmul(PS[:, 5 + nb, :], HT2[:, q, :], wt[:, c, 512 * nb:512 * nb + 512],
                                             start=(b_ == 0 and q == 0), stop=(b_ == 6 and q == 3))
                        return m
                    t = R.T(f, tw, th)
                    free[i] = t
                th = [th, t]
            for nb in range(2):
                t2 = R.A(lambda e: e.activation(Y1[:, 512 * nb:512 * nb + 512], PS[:, 5 + nb, :], ACT.Copy), t)
            for q in range(4):
                k, nb = q // 2, q % 2
                ns = slice(512 * nb, 512 * nb + 512)
                t3 = R.T(lambda e: e.matmul(PS[:, 7, :], GT1[:, 128 * k:128 * k + 128], Y1[:, ns], start=True, stop=True),
                         t2, tgt, t_e)
                t_e = R.V(lambda e: e.tensor_tensor(FACC[:, k, ns], FACC[:, k, ns], PS[:, 7, :], ALU.add), t3)
        R.wait("s", R.fence())

    U = BT[:, :, :].rearrange("p h n -> p (h n)")
    WG = U[:, 0:384].rearrange("p (l c n) -> p l c n", l=2, c=24)
    WB = U[:, 384:576].rearrange("p (j n) -> p j n", j=6)

    def load_small():
        marks = K.fence()
        for l in range(2):
            K.dma("a", d5, WG[:, l], A["ml_w_gate_2"][l].rearrange("(c p) n -> p c n", p=128), marks)
            for j, nm in enumerate(("ml_wq_2", "ml_wk_2", "ml_wv_2")):
                K.dma("a", d5, WB[:, 3 * l + j, :].rearrange("p (c d) -> p c d", d=4),
                      A[nm][l].rearrange("(c n) k d -> (n k) c d", n=32))
        return (d5, K.count[d5])

    def rms(src, dst, *deps):
        for k in range(2):
            t = ACTE(lambda e: e.activation(dst[:, k, :], src[:, k, :], ACT.Square, accum_out=RS[:, k:k + 1]), *deps)
        t = V(lambda e: e.tensor_scalar(RS, RS, 1.0 / D, None, ALU.mult), t)
        t = rsqrt(RS, RS, RMS_EPS, t)
        for k in range(2):
            t2 = V(lambda e: e.tensor_scalar(dst[:, k, :], src[:, k, :], RS[:, k:k + 1], None, ALU.mult), t)
        return t2

    def by_col(name):
        def evac(c, p, t, dst):
            return V(lambda e: e.tensor_scalar(dst, p, pcol(name, c), None, ALU.mult), t)
        return evac

    def add_x(banks, t):
        for k in range(2):
            for nb in range(2):
                b = banks[2 * k + nb]
                xs = X[:, k, 512 * nb:512 * nb + 512]
                pf[b] = V(lambda e: e.tensor_tensor(xs, xs, PS[:, b, :], ALU.add), t)
        return pf[b]

    def fm_to(dst, func, name, off, pad=0, extra=None, into=None):
        def evac(j, p, t):
            for ci in range(2):
                c = 2 * j + ci
                o = dst[:, c, pad:pad + 256]
                s_ = p[:, 256 * ci:256 * ci + 256]
                if name is None:
                    r = ACTE(lambda e: e.activation(o, s_, func), t, extra)
                else:
                    r = ACTE(lambda e: e.activation(o, s_, func, bias=pcol(name, off + c)), t, extra)
            if into is not None:
                into(j, r)
            return [r]
        return evac

    def layer2(l, t_small):
        XN = ar(2048, 2, 1024)
        XM = ar(2048, 8, 259)
        UP = ar(4120, 8, 286)
        XC = ar(6408, 8, 256)
        R8 = ar(8456, 8, 256)
        UC = ar(10504, 8, 256)
        QF = ar(12552, 8, 256)
        KF = ar(14600, 8, 256)
        VT = ar(0, 2, 1024)
        marks = K.fence()
        t = rms(X, XN, marks)
        act = to_fm(XN, X1H, X1L, [4, 5, 6, 7], t, by_col(f"norm_mix{l}"))
        tz = [G(lambda e: e.memset(UP[:, :, 0:30], 0.0), marks)]
        tz.append(G(lambda e: e.memset(XM[:, :, 0:3], 0.0), act[2]))
        gemm_fm(f"in2{l}", 1024, act, [0, 1], fm_to(XM, ACT.Identity, f"b_in{l}", 0, 3, tz))
        t_xm = K.last["a"]
        tcv = []
        for c in range(8):
            dst = XC[:, c, :]
            t = V(lambda e: e.tensor_scalar(dst, XM[:, c, 0:256], pcol(f"ml_conv_w{l}", c), pcol(f"ml_conv_b{l}", c),
                                            ALU.mult, ALU.add), t_xm, tz)
            for k in range(1, 4):
                t = V(lambda e: e.scalar_tensor_tensor(dst, XM[:, c, k:k + 256], pcol(f"ml_conv_w{l}", 8 * k + c), dst,
                                                       ALU.mult, ALU.add), t)
            tcv.append(t)
        t_xc = ACTE(lambda e: e.activation(XC, XC, ACT.Silu), tcv)
        gemm_fm(f"in2{l}", 1024, act, [0, 1], fm_to(UP, ACT.Identity, f"b_in{l}", 16, 30, tz))
        t_a = K.last["a"]

        def ev_g(j, p, t):
            for ci in range(2):
                c = 2 * j + ci
                r = ACTE(lambda e: e.activation(R8[:, c, :], p[:, 256 * ci:256 * ci + 256], ACT.Sigmoid,
                                                bias=pcol(f"b_in{l}", 24 + c)), t)
            V(lambda e: e.tensor_tensor(UP[:, 2 * j:2 * j + 2, 30:286], UP[:, 2 * j:2 * j + 2, 30:286],
                                        R8[:, 2 * j:2 * j + 2, :], ALU.mult), r, t_a)
            return [r]
        gemm_fm(f"in2{l}", 1024, act, [0, 1], ev_g)
        t_u = K.last["v"]

        bd = [UC[:, 4 * i:4 * i + 4, :].rearrange("p a b -> p (a b)").rearrange("p (c n) -> p c n", c=8)
              for i in range(2)]
        tq = {}
        prev = {}
        for j, src in enumerate((XC, XC, XM)):
            B_ = bd[j % 2]
            t = V(lambda e: e.tensor_tensor(view(B_, [128, 8], [4, 32], [1, 4]), view(WB[:, 3 * l + j, :], [4, 8], [0, 32],
                                            [1, 4]), view(CST[:, C_BD:C_BD + 32], [0, 8], [1, 32], [0, 4]), ALU.mult),
                  t_small, prev.get(j - 2), marks)
            dst = (QF, KF, R8)[j]
            off = 3 if j == 2 else 0
            for cp in range(4):
                b = 2 + cp % 2

                def f(e):
                    for ci in range(2):
                        c = 2 * cp + ci
                        m = e.matmul(PS[:, b, 256 * ci:256 * ci + 256], B_[:, c, :], src[:, c, off:off + 256],
                                     start=True, stop=True)
                    return m
                t2 = T(f, t, t_xc, t_xm, pf[b])
                pf[b] = ACTE(lambda e: e.activation(dst[:, 2 * cp:2 * cp + 2, :], PS[:, b, :].rearrange(
                    "p (c n) -> p c n", c=2), ACT.Copy), t2, t_u)
                prev[j] = t2
            tq[j] = pf[b]
        for k in range(2):
            for hf in range(2):
                b = 4 + 2 * k + hf
                t2 = T(lambda e: [e.matmul(PS[:, b, 128 * c:128 * c + 128], XM[:, 4 * hf + c, 3 + 128 * k:131 + 128 * k],
                                           B_[:, 4 * hf + c, :], start=True, stop=True) for c in range(4)][-1], pf[b])
                pf[b] = ACTE(lambda e: e.activation(VT[:, k, 512 * hf:512 * hf + 512], PS[:, b, :], ACT.Copy), t2,
                             act[2])
        t_vt = pf[b]
        t_bd = t2

        def f(e):
            for k in range(2):
                for i in range(24):
                    src = (QF, KF, R8)[i // 8]
                    m = e.matmul(PS[:, 0, 8 * k:8 * k + 8], src[:, i % 8, 128 * k:128 * k + 128], WG[:, l, i, :],
                                 start=(i == 0), stop=(i == 23))
            return m
        t = T(f, tq[0], tq[1], tq[2], pf[0])
        t_gt = t
        GA, SPF, CSF, Gc, NM, DN = [SMT[:, 16 * i:16 * i + 16] for i in range(6)]
        g2 = lambda a, n=8: a[:, 0:2 * n].rearrange("p (t h) -> p t h", t=2)
        pf[0] = V(lambda e: e.tensor_tensor(g2(GA), PS[:, 0, 0:16].rearrange("p (t h) -> p t h", t=2),
                                            view(mbg[:, l, :], [0, 2], [1, 8]), ALU.add), t, marks)
        t = softplus(SPF, GA, -1.0, [SMT[:, 96 + 16 * i:112 + 16 * i] for i in range(5)], pf[0])

        def f(e):
            e.matmul(PS[:, 1, 0:8], tri, SPF[:, 0:8], start=True, stop=True)
            e.matmul(PS[:, 1, 8:16], ones, SPF[:, 0:8], start=True, stop=False)
            return e.matmul(PS[:, 1, 8:16], tri, SPF[:, 8:16], start=False, stop=True)
        t = T(f, t, pf[1])
        t = pf[1] = V(lambda e: e.tensor_copy(CSF, PS[:, 1, 0:16]), t)
        t = V(lambda e: e.tensor_tensor(g2(Gc, 4), g2(GA)[:, :, 0:4], g2(CSF)[:, :, 4:8], ALU.add), t)
        t_g = t
        t = transposes(1, [(PS[0:4, 1, 128 * k:128 * k + 128], Gc[:, 4 * k:4 * k + 4]) for k in range(2)], t)
        GR, MR = ROWS[0:4, 0, :], ROWS[0:4, 1, :]
        pf[1] = V(lambda e: e.tensor_copy(GR, PS[0:4, 1, 0:256]), t)
        t = V(lambda e: e.tensor_tensor_scan(MR, GR, GR, 0.0, ALU.max, ALU.max), pf[1])
        t_mr = t
        t = transposes(1, [(PS[:, 1, 4 * k:4 * k + 4], MR[:, 128 * k:128 * k + 128]) for k in range(2)], t)
        pf[1] = V(lambda e: e.tensor_tensor(g2(NM, 4), g2(CSF)[:, :, 4:8], PS[:, 1, 0:8].rearrange(
            "p (t h) -> p t h", t=2), ALU.subtract), t)
        t_nm = ACTE(lambda e: e.activation(NM[:, 0:8], NM[:, 0:8], ACT.Exp), pf[1])
        EE = ar(8456, 4, 384)
        te = []
        for h in range(4):
            b = 4 + h
            t = T(lambda e: e.matmul(PS[:, b, 0:256], view(ident[0:4, h:h + 1], [0, 128]), MR, start=True, stop=True),
                  t_mr, pf[b])
            V(lambda e: e.scalar_tensor_tensor(EE[:, h, 0:256], negm, Gc[:, h:h + 1], PS[:, b, 0:256], ALU.add,
                                               ALU.subtract), t, t_g, t_gt)
            pf[b] = V(lambda e: e.scalar_tensor_tensor(EE[:, h, 256:384], negm[:, 0:128], Gc[:, 4 + h:5 + h],
                                                       PS[:, b, 128:256], ALU.add, ALU.subtract), t)
            te.append(ACTE(lambda e: e.activation(EE[:, h, :], EE[:, h, :], ACT.Exp), pf[b]))
        tp = []
        for h in range(4):
            b = 2 + h % 2

            def f(e):
                for c in (2 * h, 2 * h + 1):
                    e.matmul(PS[:, b, 0:256], KF[:, c, 0:128], QF[:, c, :], start=(c == 2 * h), stop=(c == 2 * h + 1))
                for c in (2 * h, 2 * h + 1):
                    m = e.matmul(PS[:, b, 256:384], KF[:, c, 128:256], QF[:, c, 128:256], start=(c == 2 * h),
                                 stop=(c == 2 * h + 1))
                return m
            t = T(f, tq[0], tq[1], pf[b])
            pf[b] = V(lambda e: e.scalar_tensor_tensor(EE[:, h, :], PS[:, b, 0:384], 0.0625, EE[:, h, :], ALU.mult,
                                                       ALU.mult), t, te[h])
            tp.append(pf[b])

        def f(e):
            for h in range(4):
                e.matmul(PS[:, 0, h:h + 1], EE[:, h, 0:128], ones[:, 0:1], start=True, stop=True)
                e.matmul(PS[:, 0, 4 + h:5 + h], EE[:, h, 128:256], ones[:, 0:1], start=True, stop=False)
                m = e.matmul(PS[:, 0, 4 + h:5 + h], EE[:, h, 256:384], ones[:, 0:1], start=False, stop=True)
            return m
        t = T(f, tp, pf[0])
        t = pf[0] = ACTE(lambda e: e.activation(DN[:, 0:8], PS[:, 0, 0:8], ACT.Abs), t)
        t = V(lambda e: e.tensor_tensor(DN[:, 0:8], DN[:, 0:8], NM[:, 0:8], ALU.max), t, t_nm)
        t_dn = V(lambda e: e.reciprocal(DN[:, 0:8], DN[:, 0:8]), t)
        HT = ar(2048, 2, 1024)
        MV8, R8s, ST8 = SMT[:, 96:112], SMT[:, 112:120], SMT[:, 176:224].rearrange("p (a b) -> p a b", a=8)
        for h in range(4):
            b = 4 + h

            def f(e):
                v = lambda k: VT[:, k, 256 * h:256 * h + 256]
                e.matmul(PS[:, b, 0:256], EE[:, h, 0:128], v(0), start=True, stop=True)
                e.matmul(PS[:, b, 256:512], EE[:, h, 128:256], v(0), start=True, stop=False)
                return e.matmul(PS[:, b, 256:512], EE[:, h, 256:384], v(1), start=False, stop=True)
            t = T(f, tp[h], t_vt, pf[b])
            for k in range(2):
                pf[b] = V(lambda e: e.tensor_scalar(HT[:, k, 256 * h:256 * h + 256], PS[:, b, 256 * k:256 * k + 256],
                                                    DN[:, 4 * k + h:4 * k + h + 1], None, ALU.mult), t, t_dn, t_bd)
        t = pf[7]
        for i in range(8):
            k, h = i // 4, i % 4
            t2 = V(lambda e: e.bn_stats(ST8[:, i, :], HT[:, k, 256 * h:256 * h + 256]), t)
        for i in range(8):
            t = V(lambda e: e.bn_aggr(MV8[:, 2 * i:2 * i + 2], ST8[:, i, :]), t2)
        t = rsqrt(R8s, view(MV8[:, 1:2], [2, 8]), LN_EPS, t)
        for i in range(8):
            k, h = i // 4, i % 4
            hv = HT[:, k, 256 * h:256 * h + 256]
            t2 = V(lambda e: e.tensor_scalar(hv, hv, MV8[:, 2 * i:2 * i + 1], R8s[:, i:i + 1], ALU.subtract, ALU.mult),
                   t)
        t_hn = t2
        for c in range(8):
            t_sk = ACTE(lambda e: e.activation(XC[:, c, :], XC[:, c, :], ACT.Copy, scale=pcol(f"ml_skip{l}", c)), t_bd)
        tuc = []

        def conv31(c, on):
            dst = UC[:, c, :]
            t = on(lambda e: e.tensor_scalar(dst, UP[:, c, 0:256], pcol(f"cv_dw_w{l}", c), pcol(f"cv_dw_b{l}", c),
                                             ALU.mult, ALU.add), t_u, t_bd)
            for k in range(1, 31):
                t = on(lambda e: e.scalar_tensor_tensor(dst, UP[:, c, k:k + 256], pcol(f"cv_dw_w{l}", 8 * k + c), dst,
                                                        ALU.mult, ALU.add), t)
            tuc.append(t)
        todo = [0, 1, 2, 3, 4, 5, 6, 7]

        def ev_z(j, p, t):
            for ci in range(2):
                c = 2 * j + ci
                r = ACTE(lambda e: e.activation(R8[:, c, :], p[:, 256 * ci:256 * ci + 256], ACT.Silu,
                                                bias=pcol(f"b_in{l}", 8 + c)), t, K.last["t"])
            conv31(todo.pop(0), V)
            return [r]
        gemm_fm(f"in2{l}", 1024, act, [0, 1], ev_z)
        t_z = K.last["a"]

        def ev(c, p, t, dst):
            t = V(lambda e: e.scalar_tensor_tensor(dst, p, pcol(f"ml_norm_g{l}", c), XC[:, c, :], ALU.mult, ALU.add), t,
                  t_sk)
            return V(lambda e: e.tensor_tensor(dst, dst, R8[:, c, :], ALU.mult), t, t_z)
        act2 = to_fm(HT, X2H, X2L, [2, 3], t_hn, ev)
        YM, YC = QF, R8

        def ev_y(dst, name):
            def evac(j, p, t):
                o = dst[:, 2 * j:2 * j + 2, :]
                s_ = p.rearrange("p (c n) -> p c n", c=2)
                if name is None:
                    r = ACTE(lambda e: e.activation(o, s_, ACT.Copy), t, K.last["v"])
                else:
                    for ci in range(2):
                        r = ACTE(lambda e: e.activation(o[:, ci, :], s_[:, ci, :], ACT.Identity,
                                                        bias=pcol(name, 2 * j + ci)), t, K.last["v"])
                if todo:
                    conv31(todo.pop(0), V)
                return [r]
            return evac
        gemm_fm(f"mld{l}", 1024, act2, [0, 1], ev_y(YM, None))
        t_ym = K.last["a"]
        while todo:
            conv31(todo.pop(0), V)
        UT = ar(14600, 2, 1024)
        for cp in range(4):
            b = 2 + cp % 2
            t = transposes(b, [(PS[:, b, 256 * tt + 128 * ci:256 * tt + 128 * ci + 128],
                                UC[:, 2 * cp + ci, 128 * tt:128 * tt + 128]) for ci in range(2) for tt in range(2)], tuc)
            pf[b] = ACTE(lambda e: e.activation(UT[:, :, 256 * cp:256 * cp + 256], PS[:, b, :].rearrange(
                "p (t n) -> p t n", t=2), ACT.Copy), t)
        t = pf[b]
        for k in range(2):
            t2 = bn(UT[:, k, :], STT[:, k, :], MV[:, k, :], t)
        t = rstd_of(MV[:, :, 1], RS, t2)
        for k in range(2):
            t2 = V(lambda e: e.tensor_scalar(UT[:, k, :], UT[:, k, :], MV[:, k, 0:1], RS[:, k:k + 1], ALU.subtract,
                                             ALU.mult), t)
        t_ut = t2
        GS = UC

        def ev_sig(off, into):
            def evac(j, p, t):
                for ci in range(2):
                    c = 2 * j + ci
                    r = ACTE(lambda e: e.activation(GS[:, c, :], p[:, 256 * ci:256 * ci + 256], ACT.Sigmoid,
                                                    bias=pcol(f"b_in{l}", off + c)), t, t_ut, K.last["v"])
                into(j, r)
                return [r]
            return evac

        def into_ym(j, r):
            o = YM[:, 2 * j:2 * j + 2, :]
            V(lambda e: e.tensor_tensor(o, o, GS[:, 2 * j:2 * j + 2, :], ALU.mult), r, t_ym)
        gemm_fm(f"in2{l}", 1024, act, [0, 1], ev_sig(32, into_ym))
        t_ymg = K.last["v"]

        def ev(c, p, t, dst):
            return ACTE(lambda e: e.activation(dst, p, ACT.Silu, bias=pcol(f"cv_ln_b{l}", c),
                                               scale=pcol(f"cv_ln_g{l}", c)), t, K.last["v"])

        act2 = to_fm(UT, X2H, X2L, [2, 3], t_ut, ev, K.last["t"])

        def into_keep(j, r):
            return None
        gemm_fm(f"in2{l}", 1024, act, [0, 1], ev_sig(40, into_keep))
        t_g5 = K.last["a"]

        def ev_c(j, p, t):
            o = YC[:, 2 * j:2 * j + 2, :]
            for ci in range(2):
                c = 2 * j + ci
                r = ACTE(lambda e: e.activation(YC[:, c, :], p[:, 256 * ci:256 * ci + 256], ACT.Identity,
                                                bias=pcol(f"cv_b_pw{l}", c)), t, K.last["v"])
            ym = YM[:, 2 * j:2 * j + 2, :]
            t3 = V(lambda e: e.tensor_tensor(o, o, GS[:, 2 * j:2 * j + 2, :], ALU.mult), r, t_g5)
            t3 = V(lambda e: e.tensor_tensor(ym, ym, o, ALU.add), t3, t_ymg)
            mer.extend(split_act(ym, X1H[:, 2 * j:2 * j + 2, :], X1L[:, 2 * j:2 * j + 2, :], t3, K.last["t"]))
            return [r]
        mer = []
        gemm_fm(f"cvp{l}", 1024, act2, [0, 1], ev_c)
        t = gemm_tm(f"out2{l}", (X1H, X1L, mer), [4, 5, 6, 7])
        t = add_x([4, 5, 6, 7], t)

        marks = K.fence()
        MEM = ar(4096, 2, 1024)
        XN = ar(2048, 2, 1024)
        for k in range(2):
            tm_ = K.dma("s", d4, MEM[:, k, :], A["mem_2"][0, 128 * k:128 * k + 128, :], marks)
        t = rms(MEM, XN, tm_)
        act2 = to_fm(XN, X2H, X2L, [4, 5, 6, 7], t, by_col(f"norm_mem{l}"))
        KT, VM, QT = ar(6408, 8, 256), ar(8456, 2, 1024), ar(10504, 8, 256)
        P4, PT = ar(12552, 4, 512), ar(14600, 4, 512)
        gemm_fm(f"xk{l}", 1024, act2, [0, 1], ev_y(KT, None))
        t = gemm_tm(f"xv{l}", act2, [4, 5, 6, 7])
        for k in range(2):
            for nb in range(2):
                b = 4 + 2 * k + nb
                pf[b] = ACTE(lambda e: e.activation(VM[:, k, 512 * nb:512 * nb + 512], PS[:, b, :], ACT.Copy), t)
        t_v = pf[7]
        t = rms(X, XN, act2[2])
        act = to_fm(XN, X1H, X1L, [2, 3], t, by_col(f"norm_x{l}"))
        gemm_fm(f"xq{l}", 1024, act, [0, 1], ev_y(QT, None))
        t_q = K.last["a"]
        mx, ng, den = [SMT[:, 8 * i:8 * i + 8] for i in range(3)]
        at_o = []
        for h in range(4):
            b = 4 + h

            def f(e):
                for k in range(2):
                    for c in (2 * h, 2 * h + 1):
                        m = e.matmul(PS[:, b, 256 * k:256 * k + 256], QT[:, c, 128 * k:128 * k + 128], KT[:, c, :],
                                     start=(c == 2 * h), stop=(c == 2 * h + 1))
                return m
            t = T(f, t_q, pf[b])
            t = V(lambda e: e.tensor_reduce(mx[:, 2 * h:2 * h + 2], PS[:, b, :].rearrange("p (k n) -> p k n", k=2), AX,
                                            ALU.max), t)
            t = V(lambda e: e.tensor_scalar(ng[:, 2 * h:2 * h + 2], mx[:, 2 * h:2 * h + 2], -0.0625, None, ALU.mult), t)
            for k in range(2):
                pf[b] = ACTE(lambda e: e.activation(P4[:, h, 256 * k:256 * k + 256], PS[:, b, 256 * k:256 * k + 256],
                                                    ACT.Exp, bias=ng[:, 2 * h + k:2 * h + k + 1], scale=0.0625,
                                                    accum_out=den[:, 2 * h + k:2 * h + k + 1]), t)
            t = V(lambda e: e.reciprocal(den[:, 2 * h:2 * h + 2], den[:, 2 * h:2 * h + 2]), pf[b])
            for k in range(2):
                pv = P4[:, h, 256 * k:256 * k + 256]
                t2 = V(lambda e: e.tensor_scalar(pv, pv, den[:, 2 * h + k:2 * h + k + 1], None, ALU.mult), t)
            at_o.append(t2)
        for h in range(4):
            b = 2 + h % 2
            t = transposes(b, [(PS[:, b, 256 * n_ + 128 * k:256 * n_ + 128 * k + 128],
                                P4[:, h, 256 * k + 128 * n_:256 * k + 128 * n_ + 128])
                               for n_ in range(2) for k in range(2)], at_o[h])
            pf[b] = ACTE(lambda e: e.activation(PT[:, h, :], PS[:, b, :], ACT.Copy), t)
            at_o[h] = pf[b]
        oo = []
        for h in range(4):
            b = 4 + h

            def f(e):
                for dc in range(2):
                    for n_ in range(2):
                        m = e.matmul(PS[:, b, 256 * dc:256 * dc + 256], VM[:, n_, 256 * h + 128 * dc:256 * h + 128 * dc + 128],
                                     PT[:, h, 256 * n_:256 * n_ + 256], start=(n_ == 0), stop=(n_ == 1))
                return m
            t = T(f, at_o[h], t_v, pf[b])
            pf[b] = split_act(PS[:, b, :].rearrange("p (c n) -> p c n", c=2), X2H[:, 2 * h:2 * h + 2, :],
                              X2L[:, 2 * h:2 * h + 2, :], t)
            oo += pf[b]
        t = gemm_tm(f"xo{l}", (X2H, X2L, oo), [4, 5, 6, 7])
        t = add_x([4, 5, 6, 7], t)

        marks = K.fence()
        t = rms(X, XN, marks)
        act = to_fm(XN, X1H, X1L, [2, 3], t, by_col(f"norm_ffn{l}"))
        PD = ar(4096, 2, 4, 258)
        CV = ar(6160, 2, 4, 256)
        tz = G(lambda e: e.memset(PD[:, :, :, 0:2], 0.0), marks)
        cst_ = {"n": 0}

        def conv_evac(p, got):
            n_ = cst_["n"] % 2
            cst_["n"] += 1
            (bg, tg_), (bu, tu) = got
            for q, (b, t) in enumerate(((bg, tg_), (bu, tu))):
                for ci in range(2):
                    c = 22 * q + 2 * p + ci
                    r = ACTE(lambda e: e.activation(PD[:, n_, 2 * q + ci, 2:258], PS[:, b, 256 * ci:256 * ci + 256],
                                                    ACT.Identity, bias=pcol(f"ffn_b_up{l}", c)), t, tz,
                             cst_.get(("cv", n_)))
                pf[b] = r
                for ci in range(2):
                    c = 22 * q + 2 * p + ci
                    s_, dst = PD[:, n_, 2 * q + ci, :], CV[:, n_, 2 * q + ci, :]
                    t = V(lambda e: e.tensor_scalar(dst, s_[:, 0:256], pcol(f"ffn_dw_w{l}", c), pcol(f"ffn_dw_b{l}", c),
                                                    ALU.mult, ALU.add), r, cst_.get(("sp", n_)))
                    for k in (1, 2):
                        t = V(lambda e: e.scalar_tensor_tensor(dst, s_[:, k:k + 256], pcol(f"ffn_dw_w{l}", 44 * k + c),
                                                               dst, ALU.mult, ALU.add), t)
                if q == 0:
                    sg = ACTE(lambda e: e.activation(CV[:, n_, 0:2, :], CV[:, n_, 0:2, :], ACT.Silu), t)
            cst_[("cv", n_)] = t
            hv = CV[:, n_, 2:4, :]
            t = V(lambda e: e.tensor_tensor(hv, hv, CV[:, n_, 0:2, :], ALU.mult), t, sg)
            cst_[("sp", n_)] = t
            return hv.rearrange("p c n -> p (c n)"), t
        t = ffn(f"ff2{l}", 11, act, conv_evac, True, True)
        t = add_x([4, 5, 6, 7], t)

    ROWS = ar(9992, 512).rearrange("p (a n) -> p a n", a=2)

    layer1(0)
    layer1(1)
    t_small = load_small()
    layer2(0, t_small)
    layer2(1, t_small)
    marks = K.fence()
    FN = ar(4096, 1024)
    XN = ar(2048, 2, 1024)
    tf = K.dma("s", d4, FN, AP(A["final_norm_2"].tensor, A["final_norm_2"].offset, [[0, 128], [1, D]]), marks)
    t = rms(X, XN, marks)
    for k in range(2):
        t = V(lambda e: e.tensor_tensor(XN[:, k, :], XN[:, k, :], FN, ALU.mult), t, tf)
    finish(K, out, XN)


def finish(K, out, X):
    d = K.new("out")
    marks = K.fence()
    for k in range(2):
        t = K.dma("s", d, out[0, 128 * k:128 * k + 128, :], X[:, k, :], marks)
    K.wait("s", [t])


_INS = ["x", "c", "positions", "rel_bias", "w_ada", "b_ada", "w_in", "w_out", "conv_w", "conv_b", "dt_bias", "a_log",
        "d_skip", "ssd_norm_w", "sinks", "ln_g", "ln_b", "ffn_w_gate", "ffn_w_up", "ffn_w_down", "router_w",
        "router_b", "expert_w_gate", "expert_w_up", "expert_w_down", "mem_2", "norm_mix_2", "w_in_2", "b_in_2",
        "ml_conv_w_2", "ml_conv_b_2", "ml_wq_2", "ml_wk_2", "ml_wv_2", "ml_w_gate_2", "ml_b_gate_2", "ml_norm_g_2",
        "ml_skip_2", "ml_w_down_2", "cv_dw_w_2", "cv_dw_b_2", "cv_ln_g_2", "cv_ln_b_2", "cv_w_pw_2", "cv_b_pw_2",
        "w_out_2", "norm_x_2", "norm_mem_2", "xa_wq_2", "xa_wk_2", "xa_wv_2", "xa_wo_2", "norm_ffn_2", "ffn_w_up_2",
        "ffn_b_up_2", "ffn_dw_w_2", "ffn_dw_b_2", "ffn_w_down_2", "final_norm_2"]


def kernel(**inputs):
    import concourse.bacc as _bacc
    from concourse.bass_utils import run_bass_kernel_spmd as _run

    nc = _bacc.Bacc("TRN2", target_bir_lowering=False, num_devices=1)
    arrays, A = {}, {}
    for name in _INS:
        a = np.ascontiguousarray(inputs[name])
        arrays[f"in_{name}_dram"] = a
        A[name] = nc.dram_tensor(f"in_{name}_dram", a.shape, mybir.dt.from_np(a.dtype), kind="ExternalInput").ap()
    a = constants()
    arrays["in_cst_dram"] = a
    A["cst"] = nc.dram_tensor("in_cst_dram", a.shape, mybir.dt.float32, kind="ExternalInput").ap()
    out = nc.dram_tensor("out_0_dram", (1, S, D), mybir.dt.float32, kind="ExternalOutput").ap()
    build_program(nc, A, out)
    r = _run(nc, [arrays], core_ids=[0])
    return r.results[0]["out_0_dram"]
```

```python
import math

import numpy as np
import concourse.bass as bass
from concourse import mybir
from contextlib import ExitStack

F32 = mybir.dt.float32
F32R = mybir.dt.float32r
I32 = mybir.dt.int32
ACT = mybir.ActivationFunctionType
ALU = mybir.AluOpType
AX = mybir.AxisListType.X
AP = bass.AP

D = 1024
S = 256
D_FF = 2816
NEXP = 8
D_EXP = 3584
ALPHA = 4.0 ** 0.25
LN_EPS = 1e-5
RMS_EPS = 1e-6
NEG = -1.0e30
NRAW = 4
NH = 3
USZ = 2048
ARENA = 16680

C_ID, C_ONE, C_TRI, C_NEG, C_SW = 0, 128, 256, 384, 640
C_DEC, C_INV, C_BD, C_LOW, C_IOT, C_HOT = 768, 1792, 1824, 1856, 1920, 2048
C_N = 2048 + 384


def constants():
    c = np.zeros((128, C_N), np.float64)
    p = np.arange(128)
    c[:, C_ID:C_ID + 128] = np.eye(128)
    c[:, C_ONE:C_ONE + 128] = 1.0
    c[:, C_TRI:C_TRI + 128] = p[None, :] >= p[:, None]
    c[:, C_NEG:C_NEG + 128] = np.where(p[None, :] >= p[:, None], 0.0, NEG)
    c[:, C_SW:C_SW + 128] = np.roll(np.eye(128), 64, axis=1)
    l = np.arange(256)
    diff = l[None, :] - p[:, None]
    for h in range(4):
        lg = np.log1p(-2.0 ** (-5.0 - h))
        c[:, C_DEC + 256 * h:C_DEC + 256 * h + 256] = np.where(diff >= 0, np.exp(lg * np.maximum(diff, 0)), 0.0) * 0.125
    half = 32
    c[:, C_INV:C_INV + 32] = np.exp(np.float32(-math.log(10000.0)) * np.arange(half, dtype=np.float32) / np.float32(half))
    c[:, C_BD:C_BD + 32] = np.arange(32)[None, :] == (p[:, None] // 4)
    e = np.arange(8)
    c[:, C_LOW:C_LOW + 64] = (e[None, :] < e[:, None]).reshape(-1)
    c[:, C_IOT:C_IOT + 128] = p[None, :]
    dist = 255 - np.arange(384)
    ok = (dist >= 0) & (dist < 128)
    dc = np.clip(dist, 1, 127).astype(np.float32)
    large = 16 + (np.log(dc / np.float32(16)) / np.float32(math.log(8.0)) * np.float32(16)).astype(np.int32)
    bucket = np.where(dist < 16, np.maximum(dist, 0), np.minimum(large, 31))
    for b in range(32):
        c[b, C_HOT:C_HOT + 384] = ok & (bucket == b)
    c[32, C_HOT:C_HOT + 384] = np.where(ok, 0.0, NEG)
    return c.astype(np.float32)


def param_rows(A):
    two = lambda nm: (nm + "0", nm + "1")
    rows = [(("c",), 8, A["c"].rearrange("a (r q) -> (a r) q", q=128))]
    for nm, r, key in (("b_ada", 48, "b_ada"), ("conv_b", 6, "conv_b"), ("ssd_norm", 4, "ssd_norm_w"),
                       ("norm_mix", 8, "norm_mix_2"), ("b_in", 48, "b_in_2"), ("ml_conv_b", 8, "ml_conv_b_2"),
                       ("ml_norm_g", 8, "ml_norm_g_2"), ("ml_skip", 8, "ml_skip_2"), ("cv_dw_b", 8, "cv_dw_b_2"),
                       ("cv_ln_g", 8, "cv_ln_g_2"), ("cv_ln_b", 8, "cv_ln_b_2"), ("cv_b_pw", 8, "cv_b_pw_2"),
                       ("norm_x", 8, "norm_x_2"), ("norm_mem", 8, "norm_mem_2"), ("norm_ffn", 8, "norm_ffn_2"),
                       ("ffn_b_up", 44, "ffn_b_up_2"), ("ffn_dw_b", 44, "ffn_dw_b_2")):
        rows.append((two(nm), r, A[key].rearrange("l (r q) -> (l r) q", q=128)))
    for nm, r, key in (("conv_w", 24, "conv_w"), ("ml_conv_w", 32, "ml_conv_w_2"), ("cv_dw_w", 248, "cv_dw_w_2"),
                       ("ffn_dw_w", 132, "ffn_dw_w_2")):
        rows.append((two(nm), r, A[key].rearrange("l k (r q) -> (l k r) q", q=128)))
    return rows



def u_fm(w, n0, n1, key):
    return [(key, w[:, n:min(n + 256, n1)].rearrange("(c p) n -> p c n", p=128)) for n in range(n0, n1, 256)]


def u_tm(w, k0, k1, key):
    return [(key, w[128 * k:128 * (k + 2), :].rearrange("(c p) n -> p c n", p=128)) for k in range(k0, k1, 2)]


def u_blk(w, n0, n1, key, kc=4):
    return [(key, w[128 * k:128 * (k + kc), n0:n1].rearrange("(c p) n -> p c n", p=128)) for k in range(0, 8, kc)]


def u_ffn(wg, wu, wd, n_pairs, up0, key):
    out = []
    for p in range(n_pairs + 1):
        if p < n_pairs:
            out += u_fm(wg, 256 * p, 256 * p + 256, key + "g")
            out += u_fm(wu, up0 + 256 * p, up0 + 256 * p + 256, key + "u")
        if p > 0:
            out += u_tm(wd, 2 * p - 2, 2 * p, key + "d")
    return out


def u_moe(wg, wu, wd):
    out = []
    for b in range(8):
        if b < 7:
            out += u_blk(wg, 512 * b, 512 * b + 512, "mg") + u_blk(wu, 512 * b, 512 * b + 512, "mu")
        if b > 0:
            out += u_tm(wd, 4 * b - 4, 4 * b, "md")
    return out


def stream_plan(A):
    out = []
    for l in range(2):
        w = A["w_in"][l]
        for n in (0, 512, 1024):
            out += u_blk(w, n, n + 512, f"in{l}")
        out += u_fm(w, 1536, 2304, f"in{l}") + u_fm(w, 2312, 2568, f"in{l}") + u_fm(w, 2568, 2696, f"in{l}")
        out += u_fm(w, 2696, 2824, f"in{l}") + u_fm(w, 2304, 2312, f"in{l}")
        out += u_tm(A["w_out"][l], 0, 8, f"out{l}")
        if l == 0:
            out += u_ffn(A["ffn_w_gate"][0], A["ffn_w_up"][0], A["ffn_w_down"][0], 11, 0, "ffn")
        else:
            for e in range(NEXP):
                out += u_moe(A["expert_w_gate"][0, e], A["expert_w_up"][0, e], A["expert_w_down"][0, e])
    for l in range(2):
        w = A["w_in_2"][l]
        for n in (0, 2048, 3072, 1024):
            out += u_fm(w, n, n + 1024, f"in2{l}")
        out += u_fm(A["ml_w_down_2"][l], 0, 1024, f"mld{l}")
        for n in (4096, 5120):
            out += u_fm(w, n, n + 1024, f"in2{l}")
        out += u_fm(A["xa_wk_2"][l], 0, 1024, f"xk{l}")
        out += u_tm(A["xa_wv_2"][l], 0, 8, f"xv{l}")
        out += u_fm(A["cv_w_pw_2"][l], 0, 1024, f"cvp{l}")
        out += u_tm(A["w_out_2"][l], 0, 8, f"out2{l}")
        out += u_fm(A["xa_wq_2"][l], 0, 1024, f"xq{l}")
        out += u_tm(A["xa_wo_2"][l], 0, 8, f"xo{l}")
        out += u_ffn(A["ffn_w_up_2"][l], A["ffn_w_up_2"][l], A["ffn_w_down_2"][l], 11, D_FF, f"ff2{l}")
    return out


class Core:

    def __init__(self, nc, ctx, tag="", only=None, sems=None):
        self.nc, self.ctx, self.only, self.tag = nc, ctx, only, tag
        self.engines = {"v": nc.vector, "a": nc.scalar, "g": nc.gpsimd, "t": nc.tensor, "s": nc.sync}
        self.sems = {e: self.sem("s_" + tag + e) for e in "vagt"} if sems is None else sems
        self.count = {}
        self.seen = {e: {} for e in self.engines}
        self.last = {}

    def sem(self, name):
        return self.ctx.enter_context(self.nc.semaphore(name))

    def new(self, name):
        if name not in self.sems:
            self.sems[name] = self.sem("d_" + name)
        return name

    def wait(self, eng, deps):
        for d in deps:
            if d is None:
                continue
            if isinstance(d, list):
                self.wait(eng, d)
                continue
            k, n = d
            if self.seen[eng].get(k, 0) < n:
                if self.only in (None, eng):
                    self.engines[eng].wait_ge(self.sems[k], n)
                self.seen[eng][k] = n

    def op(self, eng, f, deps):
        self.wait(eng, deps)
        self.count[eng] = self.count.get(eng, 0) + 1
        if self.only in (None, eng):
            f(self.engines[eng]).then_inc(self.sems[eng], 1)
        self.last[eng] = (eng, self.count[eng])
        return self.last[eng]

    def V(self, f, *deps):
        return self.op("v", f, deps)

    def A(self, f, *deps):
        return self.op("a", f, deps)

    def G(self, f, *deps):
        return self.op("g", f, deps)

    def T(self, f, *deps):
        return self.op("t", f, deps)

    def dma(self, eng, sem, out, in_, *deps):
        self.wait(eng, deps)
        if self.only in (None, eng):
            self.engines[eng].dma_start(out, in_).then_inc(self.sems[sem], 16)
        self.count[sem] = self.count.get(sem, 0) + 16
        return (sem, self.count[sem])

    def fence(self):
        marks = [self.last[e] for e in self.last]
        for e in "vagt":
            self.wait(e, marks)
        return marks


def view(ap, *dims):
    return AP(ap.tensor, ap.offset, [list(ap.ap[0])] + [list(d) for d in dims])


def build_program(nc, A, out):
    with ExitStack() as ctx:
        emit_program(nc, ctx, A, out)


def emit_program(nc, ctx, A, out):
    K = Core(nc, ctx)
    V, ACTE, G, T = K.V, K.A, K.G, K.T

    def sb(name, shape, dt=F32):
        return ctx.enter_context(nc.sbuf_tensor(name, shape, dt))

    RAW = sb("RAW", [128, NRAW, USZ])
    HI = sb("HI", [128, NH, USZ], F32R)
    LO = sb("LO", [128, NH, USZ], F32R)
    X1H, X1L = sb("X1H", [128, 8, 256], F32R), sb("X1L", [128, 8, 256], F32R)
    X2H, X2L = sb("X2H", [128, 8, 256], F32R), sb("X2L", [128, 8, 256], F32R)
    X = sb("X", [128, 2, D])
    CST = sb("CST", [128, C_HOT])
    PC = sb("PC", [128, 12 * 128])
    AR = sb("AR", [128, ARENA])
    MOD = sb("MOD", [128, 2, 48])
    BT = sb("BT", [128, 4, 256])
    SM = sb("SM", [128, 640])
    PS = ctx.enter_context(nc.psum_tensor("PS", [128, 8, 512], F32))

    ident = CST[:, C_ID:C_ID + 128]
    ones = CST[:, C_ONE:C_ONE + 128]
    tri = CST[:, C_TRI:C_TRI + 128]
    negm = CST[:, C_NEG:C_NEG + 256]
    swap = CST[:, C_SW:C_SW + 128]

    def ar(off, *shape):
        n = int(np.prod(shape))
        assert off + n <= ARENA, (off, shape)
        a = AR[:, off:off + n]
        if len(shape) == 2:
            a = a.rearrange("p (a b) -> p a b", a=shape[0])
        if len(shape) == 3:
            a = a.rearrange("p (a b c) -> p a b c", a=shape[0], b=shape[1])
        return a

    sm_at = [0]

    def sm(*shape):
        n = int(np.prod(shape))
        o = sm_at[0]
        sm_at[0] += n
        assert sm_at[0] <= 640
        a = SM[:, o:o + n]
        if len(shape) == 2:
            a = a.rearrange("p (a b) -> p a b", a=shape[0])
        if len(shape) == 3:
            a = a.rearrange("p (a b c) -> p a b c", a=shape[0], b=shape[1])
        return a

    plan = stream_plan(A)
    raw_sem = [K.new(f"raw{i}") for i in range(NRAW + 3)]
    ring, slot_of, before, held = list(range(NRAW)), [], [], {}
    for i, u in enumerate(plan):
        if u[0][0] == "m" and u[0][1] in "gud" and len(u[0]) == 2:
            if len(ring) == NRAW:
                ring += [NRAW, NRAW + 1, NRAW + 2]
        elif len(ring) > NRAW:
            ring = [r for r in ring if r < NRAW]
        slot_of.append(ring[0])
        ring.append(ring.pop(0))
        before.append(held.get(slot_of[i]))
        held[slot_of[i]] = i
    raw_free = {}
    hl_free = [None] * NH
    landed, split_of = {}, {}
    st = {"dma": 0, "split": 0, "next": 0, "open": 0, "aux": 6, "rate": 1, "more": None}
    hslot = {}
    n_split = [0]
    lo_pool = [4, 8]

    def uview(tile, slot, a):
        return tile[:, slot, 0:a.shape[1] * a.shape[2]].rearrange("p (c n) -> p c n", c=a.shape[1])

    def raw_at(i):
        n = plan[i][1].shape[1] * plan[i][1].shape[2]
        if slot_of[i] < NRAW:
            return RAW[:, slot_of[i], 0:n]
        o = 2048 * (slot_of[i] - NRAW)
        return AR[:, o:o + n]

    def issue_dma():
        while st["dma"] < len(plan):
            i = st["dma"]
            s, b = slot_of[i], before[i]
            if b is not None and b not in raw_free or s >= NRAW and st["more"] is None:
                return
            landed[i] = K.dma("s", raw_sem[s], raw_at(i).rearrange("p (c n) -> p c n", c=plan[i][1].shape[1]),
                              plan[i][1], raw_free.get(b), st["more"] if s >= NRAW else None)
            st["dma"] += 1

    def pump():
        while st["split"] < st["dma"]:
            i = st["split"]
            if st["open"] == NH:
                return
            st["split"] += 1
            st["open"] += 1
            h = n_split[0] % NH
            n_split[0] += 1
            n = plan[i][1].shape[1] * plan[i][1].shape[2]
            hslot[i] = h
            r, hi, lo = raw_at(i), HI[:, h, 0:n], LO[:, h, 0:n]
            t1 = ACTE(lambda e: e.activation(hi, r, ACT.Copy), landed[i], hl_free[h])
            m = n * lo_pool[0] // lo_pool[1]
            t2 = V(lambda e: e.tensor_tensor(lo[:, m:], r[:, m:], hi[:, m:].bitcast(F32), ALU.subtract), t1, landed[i],
                   hl_free[h])
            t3 = G(lambda e: e.tensor_tensor(lo[:, 0:m], r[:, 0:m], hi[:, 0:m].bitcast(F32), ALU.subtract), t1,
                   landed[i], hl_free[h])
            split_of[i] = raw_free[i] = [t1, t2, t3]
            issue_dma()

    def take(key):
        i = st["next"]
        assert plan[i][0] == key, (plan[i][0], key)
        st["next"] += 1
        a = plan[i][1]
        return i, uview(HI, hslot[i], a), uview(LO, hslot[i], a), split_of[i]

    def done(i, tok):
        hl_free[hslot[i]] = tok
        st["open"] -= 1
        pump()
        for _ in range(min(len(side), st["rate"])):
            side.pop(0)()

    side = []

    ada_sem = [K.new(f"ada{i}") for i in range(4)]
    ada_todo, ada_out = [], []

    def ada_issue(s, slot, dep):
        if ada_todo:
            l, b, k = ada_todo.pop(0)
            tok = K.dma("s", ada_sem[s], slot, A["w_ada"][l][128 * k:128 * k + 128, 2048 * b:2048 * b + 2048], dep)
            ada_out.append((s, slot, tok))

    def ada_run(blocks, slots, accs, deps):
        acc_free = [deps for _ in accs]
        wrote = [None for _ in accs]

        def step(k, j):
            acc = accs[j]
            s, slot, got = ada_out.pop(0)
            if k == 0:
                t = V(lambda e: e.tensor_scalar(acc, slot, pcol("c", 0), None, ALU.mult), got, t_pc, acc_free[j])
            else:
                t = V(lambda e: e.scalar_tensor_tensor(acc, slot, pcol("c", k), acc, ALU.mult, ALU.add), got, wrote[j])
            wrote[j] = t
            ada_issue(s, slot, t)
            return t

        def last(k, j, l, b):
            t = step(k, j)
            side.insert(0, lambda: acc_free.__setitem__(j, ada_sum(l, b, accs[j], t)))
        ada_todo.extend((l, b, k) for l, b in blocks for k in range(8))
        for s, slot in enumerate(slots):
            ada_issue(s, slot, deps)
        for n, (l, b) in enumerate(blocks):
            j = n % len(accs)
            side.extend([lambda k=k, j=j: step(k, j) for k in range(7)])
            side.append(lambda j=j, l=l, b=b: last(7, j, l, b))

    def ada_sum(l, b, acc, t0):
        for q in range(4):
            bk = st["aux"] + q % 2
            t = transposes(bk, [(PS[:, bk, 128 * j:128 * j + 128], acc[:, 512 * q + 128 * j:512 * q + 128 * j + 128])
                                for j in range(4)], t0)
            free = t
            o = MOD[:, l, 16 * b + 4 * q:16 * b + 4 * q + 4]
            pf[bk] = V(lambda e: e.tensor_reduce(o, PS[:, bk, :].rearrange("p (a n) -> p a n", a=4), AX, ALU.add), t)
        o = MOD[:, l, 16 * b:16 * b + 16]
        t = V(lambda e: e.tensor_tensor(o, o, pcols(f"b_ada{l}", 16, 16 * b), ALU.add), pf[bk])
        for q in (8, 16, 32, 40):
            if 16 * b <= q < 16 * b + 16:
                t = V(lambda e: e.tensor_scalar(MOD[:, l, q:q + 8], MOD[:, l, q:q + 8], 1.0, None, ALU.add), t)
        st["mod"] = t
        return free

    pf = [None] * 8

    def mm3(e, o, lh, ll, rh, rl, first, last, skip=False):
        e.matmul(o, lh, rh, start=first, stop=False, skip_group_check=skip)
        e.matmul(o, lh, rl, start=False, stop=False, skip_group_check=skip)
        return e.matmul(o, ll, rh, start=False, stop=last, skip_group_check=skip)

    def gemm_fm(key, ncols, act, banks, evac):
        XH, XL, ready = act
        for j, n0 in enumerate(range(0, ncols, 256)):
            w = min(256, ncols - n0)
            m, nbs = min(w, 128), max(1, w // 128)
            b = banks[j % len(banks)]
            i, hi, lo, got = take(key)

            def part(e, nb, kcs):
                c, o = slice(m * nb, m * nb + m), PS[0:m, b, 256 * nb:256 * nb + 256]
                return [mm3(e, o, hi[:, kc, c], lo[:, kc, c], XH[:, kc, :], XL[:, kc, :], kc == 0, kc == 7)
                        for kc in kcs][-1]
            t = as_they_come(j, nbs, part, ready, got, pf[b])
            pf[b] = evac(j, PS[0:m, b, 0:256 * nbs], t)
            done(i, t)

    def as_they_come(j, nbs, part, ready, *deps):
        first = j == 0 and len(ready) == 8
        if first:
            for q in range(4):
                t = T(lambda e: part(e, 0, (2 * q, 2 * q + 1)), *deps, ready[2 * q:2 * q + 2])
        if first and nbs == 1:
            return t
        return T(lambda e: [part(e, nb, range(8)) for nb in range(1 if first else 0, nbs)][-1], *deps, ready)

    def mm_down(e, hi, lo, LH, LL, banks, kcs, first, last):
        for c in range(kcs):
            for t in range(2):
                for nb in range(2):
                    o = PS[:, banks[2 * t + nb], :]
                    ts, ns = slice(128 * t, 128 * t + 128), slice(512 * nb, 512 * nb + 512)
                    m = mm3(e, o, LH(c)[:, ts], LL(c)[:, ts], hi[:, c, ns], lo[:, c, ns],
                            first and c == 0, last and c == kcs - 1)
        return m

    def gemm_tm(key, act, banks):
        XH, XL, ready = act
        for j in range(4):
            i, hi, lo, got = take(key)
            t = T(lambda e: mm3_tm(e, hi, lo, XH, XL, 2 * j, banks), got, ready[:2 * j + 2], [pf[b] for b in banks])
            done(i, t)
        return t

    def mm3_tm(e, hi, lo, XH, XL, k0, banks):
        return mm_down(e, hi, lo, lambda c: XH[:, k0 + c, :], lambda c: XL[:, k0 + c, :], banks, 2, k0 == 0, k0 == 6)

    def gemm_blk(key, act, banks, width, kc):
        XH, XL, ready = act
        for k0 in range(0, 8, kc):
            i, hi, lo, got = take(key)

            def f(e):
                for c in range(kc):
                    for t in range(2):
                        ts = slice(128 * t, 128 * t + 128)
                        m = mm3(e, PS[:, banks[t], 0:width], XH[:, k0 + c, ts], XL[:, k0 + c, ts], hi[:, c, :],
                                lo[:, c, :], k0 + c == 0, k0 + c == 7)
                return m
            t = T(f, got, ready[:k0 + kc], [pf[b] for b in banks])
            done(i, t)
        return t

    def split_act(src, H, L, *deps):
        t1 = ACTE(lambda e: e.activation(H, src, ACT.Copy), *deps)
        t2 = V(lambda e: e.tensor_tensor(L, src, H.bitcast(F32), ALU.subtract), t1, *deps)
        return [t1, t2]

    def transposes(dst_bank, parts, *deps):
        def f(e):
            for d, s_ in parts:
                n = s_.shape[0]
                m = e.transpose(d, s_, ident[0:n, 0:n])
            return m
        return T(f, pf[dst_bank], *deps)

    def to_fm(src, H, L, banks, deps, evac=None, prev=None):
        ready = []
        for cp in range(4):
            b = banks[cp % len(banks)]
            t = transposes(b, [(PS[:, b, 256 * ci + 128 * tt:256 * ci + 128 * tt + 128],
                                src[:, tt, 128 * (2 * cp + ci):128 * (2 * cp + ci) + 128])
                               for ci in range(2) for tt in range(2)], deps)
            p = PS[:, b, :].rearrange("p (c n) -> p c n", c=2)
            hs = (H[:, 2 * cp:2 * cp + 2, :], L[:, 2 * cp:2 * cp + 2, :])
            if evac is None:
                r = split_act(p, hs[0], hs[1], t, prev)
                pf[b] = r
            else:
                te = [evac(2 * cp + ci, p[:, ci, :], t, XF[:, 2 * cp + ci, :]) for ci in range(2)]
                pf[b] = te
                r = split_act(XF[:, 2 * cp:2 * cp + 2, :], hs[0], hs[1], te, prev)
            ready += r
        return (H, L, ready)

    XF = ar(0, 8, 256)

    def pcol(name, i=0):
        o = pc_at[name] + i
        return PC[:, o:o + 1]

    def pcols(name, n, i=0):
        o = pc_at[name] + i
        return PC[:, o:o + n]

    def rsqrt(dst, src, eps, *deps):
        t = V(lambda e: e.tensor_scalar(dst, src, eps, None, ALU.add), *deps)
        t = ACTE(lambda e: e.activation(dst, dst, ACT.Ln), t)
        return ACTE(lambda e: e.activation(dst, dst, ACT.Exp, scale=-0.5), t)

    def rstd_of(mv, rs, *deps):
        return rsqrt(rs, mv, LN_EPS, *deps)

    def bn(src, stats, mv, *deps):
        n = src.shape[1]
        k = max(1, n // 512)
        t = None
        for i in range(k):
            t = V(lambda e: e.bn_stats(stats[:, 6 * i:6 * i + 6], src[:, i * (n // k):(i + 1) * (n // k)]), *deps)
        return V(lambda e: e.bn_aggr(mv, stats[:, 0:6 * k]), t)

    STT = sm(2, 12)
    MV = sm(2, 2)
    RS = sm(2)
    dtb, alog, dsk = sm(2, 8), sm(2, 8), sm(2, 8)
    snk, rbias, mbg = sm(2, 4), sm(8), sm(2, 8)
    pos_i = SM[:, sm_at[0]:sm_at[0] + 2].bitcast(I32)
    sm(2)
    posf = sm(2)
    COS, SIN = sm(2, 32), sm(2, 32)
    relb = sm(4)

    d0 = K.new("cst")
    d1 = K.new("par")
    d6 = K.new("par0")
    d2 = K.new("xin")
    d3 = K.new("bt")
    d4 = K.new("ln")
    d5 = K.new("misc")
    rows = param_rows(A)
    PR = ar(0, 12, 128)
    HOT = ar(6144, 384)
    pc_at = {}
    at = 0
    n = 0
    for names, r, src in rows:
        for i, name in enumerate(names):
            pc_at[name] = at + i * r
        r *= len(names)
        o = 0
        while o < r:
            k = min(r - o, 128 - (at + o) % 128)
            K.dma("a", d6 if at + o < 128 else d1, PR[(at + o) % 128:(at + o) % 128 + k, (at + o) // 128, :], src[o:o + k, :])
            o += k
            n += 1
        at += r
        if names[0] == "c":
            K.dma("s", d0, CST[:, :], A["cst"][:, 0:C_HOT])
            K.dma("s", d0, HOT, A["cst"][:, C_HOT:C_N])
            ada_run([(0, 0)], [ar(8192 + 2048 * i, 2048) for i in range(4)], [ar(2304, 2048)], None)
    n_pr = -(-at // 128)
    assert n_pr <= 12
    last_rows = at - 128 * (n_pr - 1)
    for k in range(2):
        K.dma("a", d2, X[:, k, :], A["x"][0, 128 * k:128 * k + 128, :])
        K.dma("s", d2, pos_i[:, k:k + 1], A["positions"][0, 128 * k:128 * k + 128].rearrange("(p a) -> p a", a=1))
    for dst, src, cnt in ((dtb, A["dt_bias"], 16), (alog, A["a_log"], 16), (dsk, A["d_skip"], 16), (snk, A["sinks"], 8),
                          (rbias, A["router_b"], 8), (mbg, A["ml_b_gate_2"], 16)):
        flat = view(dst, [1, cnt])
        K.dma("s", d2, flat, AP(src.tensor, src.offset, [[0, 128], [1, cnt]]))
    V(lambda e: e.memset(relb[0:64, :], 1.0))
    K.dma("a", d2, relb[0:32, :], A["rel_bias"], K.last["v"])
    WR = sb("WR", [128, 8, 8])
    K.dma("a", d5, WR[:, :, :], A["router_w"][0].rearrange("(c p) n -> p c n", p=128))
    cst, par0, par, xin, misc = [(d, K.count[d]) for d in (d0, d6, d1, d2, d5)]
    for e in "vagt":
        K.wait(e, [cst, par0])

    def turn_params(i):
        b = i % 4
        r = 128 if i < n_pr - 1 else last_rows
        t = transposes(b, [(PS[:, b, 0:r], PR[0:r, i, :])])
        pf[b] = V(lambda e: e.tensor_copy(PC[:, 128 * i:128 * i + r], PS[:, b, 0:r]), t)
        return pf[b]
    t_pc = turn_params(0)

    while side:
        side.pop(0)()
    issue_dma()
    pump()
    for e in "vagt":
        K.wait(e, [par, xin, misc])
    for i in range(1, n_pr):
        turn_params(i)

    ang = ar(2048, 2, 32)
    kk = ar(2112, 2, 32)
    t = V(lambda e: e.tensor_copy(posf, pos_i))
    for k in range(2):
        t2 = V(lambda e: e.tensor_scalar(ang[:, k, :], CST[:, C_INV:C_INV + 32], posf[:, k:k + 1], None, ALU.mult), t)
    MAGIC = 12582912.0
    t = V(lambda e: e.tensor_scalar(kk, ang, 1.0 / (2 * math.pi), MAGIC, ALU.mult, ALU.add), t2)
    t = V(lambda e: e.tensor_scalar(kk, kk, MAGIC, None, ALU.subtract), t)
    c1 = 6.28125
    c2 = float((np.array([2 * math.pi - c1], np.float32).view(np.uint32) & np.uint32(0xFFFFF000)).view(np.float32)[0])
    c3 = 2 * math.pi - c1 - c2
    for cc in (c1, c2, c3):
        t = V(lambda e: e.scalar_tensor_tensor(ang, kk, -cc, ang, ALU.mult, ALU.add), t)
    t = V(lambda e: e.tensor_scalar(ang, ang, math.pi, -math.pi, ALU.min, ALU.max), t)
    t1 = ACTE(lambda e: e.activation(SIN, ang, ACT.Sin), t)
    t2 = ACTE(lambda e: e.activation(COS, ang, ACT.Sin, scale=0.5), t)
    t = V(lambda e: e.tensor_tensor(COS, COS, COS, ALU.mult), t2)
    t_rot = [t1, V(lambda e: e.tensor_scalar(COS, COS, -2.0, 1.0, ALU.mult, ALU.add), t)]

    RB = ar(4352, 4, 384)
    scr = nc.dram_tensor("scr_bias", [4, 128, 384], F32)
    for h in range(4):
        b = 4 + h
        lhs = view(relb[0:33, h:h + 1], [0, 128])
        t = T(lambda e: e.matmul(PS[:, b, 0:384], lhs, HOT[0:33, :], start=True, stop=True), pf[b])
        t = ACTE(lambda e: e.activation(RB[:, h, :], PS[:, b, 0:384], ACT.Copy), t)
        pf[b] = t
    tb = K.dma("a", d3, scr[:].rearrange("h p n -> p h n"), RB, t)
    scr0 = scr[0, 0:1, 0:1]
    for h in range(4):
        tb2 = K.dma("a", d3, BT[:, h, :], AP(scr0.tensor, h * 128 * 384 + 127, [[383, 128], [1, 256]]), tb)
    t_bt = tb2

    marks = K.fence()

    def modc(l, part, c):
        return MOD[:, l, 8 * part + c:8 * part + c + 1]

    def scaled(scale, bias):
        def evac(c, p, t, dst):
            return V(lambda e: e.tensor_scalar(dst, p, scale(c), bias(c) if bias else None, ALU.mult,
                                               ALU.add if bias else ALU.bypass), t)
        return evac

    LNR = ar(2048, 2, 1024)
    GB = ar(4096, 1024)
    DG = ar(5120, 8, 128)

    def rows_of(l, part, dst, banks=(0, 1)):
        for c in range(8):
            t = V(lambda e: e.tensor_scalar(DG[:, c, :], ident, modc(l, part, c), None, ALU.mult), K.last["t"], st["mod"])
        for h in range(2):
            b = banks[h]
            t2 = T(lambda e: [e.matmul(PS[:, b, 128 * c:128 * c + 128], ones, DG[:, 4 * h + c, :], start=True, stop=True)
                              for c in range(4)][-1], t, pf[b])
            pf[b] = ACTE(lambda e: e.activation(dst[:, 512 * h:512 * h + 512], PS[:, b, :], ACT.Copy), t2)
        return [pf[banks[0]], pf[banks[1]]]

    def residual(l, j, banks, tok, src=None):
        part = 2 if j == 0 else 5
        tl = K.dma("s", d4, LNR[:, 0, :], AP(A["ln_g"].tensor, A["ln_g"].offset + (2 * l + j) * D, [[0, 128], [1, D]]),
                   K.last["t"], K.last["v"], K.last["a"], K.last["g"])
        tl = K.dma("s", d4, LNR[:, 1, :], AP(A["ln_b"].tensor, A["ln_b"].offset + (2 * l + j) * D, [[0, 128], [1, D]]))
        tg = rows_of(l, part, GB)
        TT = ar(0, 2, 1024)
        for k in range(2):
            for nb in range(2):
                ns = slice(512 * nb, 512 * nb + 512)
                y = src[:, k, ns] if src is not None else PS[:, banks[2 * k + nb], :]
                t = V(lambda e: e.tensor_tensor(TT[:, k, ns], y, GB[:, ns], ALU.mult), tok, tg)
                if src is None:
                    pf[banks[2 * k + nb]] = t
            t = V(lambda e: e.scalar_tensor_tensor(X[:, k, :], X[:, k, :], ALPHA, TT[:, k, :], ALU.mult, ALU.add),
                  K.last["v"], K.last["t"])
            t = bn(X[:, k, :], STT[:, k, :], MV[:, k, :], t)
        t = rstd_of(MV[:, :, 1], RS, t)
        for k in range(2):
            t1 = V(lambda e: e.tensor_scalar(X[:, k, :], X[:, k, :], MV[:, k, 0:1], RS[:, k:k + 1], ALU.subtract,
                                             ALU.mult), t)
            t1 = V(lambda e: e.tensor_tensor(X[:, k, :], X[:, k, :], LNR[:, 0, :], ALU.mult), t1, tl)
            t1 = V(lambda e: e.tensor_tensor(X[:, k, :], X[:, k, :], LNR[:, 1, :], ALU.add), t1)
        return t1

    def ffn(key, n_pairs, act, evac_h, first, last):
        ring = {}
        prev = [None]
        RH = X2H[:, :, :].rearrange("p a b -> p (a b)").rearrange("p (s c n) -> p s c n", s=4, c=2)
        RL = X2L[:, :, :].rearrange("p a b -> p (a b)").rearrange("p (s c n) -> p s c n", s=4, c=2)
        XH, XL, ready = act
        for p in range(n_pairs + 1):
            st["aux"] = 2 * ((p + 1) % 2)
            if p < n_pairs:
                s_ = p % 3
                got2 = []
                for half, kk_ in ((0, "g"), (1, "u")):
                    b = (p % 2) * 2 + half
                    i, hi, lo, got = take(key + kk_)

                    def part(e, nb, kcs):
                        c, o = slice(128 * nb, 128 * nb + 128), PS[:, b, 256 * nb:256 * nb + 256]
                        return [mm3(e, o, hi[:, kc, c], lo[:, kc, c], XH[:, kc, :], XL[:, kc, :], kc == 0, kc == 7)
                                for kc in kcs][-1]
                    t = as_they_come(p + half, 2, part, ready, got, pf[b])
                    got2.append((b, t))
                    done(i, t)
                hf, tf = evac_h(p, got2)
                ring[p] = split_act(hf, RH[:, s_].rearrange("p c n -> p (c n)"), RL[:, s_].rearrange("p c n -> p (c n)"),
                                    tf, ring.get(("down", p - 3)))
            if p > 0:
                q = p - 1
                i, hi, lo, got = take(key + "d")
                RHs, RLs = RH[:, q % 3], RL[:, q % 3]
                t = T(lambda e: mm_down(e, hi, lo, lambda c: RHs[:, c, :], lambda c: RLs[:, c, :], [4, 5, 6, 7], 2,
                                        first and q == 0, last and q == n_pairs - 1),
                      got, ring[q], [pf[b] for b in (4, 5, 6, 7)] if first and q == 0 else None)
                ring[("down", q)] = t
                done(i, t)
        return t

    SG = ar(6144, 2, 512)
    HF = ar(7168, 2, 512)
    hst = {"n": 0}

    def swiglu_evac():
        def evac(p, got):
            n_ = hst["n"] % 2
            hst["n"] += 1
            (bg, tg_), (bu, tu) = got
            t = ACTE(lambda e: e.activation(SG[:, n_, :], PS[:, bg, :], ACT.Silu), tg_, hst.get(("hf", n_)))
            pf[bg] = t
            t = V(lambda e: e.tensor_tensor(HF[:, n_, :], SG[:, n_, :], PS[:, bu, :], ALU.mult), t, tu,
                  hst.get(("sp", n_)))
            pf[bu] = t
            hst[("hf", n_)] = t
            hst[("sp", n_)] = t
            return HF[:, n_, :], t
        return evac

    def layer1(l):
        marks = K.fence()
        act = to_fm(X, X1H, X1L, [4, 5], marks, scaled(lambda c: modc(l, 1, c), lambda c: modc(l, 0, c)))
        R = ar(6144, 2, 1024)
        SZ = ar(8192, 2, 512)
        XP = ar(9216, 6, 259)
        XC = ar(10770, 6, 256)
        QK = ar(12306, 4, 256)
        AVD = ar(13330, 2, 136)
        XS = ar(13602, 2, 512)
        XD = ar(14626, 2, 512)
        QT = ar(15650, 4, 256)
        E8 = ar(0, 8, 384)
        RT = ar(3072, 4, 384)
        LG = ar(4608, 4, 384)
        PT = ar(9216, 4, 384)
        f0 = K.fence()
        if l == 0:
            ada_run([(0, 1), (0, 2)], [ar(0, 2048), ar(4096, 2048), ar(13602, 2048)], [ar(2048, 2048)], f0)
            st["rate"] = 2
        for blk in range(3):
            bb = [[0, 1], [2, 3], [0, 1]][blk]
            t = gemm_blk(f"in{l}", act, bb, 512, 4)
            for k in range(2):
                dst = R[:, k, 512 * blk:512 * blk + 512] if blk < 2 else SZ[:, k, :]
                fn = ACT.Copy if blk < 2 else ACT.Silu
                pf[bb[k]] = ACTE(lambda e: e.activation(dst, PS[:, bb[k], :], fn), t, f0)
        t_r = K.last["a"]
        t_sz = t_r
        tz = G(lambda e: e.memset(XP[:, :, 0:3], 0.0), f0)

        txp = []

        def ev_x(j, p, t):
            r = ACTE(lambda e: e.activation(XP[:, 2 * j:2 * j + 2, 3:259], p.rearrange("p (c n) -> p c n", c=2),
                                            ACT.Copy), t, tz)
            txp.append(r)
            return [r]
        gemm_fm(f"in{l}", 768, act, [4, 5], ev_x)

        tcv = []
        for c in range(6):
            dst = XC[:, c, :]
            t = V(lambda e: e.tensor_scalar(dst, XP[:, c, 0:256], pcol(f"conv_w{l}", c), pcol(f"conv_b{l}", c),
                                            ALU.mult, ALU.add), txp, tz)
            for k in range(1, 4):
                t = V(lambda e: e.scalar_tensor_tensor(dst, XP[:, c, k:k + 256], pcol(f"conv_w{l}", 6 * k + c), dst,
                                                       ALU.mult, ALU.add), t)
            tcv.append(t)
        t_xc = ACTE(lambda e: e.activation(XC, XC, ACT.Silu), tcv)


        def ev_q(j, p, t):
            return [ACTE(lambda e: e.activation(QK[:, 0:2, :], p.rearrange("p (c n) -> p c n", c=2), ACT.Copy), t)]
        gemm_fm(f"in{l}", 256, act, [6], ev_q)

        def ev_k(j, p, t):
            return [ACTE(lambda e: e.activation(QK[:, 2, :], p, ACT.Copy), t)]
        gemm_fm(f"in{l}", 128, act, [7], ev_k)
        t_k = K.last["a"]

        for n_, bk, off, F_ in ((128, 2, 0, ar(15650, 256)), (8, 3, 128, ar(15906, 256))):
            gemm_fm(f"in{l}", n_, act, [bk], lambda j, p, t: [ACTE(lambda e: e.activation(F_[0:n_, :], p, ACT.Copy), t, f0)])
            t = transposes(bk, [(PS[:, bk, n_ * k:n_ * k + n_], F_[0:n_, 128 * k:128 * k + 128]) for k in range(2)])
            pf[bk] = ACTE(lambda e: e.activation(AVD[:, :, off:off + n_], PS[:, bk, 0:2 * n_].rearrange(
                "p (k n) -> p k n", k=2), ACT.Copy), t)
        t_av = K.last["a"]
        while side:
            side.pop(0)()
        st["rate"] = 1
        f0 = [f0, K.last["v"], K.last["t"]]
        rq = R[:, :, 0:512].rearrange("p t (h x d) -> p t h x d", h=8, x=2)
        tmp = [ar(3072 + 512 * i, 2, 8, 32) for i in range(4)]
        bc = lambda tab: AP(tab.tensor, tab.offset, [list(tab.ap[0]), [32, 2], [0, 8], [1, 32]])
        ops = ((0, COS), (1, SIN), (0, SIN), (1, COS))
        for i, (half, tab) in enumerate(ops):
            t = V(lambda e: e.tensor_tensor(tmp[i], rq[:, :, :, half, :], bc(tab), ALU.mult), t_r, t_rot, f0)
        t = V(lambda e: e.tensor_tensor(rq[:, :, :, 0, :], tmp[0], tmp[1], ALU.subtract), t)
        t_rq = V(lambda e: e.tensor_tensor(rq[:, :, :, 1, :], tmp[2], tmp[3], ALU.add), t)
        mix = {}
        g2 = lambda a: a.rearrange("p (t h) -> p t h", t=2)

        def retention():
            for cp in range(2):
                b = 6 + cp
                t2 = transposes(b, [(PS[:, b, 256 * ci + 128 * tt:256 * ci + 128 * tt + 128],
                                     R[:, tt, 128 * (2 * cp + ci):128 * (2 * cp + ci) + 128])
                                    for ci in range(2) for tt in range(2)], t_rq)
                pf[b] = ACTE(lambda e: e.activation(QT[:, 2 * cp:2 * cp + 2, :], PS[:, b, :].rearrange(
                    "p (c n) -> p c n", c=2), ACT.Copy), t2)
            t_qt = [pf[6], pf[7]]
            yield
            tr = []
            for h in range(4):
                b = 6 + h % 2
                pr, ch = slice(64 * (h % 2), 64 * (h % 2) + 64), h // 2

                def f(e):
                    e.matmul(PS[:, b, 0:256], QT[pr, 2 + ch, 0:128], QT[pr, ch, :], start=True, stop=True)
                    return e.matmul(PS[:, b, 256:384], QT[pr, 2 + ch, 128:256], QT[pr, ch, 128:256], start=True, stop=True)
                t = T(f, t_qt, pf[b])
                dec = CST[:, C_DEC + 256 * h:C_DEC + 256 * h + 256]
                V(lambda e: e.tensor_tensor(RT[:, h, 0:256], PS[:, b, 0:256], dec, ALU.mult), t, t_rq)
                pf[b] = V(lambda e: e.tensor_tensor(RT[:, h, 256:384], PS[:, b, 256:384], dec[:, 0:128], ALU.mult), t)
                tr.append(pf[b])
                yield
            rv = lambda k, h: R[:, k, 512 + 64 * h:512 + 64 * h + 64]

            def f(e):
                for h in range(4):
                    e.matmul(PS[:, 0, 64 * h:64 * h + 64], RT[:, h, 0:128], rv(0, h), start=True, stop=True)
                    e.matmul(PS[:, 0, 256 + 64 * h:256 + 64 * h + 64], RT[:, h, 128:256], rv(0, h), start=True, stop=False)
                    m = e.matmul(PS[:, 0, 256 + 64 * h:256 + 64 * h + 64], RT[:, h, 256:384], rv(1, h), start=False,
                                 stop=True)
                return m
            t = T(f, tr, t_r, pf[0])
            yield
            O8, O8s = ar(15650, 8, 64), ar(16162, 8, 64)
            m8, v8 = SMT[:, 0:8], SMT[:, 8:16]
            b8 = lambda a: view(a, [1, 8], [0, 64])
            po = PS[:, 0, :].rearrange("p (a b) -> p a b", a=8)
            t = V(lambda e: e.tensor_reduce(m8, po, AX, ALU.add), t, f0)
            t = V(lambda e: e.tensor_scalar(m8, m8, 1.0 / 64, None, ALU.mult), t)
            t = V(lambda e: e.tensor_tensor(O8, po, b8(m8), ALU.subtract), t)
            pf[0] = t
            t = V(lambda e: e.tensor_tensor(O8s, O8, O8, ALU.mult), t)
            t = V(lambda e: e.tensor_reduce(v8, O8s, AX, ALU.add), t)
            t = V(lambda e: e.tensor_scalar(v8, v8, 1.0 / 64, None, ALU.mult), t)
            yield
            t = rsqrt(v8, v8, LN_EPS, t)
            yield
            t = V(lambda e: e.tensor_tensor(O8, O8, b8(v8), ALU.mult), t)
            t2 = ACTE(lambda e: e.activation(R[:, :, 768:1024], R[:, :, 768:1024], ACT.Silu), t_r)
            mix["ret"] = V(lambda e: e.tensor_tensor(R[:, :, 0:256], R[:, :, 768:1024],
                                                O8.rearrange("p (t h) d -> p t (h d)", t=2), ALU.mult), t, t2,
                      t_qt)


        def state_space():
            for c in range(4):
                b = 4 + c % 2
                t = transposes(b, [(PS[:, b, 128 * tt:128 * tt + 128], XC[:, c, 128 * tt:128 * tt + 128])
                                   for tt in range(2)], t_xc)
                pf[b] = ACTE(lambda e: e.activation(XS[:, :, 128 * c:128 * c + 128], PS[:, b, 0:256].rearrange(
                    "p (t n) -> p t n", t=2), ACT.Copy), t, f0)
            t_xs = pf[b]
            yield
            DTt, AA, T8, U8, CS, CSN = [SMT[:, 16 + 16 * i:32 + 16 * i] for i in range(6)]
            dtr = AVD[:, :, 128:136]
            t = V(lambda e: e.tensor_tensor(g2(DTt), dtr, view(dtb[:, l, :], [0, 2], [1, 8]), ALU.add), t_av)
            t = softplus(DTt, DTt, 1.0, (T8, U8, CS, CSN, AA), t)
            t_dt = t
            yield
            ta = ACTE(lambda e: e.activation(T8[:, 0:8], alog[:, l, :], ACT.Exp), t)
            t = V(lambda e: e.scalar_tensor_tensor(g2(AA), g2(DTt), -1.0, view(T8, [0, 2], [1, 8]), ALU.mult, ALU.mult), t,
                  ta)
            t_a = t

            def f(e):
                e.matmul(PS[:, 4, 0:8], tri, AA[:, 0:8], start=True, stop=True)
                e.matmul(PS[:, 4, 8:16], ones, AA[:, 0:8], start=True, stop=False)
                return e.matmul(PS[:, 4, 8:16], tri, AA[:, 8:16], start=False, stop=True)
            t = T(f, t, pf[4])
            yield
            pf[4] = t_cs = V(lambda e: e.tensor_copy(CS, PS[:, 4, 0:16]), t)
            t_xd = V(lambda e: e.tensor_tensor(XD.rearrange("p t (h d) -> p t h d", h=8),
                                               XS.rearrange("p t (h d) -> p t h d", h=8),
                                               view(DTt, [8, 2], [1, 8], [0, 64]), ALU.mult), t_xs, t_dt, f0)
            tt2 = []
            for h in range(8):
                b = 4 + h % 2
                col = lambda k: view(AA[:, 8 * k + h:8 * k + h + 1], [0, 128])

                def f(e):
                    e.matmul(PS[:, b, 0:128], col(0), tri, start=True, stop=True)
                    e.matmul(PS[:, b, 128:256], col(0), ones, start=True, stop=False)
                    return e.matmul(PS[:, b, 128:256], col(1), tri, start=False, stop=True)
                t = T(f, t_a, pf[b])
                V(lambda e: e.scalar_tensor_tensor(E8[:, h, 0:256], negm, CS[:, h:h + 1], PS[:, b, 0:256], ALU.subtract,
                                                   ALU.add), t, t_cs, f0)
                pf[b] = V(lambda e: e.scalar_tensor_tensor(E8[:, h, 256:384], negm[:, 0:128], CS[:, 8 + h:9 + h],
                                                           PS[:, b, 128:256], ALU.subtract, ALU.add), t, t_cs)
                tt2.append(pf[b])
                yield
            t_e = ACTE(lambda e: e.activation(E8, E8, ACT.Exp), tt2)
            for g in range(2):
                b = 4 + g
                pr = slice(64 * g, 64 * g + 64)

                def f(e):
                    e.matmul(PS[:, b, 0:256], XC[pr, 4, 0:128], XC[pr, 5, :], start=True, stop=True)
                    return e.matmul(PS[:, b, 256:384], XC[pr, 4, 128:256], XC[pr, 5, 128:256], start=True, stop=True)
                t = T(f, t_xc, pf[b])
                for r in range(4):
                    h = 4 * g + r
                    t2 = V(lambda e: e.tensor_tensor(E8[:, h, :], E8[:, h, :], PS[:, b, 0:384], ALU.mult), t, t_e)
                pf[b] = t2
                yield

            def f(e):
                for h in range(8):
                    v = lambda k: XD[:, k, 64 * h:64 * h + 64]
                    e.matmul(PS[:, 4, 64 * h:64 * h + 64], E8[:, h, 0:128], v(0), start=True, stop=True)
                    e.matmul(PS[:, 5, 64 * h:64 * h + 64], E8[:, h, 128:256], v(0), start=True, stop=False)
                    m = e.matmul(PS[:, 5, 64 * h:64 * h + 64], E8[:, h, 256:384], v(1), start=False, stop=True)
                return m
            t = T(f, t2, t_xd, pf[4], pf[5])
            yield
            h8 = lambda a: a.rearrange("p t (h d) -> p t h d", h=8)
            t3 = V(lambda e: e.tensor_tensor(h8(XS), h8(XS), view(dsk[:, l, :], [0, 2], [1, 8], [0, 64]), ALU.mult), t_xd)
            for k in range(2):
                pf[4 + k] = V(lambda e: e.tensor_tensor(XS[:, k, :], PS[:, 4 + k, :], XS[:, k, :], ALU.add), t, t3)
            t = V(lambda e: e.tensor_tensor(XS, XS, SZ, ALU.mult), pf[4], pf[5], t_sz)
            t = V(lambda e: e.tensor_tensor(XD, XS, XS, ALU.mult), t)
            yield
            m4 = SMT[:, 112:116]
            t = V(lambda e: e.tensor_reduce(m4, XD.rearrange("p t (g d) -> p (t g) d", g=2), AX, ALU.add), t)
            t = V(lambda e: e.tensor_scalar(m4, m4, 1.0 / 256, None, ALU.mult), t)
            yield
            t = rsqrt(m4, m4, LN_EPS, t)
            yield
            mix["ssd"] = V(lambda e: e.tensor_tensor(R[:, :, 256:768].rearrange("p t (g d) -> p t g d", g=2),
                                                XS.rearrange("p t (g d) -> p t g d", g=2),
                                                view(m4, [2, 2], [1, 2], [0, 256]), ALU.mult), t, mix["ret"])


        def window():
            t = T(lambda e: e.matmul(PS[:, 1, 0:256], swap, QK[:, 2, :], start=True, stop=True), t_k, pf[1])
            t_ks = pf[1] = ACTE(lambda e: e.activation(QK[:, 3, :], PS[:, 1, 0:256], ACT.Copy), t)

            yield
            mx, ng, den, ek = [SMT[:, 128 + 8 * i:136 + 8 * i] for i in range(4)]
            for h in range(4):
                b = 1 + h % 3
                base, kv = 64 * (h % 2), h // 2
                kc = 2 if base == 64 * kv else 3
                pr = slice(base, base + 64)

                def f(e):
                    e.matmul(PS[:, b, 0:128], QK[pr, h // 2, 0:128], QK[pr, kc, 0:128], start=True, stop=True)
                    return e.matmul(PS[:, b, 128:384], QK[pr, h // 2, 128:256], QK[pr, kc, :], start=True, stop=True)
                t = T(f, t_ks, t_k, pf[b])
                V(lambda e: e.scalar_tensor_tensor(LG[:, h, 0:128], PS[:, b, 0:128], 0.125, BT[:, h, 128:256], ALU.mult,
                                                   ALU.add), t, t_bt, t_rq)
                pf[b] = V(lambda e: e.scalar_tensor_tensor(LG[:, h, 128:384], PS[:, b, 128:384], 0.125, BT[:, h, :],
                                                           ALU.mult, ALU.add), t)
                yield
            t = pf[b]
            V(lambda e: e.tensor_reduce(mx[:, 0:4], LG[:, :, 0:128], AX, ALU.max), t)
            t = V(lambda e: e.tensor_reduce(mx[:, 4:8], LG[:, :, 128:384], AX, ALU.max), t)
            t = V(lambda e: e.tensor_tensor(g2(mx), g2(mx), view(snk[:, l, :], [0, 2], [1, 4]), ALU.max), t)
            tn = V(lambda e: e.tensor_scalar(ng, mx, -1.0, None, ALU.mult), t)
            t = V(lambda e: e.tensor_tensor(g2(ek), g2(ng), view(snk[:, l, :], [0, 2], [1, 4]), ALU.add), tn)
            t5 = ACTE(lambda e: e.activation(ek, ek, ACT.Exp), t)
            yield
            for h in range(4):
                ACTE(lambda e: e.activation(LG[:, h, 0:128], LG[:, h, 0:128], ACT.Exp, bias=ng[:, h:h + 1],
                                            accum_out=den[:, h:h + 1]), tn)
                t = ACTE(lambda e: e.activation(LG[:, h, 128:384], LG[:, h, 128:384], ACT.Exp, bias=ng[:, 4 + h:5 + h],
                                                accum_out=den[:, 4 + h:5 + h]), tn)
            t = V(lambda e: e.tensor_tensor(den, den, ek, ALU.add), t, t5)
            t_den = V(lambda e: e.reciprocal(den, den), t)
            tp = []
            yield
            for h in range(4):
                b = 1 + h % 3
                t = transposes(b, [(PS[:, b, 128 * i:128 * i + 128], LG[:, h, 128 * i:128 * i + 128]) for i in range(3)],
                               t_den)
                pf[b] = ACTE(lambda e: e.activation(PT[:, h, :], PS[:, b, 0:384], ACT.Copy), t, tcv)
                tp.append(pf[b])
                yield

            def f(e):
                for h in range(4):
                    v = lambda k: AVD[:, k, 64 * (h // 2):64 * (h // 2) + 64]
                    e.matmul(PS[:, 2, 64 * h:64 * h + 64], PT[:, h, 0:128], v(0), start=True, stop=True)
                    e.matmul(PS[:, 2, 256 + 64 * h:256 + 64 * h + 64], PT[:, h, 128:256], v(0), start=True, stop=False)
                    m = e.matmul(PS[:, 2, 256 + 64 * h:256 + 64 * h + 64], PT[:, h, 256:384], v(1), start=False, stop=True)
                return m
            t = T(f, tp, t_av, pf[2])
            yield
            pf[2] = mix["swa"] = V(lambda e: e.tensor_tensor(R[:, :, 768:1024].rearrange("p t (h d) -> p t h d", h=4),
                                                PS[:, 2, :].rearrange("p (t h d) -> p t h d", t=2, h=4),
                                                view(den, [4, 2], [1, 4], [0, 64]), ALU.mult), t, t_den, mix["ret"])

        work = [retention(), window(), state_space()]
        while work:
            work = [w for w in work if next(w, 0) is None]
        t = [mix["swa"], mix["ssd"], mix["ret"]]
        marks = K.fence()

        def ev(c, p, t, dst):
            if 2 <= c < 6:
                return V(lambda e: e.tensor_scalar(dst, p, pcol(f"ssd_norm{l}", c - 2), None, ALU.mult), t)
            return V(lambda e: e.tensor_copy(dst, p), t)
        act = to_fm(R, X2H, X2L, [2, 3], marks, ev)
        t = gemm_tm(f"out{l}", act, [4, 5, 6, 7])
        t = residual(l, 0, [4, 5, 6, 7], t)
        marks = K.fence()
        if l == 0:
            act = to_fm(X, X1H, X1L, [2, 3], marks, scaled(lambda c: modc(l, 4, c), lambda c: modc(l, 3, c)))
            ada_run([(1, 0), (1, 1), (1, 2)], [ar(8192, 2048), ar(10240, 2048)],
                    [ar(12288, 2048), ar(14336, 2048)], marks)
            lo_pool[:] = [4, 8]
            t = ffn("ffn", 11, act, swiglu_evac(), True, True)
            while side:
                side.pop(0)()
            lo_pool[:] = [4, 8]
            t = residual(l, 1, [4, 5, 6, 7], t)
        else:
            t = moe()
            t = residual(l, 1, None, t, ar(14080, 2, 1024))

    SMT = sm(256)
    FLAG = SM[:, sm_at[0]:sm_at[0] + 1].bitcast(I32)
    sm(1)

    def softplus(dst, src, sign, tmps, *deps):
        a, tt_, u, w, z = tmps
        t = V(lambda e: e.tensor_scalar(a, src, sign, None, ALU.mult), *deps)
        t = ACTE(lambda e: e.activation(tt_, a, ACT.Abs), t)
        t = ACTE(lambda e: e.activation(tt_, tt_, ACT.Exp, scale=-1.0), t)
        t = V(lambda e: e.tensor_scalar(u, tt_, 1.0, None, ALU.add), t)
        t2 = ACTE(lambda e: e.activation(w, u, ACT.Ln), t)
        t = V(lambda e: e.tensor_scalar(u, u, -1.0, None, ALU.add), t, t2)
        t = V(lambda e: e.tensor_scalar(z, u, 0.0, None, ALU.is_equal), t)
        t = V(lambda e: e.tensor_tensor(u, u, z, ALU.add), t)
        t = V(lambda e: e.reciprocal(u, u), t)
        t = V(lambda e: e.tensor_tensor(w, w, tt_, ALU.mult), t)
        t = V(lambda e: e.tensor_tensor(w, w, u, ALU.mult), t)
        t = V(lambda e: e.tensor_tensor(z, z, tt_, ALU.mult), t)
        t = V(lambda e: e.tensor_tensor(w, w, z, ALU.add), t)
        return V(lambda e: e.scalar_tensor_tensor(dst, a, 0.0, w, ALU.max, ALU.add), t)

    HM = ar(6144, 2, 1024)
    RK, RP, RP2, GG, LGT = [ar(8192 + 16 * i, 2, 8) for i in range(5)]
    m1, den2, CNT = ar(8272, 2), ar(8274, 2), ar(8280, 8)
    PP, PG, PGT = ar(8448, 2, 2, 128), ar(8960, 2, 2, 128), ar(9472, 2, 256)
    SGm, HFm = ar(9984, 2, 512), ar(11008, 2, 512)
    YE = ar(12032, 2, 1024)
    FACC = ar(14080, 2, 1024)

    def router():
        CMP, CM2 = ar(9984, 2, 8, 8), ar(10112, 2, 8, 8)
        SCR, SHR = ar(12032, 1024), ar(13056, 1024)
        t1 = rows_of(1, 4, SCR)
        t2 = rows_of(1, 3, SHR)
        for k in range(2):
            t = V(lambda e: e.tensor_tensor(HM[:, k, :], X[:, k, :], SCR, ALU.mult), t1, K.last["v"])
            t = V(lambda e: e.tensor_tensor(HM[:, k, :], HM[:, k, :], SHR, ALU.add), t, t2)
        for cp in range(4):
            b = 2 + cp % 2
            t3 = transposes(b, [(PS[:, b, 256 * ci + 128 * tt:256 * ci + 128 * tt + 128],
                                 HM[:, tt, 128 * (2 * cp + ci):128 * (2 * cp + ci) + 128])
                                for ci in range(2) for tt in range(2)], t)
            pf[b] = ACTE(lambda e: e.activation(XF[:, 2 * cp:2 * cp + 2, :], PS[:, b, :].rearrange(
                "p (c n) -> p c n", c=2), ACT.Copy), t3)

        def f(e):
            for k in range(2):
                for c in range(8):
                    m = e.matmul(PS[:, 0, 8 * k:8 * k + 8], XF[:, c, 128 * k:128 * k + 128], WR[:, c, :],
                                 start=(c == 0), stop=(c == 7))
            return m
        t = T(f, pf[2], pf[3], pf[0])
        t = V(lambda e: e.tensor_tensor(LGT, PS[:, 0, 0:16].rearrange("p (k n) -> p k n", k=2),
                                        view(rbias, [0, 2], [1, 8]), ALU.add), t)
        pf[0] = t
        mine = view(LGT, [8, 2], [1, 8], [0, 8])
        other = view(LGT, [8, 2], [0, 8], [1, 8])
        low = view(CST[:, C_LOW:C_LOW + 64], [0, 2], [8, 8], [1, 8])
        t1 = V(lambda e: e.tensor_tensor(CMP, other, mine, ALU.is_gt), t)
        t2 = V(lambda e: e.tensor_tensor(CM2, other, mine, ALU.is_equal), t)
        t2 = V(lambda e: e.tensor_tensor(CM2, CM2, low, ALU.mult), t2)
        t2 = V(lambda e: e.tensor_tensor(CMP, CMP, CM2, ALU.add), t1, t2)
        t2 = V(lambda e: e.tensor_reduce(RK, CMP, AX, ALU.add), t2)
        t_sel = V(lambda e: e.tensor_scalar(RK, RK, 1.5, None, ALU.is_lt), t2)
        t = V(lambda e: e.tensor_reduce(m1, LGT, AX, ALU.max), t)
        t = V(lambda e: e.tensor_tensor(GG, LGT, view(m1, [1, 2], [0, 8]), ALU.subtract), t)
        t = ACTE(lambda e: e.activation(GG, GG, ACT.Exp), t)
        t = V(lambda e: e.tensor_tensor(GG, GG, RK, ALU.mult), t, t_sel)
        t = V(lambda e: e.tensor_reduce(den2, GG, AX, ALU.add), t)
        t = V(lambda e: e.reciprocal(den2, den2), t)
        t_gg = V(lambda e: e.tensor_tensor(GG, GG, view(den2, [1, 2], [0, 8]), ALU.mult), t)

        def f(e):
            e.matmul(PS[:, 1, 0:8], tri, RK[:, 0, :], start=True, stop=True)
            e.matmul(PS[:, 1, 8:16], ones, RK[:, 0, :], start=True, stop=False)
            e.matmul(PS[:, 1, 8:16], tri, RK[:, 1, :], start=False, stop=True)
            e.matmul(PS[:, 1, 16:24], ones, RK[:, 0, :], start=True, stop=False)
            return e.matmul(PS[:, 1, 16:24], ones, RK[:, 1, :], start=False, stop=True)
        t = T(f, t_sel, pf[1])
        t2 = V(lambda e: e.tensor_scalar(RP, RK, -1001.0, 1000.0, ALU.mult, ALU.add), t_sel)
        t2 = V(lambda e: e.tensor_tensor(RP, RP, PS[:, 1, 0:16].rearrange("p (k n) -> p k n", k=2), ALU.add), t, t2)
        t_rp = V(lambda e: e.tensor_scalar(RP2, RP, -128.0, None, ALU.add), t2)
        pf[1] = t3 = V(lambda e: e.tensor_reduce(CNT[:, 0:1], PS[:, 1, 16:24], AX, ALU.max), t)
        t_fl = V(lambda e: e.tensor_scalar(FLAG, CNT[:, 0:1], 128.5, None, ALU.is_gt), t3)
        return [t_gg, t_rp, t_fl]

    def moe():
        t_r = router()
        f0 = K.fence()
        st["more"] = f0
        issue_dma()
        pump()
        t_f = V(lambda e: e.memset(FACC, 0.0), f0)
        GH = X1H[:, :, :].rearrange("p a b -> p (a b)").rearrange("p (s c n) -> p s c n", s=2, c=8)
        GL = X1L[:, :, :].rearrange("p a b -> p (a b)").rearrange("p (s c n) -> p s c n", s=2, c=8)
        RH = X2H[:, :, :].rearrange("p a b -> p (a b)").rearrange("p (s c n) -> p s c n", s=4, c=4)
        RL = X2L[:, :, :].rearrange("p a b -> p (a b)").rearrange("p (s c n) -> p s c n", s=4, c=4)
        iota = CST[:, C_IOT:C_IOT + 128]
        gx, pgt, used, yev = {}, {}, {}, {}

        def select(e_):
            s_ = e_ % 2
            for k in range(2):
                V(lambda e: e.tensor_scalar(PP[:, s_, k, :], iota, RP[:, k, e_:e_ + 1], None, ALU.is_equal), t_r,
                  used.get(("p", e_ - 2)))
                t = V(lambda e: e.tensor_scalar(PG[:, s_, k, :], iota, RP[:, k, e_:e_ + 1], GG[:, k, e_:e_ + 1],
                                                ALU.is_equal, ALU.mult))
            gx[e_] = []
            pgt[("pp", e_)] = t

        def gather(e_, half):
            s_ = e_ % 2

            def f(e):
                for c in range(4):
                    for k in range(2):
                        m = e.matmul(PS[:, 7, 128 * c:128 * c + 128], HM[:, k, 512 * half + 128 * c:512 * half + 128 * c + 128],
                                     PP[:, s_, k, :], start=(k == 0), stop=(k == 1))
                return m
            t = T(f, pgt[("pp", e_)], pf[7])
            pf[7] = split_act(PS[:, 7, :].rearrange("p (c n) -> p c n", c=4), GH[:, s_, 4 * half:4 * half + 4, :],
                              GL[:, s_, 4 * half:4 * half + 4, :], t, used.get(("x", e_ - 2)))
            gx[e_] += pf[7]

        def turn(e_):
            s_ = e_ % 2
            t = transposes(7, [(PS[:, 7, 128 * k:128 * k + 128], PG[:, s_, k, :]) for k in range(2)],
                           pgt[("pp", e_)])
            used[("p", e_)] = t
            pf[7] = pgt[e_] = ACTE(lambda e: e.activation(PGT[:, s_, :], PS[:, 7, 0:256], ACT.Copy), t,
                                   used.get(("s", e_ - 2)))

        def scatter(e_, q):
            s_, k, nb = e_ % 2, q // 2, q % 2
            ns = slice(512 * nb, 512 * nb + 512)
            t = T(lambda e: e.matmul(PS[:, 7, :], PGT[:, s_, 128 * k:128 * k + 128], YE[:, s_, ns], start=True, stop=True),
                  pgt[e_], yev[e_], pf[7])
            used[("s", e_)] = t
            pf[7] = V(lambda e: e.tensor_tensor(FACC[:, k, ns], FACC[:, k, ns], PS[:, 7, :], ALU.add), t, t_f)

        todo = []

        def between():
            if todo:
                todo.pop(0)()

        select(0)
        gather(0, 0)
        gather(0, 1)
        turn(0)
        hid = {}
        n = 0
        for e_ in range(NEXP):
            XH, XL = GH[:, e_ % 2], GL[:, e_ % 2]
            if e_ > 0:
                todo.extend([lambda q=q, e_=e_: scatter(e_ - 1, q) for q in range(4)])
            if e_ < NEXP - 1:
                todo.extend([lambda e_=e_: select(e_ + 1), lambda e_=e_: gather(e_ + 1, 0),
                             lambda e_=e_: gather(e_ + 1, 1), lambda e_=e_: turn(e_ + 1)])
            for b_ in range(8):
                if b_ < 7:
                    got2 = []
                    for q, kk_ in ((0, "mg"), (1, "mu")):
                        bk = 2 * q + b_ % 2
                        for k0 in (0, 4):
                            i, hi, lo, got = take(kk_)

                            def f(e):
                                for c in range(4):
                                    m = mm3(e, PS[:, bk, :], XH[:, k0 + c, :], XL[:, k0 + c, :], hi[:, c, :], lo[:, c, :],
                                            k0 + c == 0, k0 + c == 7)
                                return m
                            t = T(f, got, gx[e_], pf[bk])
                            done(i, t)
                            if q == 0 and k0 == 0 and b_ > 0:
                                tr = transposes(4, [(PS[:, 4, 128 * j:128 * j + 128], HFm[:, (b_ - 1) % 2, 128 * j:128 * j + 128])
                                                    for j in range(4)], hid["t"])
                                sl = (7 * e_ + b_ - 1) % 3
                                hid[("tr", (b_ - 1) % 2)] = tr
                                pf[4] = hid["s"] = split_act(PS[:, 4, :].rearrange("p (c n) -> p c n", c=4), RH[:, sl],
                                                             RL[:, sl], tr, hid.get(("d", sl)))
                            else:
                                between()
                        got2.append((bk, t))
                    (bg, tg_), (bu, tu) = got2
                    s2 = b_ % 2
                    if b_ == 6:
                        used[("x", e_)] = tu
                    t = ACTE(lambda e: e.activation(SGm[:, s2, :], PS[:, bg, :], ACT.Silu), tg_, hid.get(("h", s2)))
                    pf[bg] = t
                    t = V(lambda e: e.tensor_tensor(HFm[:, s2, :], SGm[:, s2, :], PS[:, bu, :], ALU.mult), t, tu,
                          hid.get(("tr", s2)))
                    pf[bu] = hid[("h", s2)] = hid["t"] = t
                else:
                    tr = transposes(4, [(PS[:, 4, 128 * j:128 * j + 128], HFm[:, (b_ - 1) % 2, 128 * j:128 * j + 128])
                                        for j in range(4)], hid["t"])
                    sl = (7 * e_ + b_ - 1) % 3
                    hid[("tr", (b_ - 1) % 2)] = tr
                    pf[4] = hid["s"] = split_act(PS[:, 4, :].rearrange("p (c n) -> p c n", c=4), RH[:, sl], RL[:, sl], tr,
                                                 hid.get(("d", sl)))
                if b_ > 0:
                    sl = (7 * e_ + b_ - 1) % 3
                    for half in range(2):
                        i, hi, lo, got = take("md")

                        def f(e):
                            for c in range(2):
                                q = 2 * half + c
                                for nb in range(2):
                                    ns = slice(512 * nb, 512 * nb + 512)
                                    m = mm3(e, PS[:, 5 + nb, :], RH[:, sl, q, :], RL[:, sl, q, :], hi[:, c, ns],
                                            lo[:, c, ns], b_ == 1 and q == 0, b_ == 7 and q == 3)
                            return m
                        t = T(f, got, hid["s"], [pf[5], pf[6]] if b_ == 1 and half == 0 else None)
                        hid[("d", sl)] = t
                        done(i, t)
                        between()
            for nb in range(2):
                ns = slice(512 * nb, 512 * nb + 512)
                pf[5 + nb] = ACTE(lambda e: e.activation(YE[:, e_ % 2, ns], PS[:, 5 + nb, :], ACT.Copy), t,
                                  used.get(("s", e_ - 2)))
            yev[e_] = [pf[5], pf[6]]
            assert not todo
        for q in range(4):
            scatter(NEXP - 1, q)
        marks = K.fence()
        K.wait("s", marks)
        rest_of_rows()
        return marks

    def rest_of_rows():
        sems = {e: K.sem("s_r" + e) for e in "vagt"}
        sems.update({f"r{i}": K.sem(f"s_r{i}") for i in range(2)})
        names = {"v": "vector", "a": "scalar", "g": "gpsimd", "t": "tensor", "s": "sync"}
        with nc.Block() as blk:
            def part(n):
                def _(eng):
                    over = eng.value_load(FLAG[0:1, 0:1], min_val=0, max_val=1)
                    with eng.If(over > 0):
                        rest_body(Core(nc, ctx, "r", n, sems))
                return _
            blk.vector(part("v"))
            blk.scalar(part("a"))
            blk.gpsimd(part("g"))
            blk.tensor(part("t"))
            blk.sync(part("s"))

    def rest_body(R):
        XG, HT2 = ar(0, 8, 128), ar(1024, 4, 128)
        WB2 = [ar(2048, 2048), ar(4096, 2048)]
        P1, G1, GT1, Y1 = ar(8448, 2, 128), ar(8704, 2, 128), ar(8960, 256), ar(12032, 1024)
        H1 = ar(9984, 512)
        iota = CST[:, C_IOT:C_IOT + 128]
        free = [None, None]
        n = [0]

        def load(src):
            i = n[0] % 2
            n[0] += 1
            dst = WB2[i].rearrange("p (c n) -> p c n", c=src.shape[1])
            return i, dst, R.dma("s", f"r{i}", dst, src, free[i])
        t_e = None
        for e_ in range(NEXP):
            for k in range(2):
                R.V(lambda e: e.tensor_scalar(P1[:, k, :], iota, RP2[:, k, e_:e_ + 1], None, ALU.is_equal), t_e)
                t = R.V(lambda e: e.tensor_scalar(G1[:, k, :], iota, RP2[:, k, e_:e_ + 1], GG[:, k, e_:e_ + 1],
                                                  ALU.is_equal, ALU.mult))
            for half in range(2):
                def f(e):
                    for c in range(4):
                        for k in range(2):
                            m = e.matmul(PS[:, half, 128 * c:128 * c + 128],
                                         HM[:, k, 512 * half + 128 * c:512 * half + 128 * c + 128], P1[:, k, :],
                                         start=(k == 0), stop=(k == 1))
                    return m
                t2 = R.T(f, t)
                tx = R.A(lambda e: e.activation(XG[:, 4 * half:4 * half + 4, :], PS[:, half, :].rearrange(
                    "p (c n) -> p c n", c=4), ACT.Copy), t2)

            def f(e):
                for k in range(2):
                    m = e.transpose(PS[:, 2, 128 * k:128 * k + 128], G1[:, k, :], ident)
                return m
            t2 = R.T(f, t)
            tgt = R.A(lambda e: e.activation(GT1, PS[:, 2, 0:256], ACT.Copy), t2)
            th = None
            for b_ in range(7):
                for q, w in ((0, A["expert_w_gate"][0, e_]), (1, A["expert_w_up"][0, e_])):
                    for _, src in u_blk(w, 512 * b_, 512 * b_ + 512, ""):
                        i, wt, tw = load(src)
                        k0 = 0 if src.offset == w[0:1, 512 * b_:512 * b_ + 1].offset else 4

                        def f(e):
                            for c in range(4):
                                m = e.matmul(PS[:, q, :], XG[:, k0 + c, :], wt[:, c, :], start=(k0 + c == 0),
                                             stop=(k0 + c == 7))
                            return m
                        t = R.T(f, tw, tx, th)
                        free[i] = t
                t2 = R.A(lambda e: e.activation(H1, PS[:, 0, :], ACT.Silu), t)
                t2 = R.V(lambda e: e.tensor_tensor(H1, H1, PS[:, 1, :], ALU.mult), t2)

                def f(e):
                    for j in range(4):
                        m = e.transpose(PS[:, 3, 128 * j:128 * j + 128], H1[:, 128 * j:128 * j + 128], ident)
                    return m
                t2 = R.T(f, t2)
                th = R.A(lambda e: e.activation(HT2, PS[:, 3, :].rearrange("p (c n) -> p c n", c=4), ACT.Copy), t2)
                for half, (_, src) in enumerate(u_tm(A["expert_w_down"][0, e_], 4 * b_, 4 * b_ + 4, "")):
                    i, wt, tw = load(src)

                    def f(e):
                        for c in range(2):
                            q = 2 * half + c
                            for nb in range(2):
                                m = e.matmul(PS[:, 5 + nb, :], HT2[:, q, :], wt[:, c, 512 * nb:512 * nb + 512],
                                             start=(b_ == 0 and q == 0), stop=(b_ == 6 and q == 3))
                        return m
                    t = R.T(f, tw, th)
                    free[i] = t
                th = [th, t]
            for nb in range(2):
                t2 = R.A(lambda e: e.activation(Y1[:, 512 * nb:512 * nb + 512], PS[:, 5 + nb, :], ACT.Copy), t)
            for q in range(4):
                k, nb = q // 2, q % 2
                ns = slice(512 * nb, 512 * nb + 512)
                t3 = R.T(lambda e: e.matmul(PS[:, 7, :], GT1[:, 128 * k:128 * k + 128], Y1[:, ns], start=True, stop=True),
                         t2, tgt, t_e)
                t_e = R.V(lambda e: e.tensor_tensor(FACC[:, k, ns], FACC[:, k, ns], PS[:, 7, :], ALU.add), t3)
        R.wait("s", R.fence())

    U = BT[:, :, :].rearrange("p h n -> p (h n)")
    WG = U[:, 0:384].rearrange("p (l c n) -> p l c n", l=2, c=24)
    WB = U[:, 384:576].rearrange("p (j n) -> p j n", j=6)

    def load_small():
        marks = K.fence()
        for l in range(2):
            K.dma("a", d5, WG[:, l], A["ml_w_gate_2"][l].rearrange("(c p) n -> p c n", p=128), marks)
            for j, nm in enumerate(("ml_wq_2", "ml_wk_2", "ml_wv_2")):
                K.dma("a", d5, WB[:, 3 * l + j, :].rearrange("p (c d) -> p c d", d=4),
                      A[nm][l].rearrange("(c n) k d -> (n k) c d", n=32))
        return (d5, K.count[d5])

    def rms(src, dst, *deps, sq=None, sqd=None):
        t = None
        for k in range(2):
            o = dst[:, k, :] if sq is None else sq
            t = ACTE(lambda e: e.activation(o, src[:, k, :], ACT.Square, accum_out=RS[:, k:k + 1]), *deps, sqd, t)
        t = V(lambda e: e.tensor_scalar(RS, RS, 1.0 / D, None, ALU.mult), t)
        t = rsqrt(RS, RS, RMS_EPS, t)
        for k in range(2):
            t2 = V(lambda e: e.tensor_scalar(dst[:, k, :], src[:, k, :], RS[:, k:k + 1], None, ALU.mult), t)
        return t2

    def by_col(name):
        def evac(c, p, t, dst):
            return V(lambda e: e.tensor_scalar(dst, p, pcol(name, c), None, ALU.mult), t)
        return evac

    def add_x(banks, t):
        for k in range(2):
            for nb in range(2):
                b = banks[2 * k + nb]
                xs = X[:, k, 512 * nb:512 * nb + 512]
                pf[b] = V(lambda e: e.tensor_tensor(xs, xs, PS[:, b, :], ALU.add), t)
        return pf[b]

    def fm_to(dst, func, name, off, pad=0, extra=None, into=None):
        def evac(j, p, t):
            for ci in range(2):
                c = 2 * j + ci
                o = dst[:, c, pad:pad + 256]
                s_ = p[:, 256 * ci:256 * ci + 256]
                if name is None:
                    r = ACTE(lambda e: e.activation(o, s_, func), t, extra)
                else:
                    r = ACTE(lambda e: e.activation(o, s_, func, bias=pcol(name, off + c)), t, extra)
            if into is not None:
                into(j, r)
            return [r]
        return evac

    def layer2(l, t_small):
        XN = ar(2048, 2, 1024)
        XM = ar(2048, 8, 259)
        UP = ar(4120, 8, 286)
        XC = ar(6408, 8, 256)
        R8 = ar(8456, 8, 256)
        UC = ar(10504, 8, 256)
        QF = ar(12552, 8, 256)
        KF = ar(14600, 8, 256)
        VT = ar(0, 2, 1024)
        marks = K.fence()
        t = rms(X, XN, marks)
        act = to_fm(XN, X1H, X1L, [4, 5, 6, 7], t, by_col(f"norm_mix{l}"))
        tz = [G(lambda e: e.memset(UP[:, :, 0:30], 0.0), marks)]
        tz.append(G(lambda e: e.memset(XM[:, :, 0:3], 0.0), act[2]))
        gemm_fm(f"in2{l}", 1024, act, [0, 1], fm_to(XM, ACT.Identity, f"b_in{l}", 0, 3, tz))
        t_xm = K.last["a"]
        tcv = []
        for c in range(8):
            dst = XC[:, c, :]
            t = V(lambda e: e.tensor_scalar(dst, XM[:, c, 0:256], pcol(f"ml_conv_w{l}", c), pcol(f"ml_conv_b{l}", c),
                                            ALU.mult, ALU.add), t_xm, tz)
            for k in range(1, 4):
                t = V(lambda e: e.scalar_tensor_tensor(dst, XM[:, c, k:k + 256], pcol(f"ml_conv_w{l}", 8 * k + c), dst,
                                                       ALU.mult, ALU.add), t)
            tcv.append(t)
        t_xc = ACTE(lambda e: e.activation(XC, XC, ACT.Silu), tcv)
        gemm_fm(f"in2{l}", 1024, act, [0, 1], fm_to(UP, ACT.Identity, f"b_in{l}", 16, 30, tz))
        t_a = K.last["a"]

        tuc, t_u = [], []
        taps = [(c + i, k) for c in (0, 2, 4, 6) for k in range(31) for i in range(2)]
        tap_tok = {}

        def conv_taps(n):
            for c, k in taps[:n]:
                dst, wk = UC[:, c, :], pcol(f"cv_dw_w{l}", 8 * k + c)
                if k == 0:
                    t = V(lambda e: e.tensor_scalar(dst, UP[:, c, 0:256], wk, pcol(f"cv_dw_b{l}", c), ALU.mult,
                                                    ALU.add), t_u[c // 2])
                else:
                    t = V(lambda e: e.scalar_tensor_tensor(dst, UP[:, c, k:k + 256], wk, dst, ALU.mult, ALU.add),
                          tap_tok[c])
                tap_tok[c] = t
                if k == 30:
                    tuc.append(t)
            del taps[:n]

        def ev_g(j, p, t):
            for ci in range(2):
                c = 2 * j + ci
                r = ACTE(lambda e: e.activation(R8[:, c, :], p[:, 256 * ci:256 * ci + 256], ACT.Sigmoid,
                                                bias=pcol(f"b_in{l}", 24 + c)), t)
            t = V(lambda e: e.tensor_tensor(UP[:, 2 * j:2 * j + 2, 30:286], UP[:, 2 * j:2 * j + 2, 30:286],
                                            R8[:, 2 * j:2 * j + 2, :], ALU.mult), r, t_a)
            t_u.append(t)
            if j > 0:
                conv_taps(6)
            return [r]
        gemm_fm(f"in2{l}", 1024, act, [0, 1], ev_g)

        bd = [ar(o, 8, 128) for o in (14600, 2048, 12552)]
        tq = {}

        def build(j, *deps):
            return V(lambda e: e.tensor_tensor(view(bd[j], [128, 8], [4, 32], [1, 4]),
                                               view(WB[:, 3 * l + j, :], [4, 8], [0, 32], [1, 4]),
                                               view(CST[:, C_BD:C_BD + 32], [0, 8], [1, 32], [0, 4]), ALU.mult),
                     t_small, marks, *deps)

        def product(j, t):
            src, dst, off = ((XC, QF, 0), (XC, KF, 0), (XM, R8, 3))[j]
            for cp in range(4):
                b = 2 + cp % 2

                def f(e):
                    for ci in range(2):
                        c = 2 * cp + ci
                        m = e.matmul(PS[:, b, 256 * ci:256 * ci + 256], bd[j][:, c, :], src[:, c, off:off + 256],
                                     start=True, stop=True)
                    return m
                t2 = T(f, t, t_xc, t_xm, pf[b])
                pf[b] = ACTE(lambda e: e.activation(dst[:, 2 * cp:2 * cp + 2, :], PS[:, b, :].rearrange(
                    "p (c n) -> p c n", c=2), ACT.Copy), t2, t_u, tq.get("free"))
            tq[j] = pf[b]
            return t2
        tb = [build(0), None, build(2)]
        conv_taps(25)
        product(2, tb[2])
        for k in range(2):
            for hf in range(2):
                b = 4 + 2 * k + hf
                t2 = T(lambda e: [e.matmul(PS[:, b, 128 * c:128 * c + 128], XM[:, 4 * hf + c, 3 + 128 * k:131 + 128 * k],
                                           bd[2][:, 4 * hf + c, :], start=True, stop=True) for c in range(4)][-1], pf[b])
                pf[b] = ACTE(lambda e: e.activation(VT[:, k, 512 * hf:512 * hf + 512], PS[:, b, :], ACT.Copy), t2,
                             act[2])
        t_vt = pf[b]
        tq["free"] = t2
        tb[1] = build(1, t2)
        conv_taps(25)
        tq["free"] = product(0, tb[0])
        t2 = product(1, tb[1])
        t_bd = t2

        def f(e):
            for k in range(2):
                for i in range(24):
                    src = (QF, KF, R8)[i // 8]
                    m = e.matmul(PS[:, 0, 8 * k:8 * k + 8], src[:, i % 8, 128 * k:128 * k + 128], WG[:, l, i, :],
                                 start=(i == 0), stop=(i == 23))
            return m
        t = T(f, tq[0], tq[1], tq[2], pf[0])
        t_gt = t
        GA, SPF, CSF, Gc, NM, DN = [SMT[:, 16 * i:16 * i + 16] for i in range(6)]
        g2 = lambda a, n=8: a[:, 0:2 * n].rearrange("p (t h) -> p t h", t=2)
        pf[0] = V(lambda e: e.tensor_tensor(g2(GA), PS[:, 0, 0:16].rearrange("p (t h) -> p t h", t=2),
                                            view(mbg[:, l, :], [0, 2], [1, 8]), ALU.add), t, marks)
        t = softplus(SPF, GA, -1.0, [SMT[:, 96 + 16 * i:112 + 16 * i] for i in range(5)], pf[0])

        conv_taps(2)

        def f(e):
            e.matmul(PS[:, 1, 0:8], tri, SPF[:, 0:8], start=True, stop=True)
            e.matmul(PS[:, 1, 8:16], ones, SPF[:, 0:8], start=True, stop=False)
            return e.matmul(PS[:, 1, 8:16], tri, SPF[:, 8:16], start=False, stop=True)
        t = T(f, t, pf[1])
        conv_taps(2)
        t = pf[1] = V(lambda e: e.tensor_copy(CSF, PS[:, 1, 0:16]), t)
        t = V(lambda e: e.tensor_tensor(g2(Gc, 4), g2(GA)[:, :, 0:4], g2(CSF)[:, :, 4:8], ALU.add), t)
        t_g = t
        t = transposes(1, [(PS[0:4, 1, 128 * k:128 * k + 128], Gc[:, 4 * k:4 * k + 4]) for k in range(2)], t)
        conv_taps(2)
        GR, MR = ROWS[0:4, 0, :], ROWS[0:4, 1, :]
        pf[1] = V(lambda e: e.tensor_copy(GR, PS[0:4, 1, 0:256]), t)
        t = V(lambda e: e.tensor_tensor_scan(MR, GR, GR, 0.0, ALU.max, ALU.max), pf[1])
        t_mr = t
        t = transposes(1, [(PS[:, 1, 4 * k:4 * k + 4], MR[:, 128 * k:128 * k + 128]) for k in range(2)], t)
        conv_taps(2)
        pf[1] = V(lambda e: e.tensor_tensor(g2(NM, 4), g2(CSF)[:, :, 4:8], PS[:, 1, 0:8].rearrange(
            "p (t h) -> p t h", t=2), ALU.subtract), t)
        t_nm = ACTE(lambda e: e.activation(NM[:, 0:8], NM[:, 0:8], ACT.Exp), pf[1])
        EE = ar(8456, 4, 384)
        te = []
        for h in range(4):
            b = 4 + h
            t = T(lambda e: e.matmul(PS[:, b, 0:256], view(ident[0:4, h:h + 1], [0, 128]), MR, start=True, stop=True),
                  t_mr, pf[b])
            conv_taps(2)
            V(lambda e: e.scalar_tensor_tensor(EE[:, h, 0:256], negm, Gc[:, h:h + 1], PS[:, b, 0:256], ALU.add,
                                               ALU.subtract), t, t_g, t_gt)
            pf[b] = V(lambda e: e.scalar_tensor_tensor(EE[:, h, 256:384], negm[:, 0:128], Gc[:, 4 + h:5 + h],
                                                       PS[:, b, 128:256], ALU.add, ALU.subtract), t)
            te.append(ACTE(lambda e: e.activation(EE[:, h, :], EE[:, h, :], ACT.Exp), pf[b]))
        tp = []
        for h in range(4):
            b = 2 + h % 2

            def f(e):
                for c in (2 * h, 2 * h + 1):
                    e.matmul(PS[:, b, 0:256], KF[:, c, 0:128], QF[:, c, :], start=(c == 2 * h), stop=(c == 2 * h + 1))
                for c in (2 * h, 2 * h + 1):
                    m = e.matmul(PS[:, b, 256:384], KF[:, c, 128:256], QF[:, c, 128:256], start=(c == 2 * h),
                                 stop=(c == 2 * h + 1))
                return m
            t = T(f, tq[0], tq[1], pf[b])
            conv_taps(2)
            pf[b] = V(lambda e: e.scalar_tensor_tensor(EE[:, h, :], PS[:, b, 0:384], 0.0625, EE[:, h, :], ALU.mult,
                                                       ALU.mult), t, te[h])
            tp.append(pf[b])

        def f(e):
            for h in range(4):
                e.matmul(PS[:, 0, h:h + 1], EE[:, h, 0:128], ones[:, 0:1], start=True, stop=True)
                e.matmul(PS[:, 0, 4 + h:5 + h], EE[:, h, 128:256], ones[:, 0:1], start=True, stop=False)
                m = e.matmul(PS[:, 0, 4 + h:5 + h], EE[:, h, 256:384], ones[:, 0:1], start=False, stop=True)
            return m
        t = T(f, tp, pf[0])
        conv_taps(2)
        t = pf[0] = ACTE(lambda e: e.activation(DN[:, 0:8], PS[:, 0, 0:8], ACT.Abs), t)
        t = V(lambda e: e.tensor_tensor(DN[:, 0:8], DN[:, 0:8], NM[:, 0:8], ALU.max), t, t_nm)
        t_dn = V(lambda e: e.reciprocal(DN[:, 0:8], DN[:, 0:8]), t)
        HT = ar(2048, 2, 1024)
        MV8, R8s, ST8 = SMT[:, 96:112], SMT[:, 112:120], SMT[:, 176:224].rearrange("p (a b) -> p a b", a=8)
        for h in range(4):
            b = 4 + h

            def f(e):
                v = lambda k: VT[:, k, 256 * h:256 * h + 256]
                e.matmul(PS[:, b, 0:256], EE[:, h, 0:128], v(0), start=True, stop=True)
                e.matmul(PS[:, b, 256:512], EE[:, h, 128:256], v(0), start=True, stop=False)
                return e.matmul(PS[:, b, 256:512], EE[:, h, 256:384], v(1), start=False, stop=True)
            t = T(f, tp[h], t_vt, pf[b])
            conv_taps(2)
            for k in range(2):
                pf[b] = V(lambda e: e.tensor_scalar(HT[:, k, 256 * h:256 * h + 256], PS[:, b, 256 * k:256 * k + 256],
                                                    DN[:, 4 * k + h:4 * k + h + 1], None, ALU.mult), t, t_dn, t_bd)
        t = pf[7]
        for i in range(8):
            k, h = i // 4, i % 4
            t2 = V(lambda e: e.bn_stats(ST8[:, i, :], HT[:, k, 256 * h:256 * h + 256]), t)
        for i in range(8):
            t = V(lambda e: e.bn_aggr(MV8[:, 2 * i:2 * i + 2], ST8[:, i, :]), t2)
        t = rsqrt(R8s, view(MV8[:, 1:2], [2, 8]), LN_EPS, t)
        for i in range(8):
            k, h = i // 4, i % 4
            hv = HT[:, k, 256 * h:256 * h + 256]
            t2 = V(lambda e: e.tensor_scalar(hv, hv, MV8[:, 2 * i:2 * i + 1], R8s[:, i:i + 1], ALU.subtract, ALU.mult),
                   t)
        t_hn = t2
        for c in range(8):
            t_sk = ACTE(lambda e: e.activation(XC[:, c, :], XC[:, c, :], ACT.Copy, scale=pcol(f"ml_skip{l}", c)), t_bd)
        def slice_():
            conv_taps(9)
        side.extend([slice_] * 16)

        def ev_z(j, p, t):
            for ci in range(2):
                c = 2 * j + ci
                r = ACTE(lambda e: e.activation(R8[:, c, :], p[:, 256 * ci:256 * ci + 256], ACT.Silu,
                                                bias=pcol(f"b_in{l}", 8 + c)), t, K.last["t"])
            return [r]
        gemm_fm(f"in2{l}", 1024, act, [0, 1], ev_z)
        t_z = K.last["a"]

        def ev(c, p, t, dst):
            t = V(lambda e: e.scalar_tensor_tensor(dst, p, pcol(f"ml_norm_g{l}", c), XC[:, c, :], ALU.mult, ALU.add), t,
                  t_sk)
            return V(lambda e: e.tensor_tensor(dst, dst, R8[:, c, :], ALU.mult), t, t_z)
        act2 = to_fm(HT, X2H, X2L, [2, 3], t_hn, ev)
        YM, YC = QF, R8
        MEM = ar(6408, 2, 1024)
        for k in range(2):
            tm_ = K.dma("s", d4, MEM[:, k, :], A["mem_2"][0, 128 * k:128 * k + 128, :], act2[2])

        def ev_y(dst, name, free=None):
            def evac(j, p, t):
                o = dst[:, 2 * j:2 * j + 2, :]
                s_ = p.rearrange("p (c n) -> p c n", c=2)
                if name is None:
                    r = ACTE(lambda e: e.activation(o, s_, ACT.Copy), t, free if free else K.last["v"])
                else:
                    for ci in range(2):
                        r = ACTE(lambda e: e.activation(o[:, ci, :], s_[:, ci, :], ACT.Identity,
                                                        bias=pcol(name, 2 * j + ci)), t, K.last["v"])
                return [r]
            return evac
        gemm_fm(f"mld{l}", 1024, act2, [0, 1], ev_y(YM, None))
        t_ym = K.last["a"]
        t_mem = rms(MEM, MEM, tm_, sq=ar(0, 1024), sqd=act2[2])
        GS = ar(2048, 8, 256)

        def ev_sig(off, into):
            def evac(j, p, t):
                for ci in range(2):
                    c = 2 * j + ci
                    r = ACTE(lambda e: e.activation(GS[:, c, :], p[:, 256 * ci:256 * ci + 256], ACT.Sigmoid,
                                                    bias=pcol(f"b_in{l}", off + c)), t, act2[2], tgs.get(j))
                into(j, r)
                return [r]
            return evac
        tgs = {}

        def into_ym(j, r):
            o = YM[:, 2 * j:2 * j + 2, :]
            tgs[j] = V(lambda e: e.tensor_tensor(o, o, GS[:, 2 * j:2 * j + 2, :], ALU.mult), r, t_ym)
        gemm_fm(f"in2{l}", 1024, act, [0, 1], ev_sig(32, into_ym))
        t_ymg = K.last["v"]
        gemm_fm(f"in2{l}", 1024, act, [0, 1], ev_sig(40, lambda j, r: None))
        t_g5 = K.last["a"]
        KT, VM = ar(4120, 8, 256), ar(6408, 2, 1024)
        actm = to_fm(MEM, X1H, X1L, [4, 5, 6, 7], t_mem, by_col(f"norm_mem{l}"), K.last["t"])
        t_mt = K.last["t"]
        del side[:]
        conv_taps(248)
        t_cd = list(tuc)
        gemm_fm(f"xk{l}", 1024, actm, [0, 1], ev_y(KT, None, t_cd))
        UT = ar(14600, 2, 1024)
        for cp in range(4):
            b = 2 + cp % 2
            t = transposes(b, [(PS[:, b, 256 * tt + 128 * ci:256 * tt + 128 * ci + 128],
                                UC[:, 2 * cp + ci, 128 * tt:128 * tt + 128]) for ci in range(2) for tt in range(2)], tuc)
            pf[b] = ACTE(lambda e: e.activation(UT[:, :, 256 * cp:256 * cp + 256], PS[:, b, :].rearrange(
                "p (t n) -> p t n", t=2), ACT.Copy), t)
        t = pf[b]
        t = pf[b]
        for k in range(2):
            t2 = bn(UT[:, k, :], STT[:, k, :], MV[:, k, :], t)
        t = rstd_of(MV[:, :, 1], RS, t2)
        for k in range(2):
            t2 = V(lambda e: e.tensor_scalar(UT[:, k, :], UT[:, k, :], MV[:, k, 0:1], RS[:, k:k + 1], ALU.subtract,
                                             ALU.mult), t)
        t_ut = t2
        t = gemm_tm(f"xv{l}", actm, [4, 5, 6, 7])
        for k in range(2):
            for nb in range(2):
                b = 4 + 2 * k + nb
                pf[b] = ACTE(lambda e: e.activation(VM[:, k, 512 * nb:512 * nb + 512], PS[:, b, :], ACT.Copy), t, t_mt)
        t_v = pf[7]
        def ev(c, p, t, dst):
            return ACTE(lambda e: e.activation(dst, p, ACT.Silu, bias=pcol(f"cv_ln_b{l}", c),
                                               scale=pcol(f"cv_ln_g{l}", c)), t, K.last["v"])

        act2 = to_fm(UT, X2H, X2L, [2, 3], t_ut, ev, K.last["t"])

        def ev_c(j, p, t):
            o = YC[:, 2 * j:2 * j + 2, :]
            for ci in range(2):
                c = 2 * j + ci
                r = ACTE(lambda e: e.activation(YC[:, c, :], p[:, 256 * ci:256 * ci + 256], ACT.Identity,
                                                bias=pcol(f"cv_b_pw{l}", c)), t, K.last["v"])
            ym = YM[:, 2 * j:2 * j + 2, :]
            t3 = V(lambda e: e.tensor_tensor(o, o, GS[:, 2 * j:2 * j + 2, :], ALU.mult), r, t_g5)
            t3 = V(lambda e: e.tensor_tensor(ym, ym, o, ALU.add), t3, t_ymg)
            mer.extend(split_act(ym, X1H[:, 2 * j:2 * j + 2, :], X1L[:, 2 * j:2 * j + 2, :], t3, K.last["t"]))
            return [r]
        mer = []
        gemm_fm(f"cvp{l}", 1024, act2, [0, 1], ev_c)
        t_x1 = t = gemm_tm(f"out2{l}", (X1H, X1L, mer), [4, 5, 6, 7])
        t = add_x([4, 5, 6, 7], t)

        marks = K.fence()
        XN = ar(2048, 2, 1024)
        QT = ar(10504, 8, 256)
        P4, PT = ar(12552, 4, 512), ar(14600, 4, 512)
        t = rms(X, XN)
        act = to_fm(XN, X1H, X1L, [2, 3], t, by_col(f"norm_x{l}"))
        gemm_fm(f"xq{l}", 1024, act, [0, 1], ev_y(QT, None))
        t_q = K.last["a"]
        mx, ng, den = [SMT[:, 8 * i:8 * i + 8] for i in range(3)]
        at_o = []
        for h in range(4):
            b = 4 + h

            def f(e):
                for k in range(2):
                    for c in (2 * h, 2 * h + 1):
                        m = e.matmul(PS[:, b, 256 * k:256 * k + 256], QT[:, c, 128 * k:128 * k + 128], KT[:, c, :],
                                     start=(c == 2 * h), stop=(c == 2 * h + 1))
                return m
            t = T(f, t_q, pf[b])
            t = V(lambda e: e.tensor_reduce(mx[:, 2 * h:2 * h + 2], PS[:, b, :].rearrange("p (k n) -> p k n", k=2), AX,
                                            ALU.max), t)
            t = V(lambda e: e.tensor_scalar(ng[:, 2 * h:2 * h + 2], mx[:, 2 * h:2 * h + 2], -0.0625, None, ALU.mult), t)
            for k in range(2):
                pf[b] = ACTE(lambda e: e.activation(P4[:, h, 256 * k:256 * k + 256], PS[:, b, 256 * k:256 * k + 256],
                                                    ACT.Exp, bias=ng[:, 2 * h + k:2 * h + k + 1], scale=0.0625,
                                                    accum_out=den[:, 2 * h + k:2 * h + k + 1]), t)
            t = V(lambda e: e.reciprocal(den[:, 2 * h:2 * h + 2], den[:, 2 * h:2 * h + 2]), pf[b])
            for k in range(2):
                pv = P4[:, h, 256 * k:256 * k + 256]
                t2 = V(lambda e: e.tensor_scalar(pv, pv, den[:, 2 * h + k:2 * h + k + 1], None, ALU.mult), t)
            at_o.append(t2)
        for h in range(4):
            b = 2 + h % 2
            t = transposes(b, [(PS[:, b, 256 * n_ + 128 * k:256 * n_ + 128 * k + 128],
                                P4[:, h, 256 * k + 128 * n_:256 * k + 128 * n_ + 128])
                               for n_ in range(2) for k in range(2)], at_o[h])
            pf[b] = ACTE(lambda e: e.activation(PT[:, h, :], PS[:, b, :], ACT.Copy), t)
            at_o[h] = pf[b]
        oo = []
        for h in range(4):
            b = 4 + h

            def f(e):
                for dc in range(2):
                    for n_ in range(2):
                        m = e.matmul(PS[:, b, 256 * dc:256 * dc + 256], VM[:, n_, 256 * h + 128 * dc:256 * h + 128 * dc + 128],
                                     PT[:, h, 256 * n_:256 * n_ + 256], start=(n_ == 0), stop=(n_ == 1))
                return m
            t = T(f, at_o[h], t_v, pf[b])
            pf[b] = split_act(PS[:, b, :].rearrange("p (c n) -> p c n", c=2), X2H[:, 2 * h:2 * h + 2, :],
                              X2L[:, 2 * h:2 * h + 2, :], t)
            oo += pf[b]
        t = gemm_tm(f"xo{l}", (X2H, X2L, oo), [4, 5, 6, 7])
        t = add_x([4, 5, 6, 7], t)

        marks = K.fence()
        t = rms(X, XN, marks)
        act = to_fm(XN, X1H, X1L, [2, 3], t, by_col(f"norm_ffn{l}"))
        PD = ar(4096, 2, 4, 258)
        CV = ar(6160, 2, 4, 256)
        tz = G(lambda e: e.memset(PD[:, :, :, 0:2], 0.0), marks)
        cst_ = {"n": 0}

        def conv_evac(p, got):
            n_ = cst_["n"] % 2
            cst_["n"] += 1
            (bg, tg_), (bu, tu) = got
            for q, (b, t) in enumerate(((bg, tg_), (bu, tu))):
                for ci in range(2):
                    c = 22 * q + 2 * p + ci
                    r = ACTE(lambda e: e.activation(PD[:, n_, 2 * q + ci, 2:258], PS[:, b, 256 * ci:256 * ci + 256],
                                                    ACT.Identity, bias=pcol(f"ffn_b_up{l}", c)), t, tz,
                             cst_.get(("cv", n_)))
                pf[b] = r
                for ci in range(2):
                    c = 22 * q + 2 * p + ci
                    s_, dst = PD[:, n_, 2 * q + ci, :], CV[:, n_, 2 * q + ci, :]
                    t = V(lambda e: e.tensor_scalar(dst, s_[:, 0:256], pcol(f"ffn_dw_w{l}", c), pcol(f"ffn_dw_b{l}", c),
                                                    ALU.mult, ALU.add), r, cst_.get(("sp", n_)))
                    for k in (1, 2):
                        t = V(lambda e: e.scalar_tensor_tensor(dst, s_[:, k:k + 256], pcol(f"ffn_dw_w{l}", 44 * k + c),
                                                               dst, ALU.mult, ALU.add), t)
                if q == 0:
                    sg = ACTE(lambda e: e.activation(CV[:, n_, 0:2, :], CV[:, n_, 0:2, :], ACT.Silu), t)
            cst_[("cv", n_)] = t
            hv = CV[:, n_, 2:4, :]
            t = V(lambda e: e.tensor_tensor(hv, hv, CV[:, n_, 0:2, :], ALU.mult), t, sg)
            cst_[("sp", n_)] = t
            return hv.rearrange("p c n -> p (c n)"), t
        t = ffn(f"ff2{l}", 11, act, conv_evac, True, True)
        t = add_x([4, 5, 6, 7], t)

    ROWS = ar(9992, 512).rearrange("p (a n) -> p a n", a=2)

    layer1(0)
    layer1(1)
    t_small = load_small()
    lo_pool[:] = [5, 8]
    layer2(0, t_small)
    layer2(1, t_small)
    marks = K.fence()
    FN = ar(4096, 1024)
    XN = ar(2048, 2, 1024)
    tf = K.dma("s", d4, FN, AP(A["final_norm_2"].tensor, A["final_norm_2"].offset, [[0, 128], [1, D]]), marks)
    t = rms(X, XN, marks)
    for k in range(2):
        t = V(lambda e: e.tensor_tensor(XN[:, k, :], XN[:, k, :], FN, ALU.mult), t, tf)
    finish(K, out, XN)


def finish(K, out, X):
    d = K.new("out")
    marks = K.fence()
    for k in range(2):
        t = K.dma("s", d, out[0, 128 * k:128 * k + 128, :], X[:, k, :], marks)
    K.wait("s", [t])


_INS = ["x", "c", "positions", "rel_bias", "w_ada", "b_ada", "w_in", "w_out", "conv_w", "conv_b", "dt_bias", "a_log",
        "d_skip", "ssd_norm_w", "sinks", "ln_g", "ln_b", "ffn_w_gate", "ffn_w_up", "ffn_w_down", "router_w",
        "router_b", "expert_w_gate", "expert_w_up", "expert_w_down", "mem_2", "norm_mix_2", "w_in_2", "b_in_2",
        "ml_conv_w_2", "ml_conv_b_2", "ml_wq_2", "ml_wk_2", "ml_wv_2", "ml_w_gate_2", "ml_b_gate_2", "ml_norm_g_2",
        "ml_skip_2", "ml_w_down_2", "cv_dw_w_2", "cv_dw_b_2", "cv_ln_g_2", "cv_ln_b_2", "cv_w_pw_2", "cv_b_pw_2",
        "w_out_2", "norm_x_2", "norm_mem_2", "xa_wq_2", "xa_wk_2", "xa_wv_2", "xa_wo_2", "norm_ffn_2", "ffn_w_up_2",
        "ffn_b_up_2", "ffn_dw_w_2", "ffn_dw_b_2", "ffn_w_down_2", "final_norm_2"]


def kernel(**inputs):
    import concourse.bacc as _bacc
    from concourse.bass_utils import run_bass_kernel_spmd as _run

    nc = _bacc.Bacc("TRN2", target_bir_lowering=False, num_devices=1)
    arrays, A = {}, {}
    for name in _INS:
        a = np.ascontiguousarray(inputs[name])
        arrays[f"in_{name}_dram"] = a
        A[name] = nc.dram_tensor(f"in_{name}_dram", a.shape, mybir.dt.from_np(a.dtype), kind="ExternalInput").ap()
    a = constants()
    arrays["in_cst_dram"] = a
    A["cst"] = nc.dram_tensor("in_cst_dram", a.shape, mybir.dt.float32, kind="ExternalInput").ap()
    out = nc.dram_tensor("out_0_dram", (1, S, D), mybir.dt.float32, kind="ExternalOutput").ap()
    build_program(nc, A, out)
    r = _run(nc, [arrays], core_ids=[0])
    return r.results[0]["out_0_dram"]
```
